# Optimizing a Trainium2 kernel written in Bass

```python
import math
import jax
import jax.numpy as jnp
from jax import lax
import numpy as np

D_MODEL = 1024
BATCH = 1
SEQ = 128
DEPTH = 2
DEC_BATCH = 1
DEC_SEQ = 256
PAST_LEN = 128

GRID_W = 64
N_EVEN = (DEPTH + 1) // 2
N_ODD = DEPTH // 2
NORM_EPS = 1e-6
ROPE_THETA = 10000.0
Q_BLOCK = 128

A_HEADS = 8
A_KV_HEADS = 2
A_DIM = 64
A_GROUP = A_HEADS // A_KV_HEADS
B_HEADS = 8
B_DIM = 64
B_WIDTH = B_HEADS * B_DIM
DECAY_LORA = 64
ICLR_LORA = 64
GATE_LORA = 128
B_COLS = 3 * B_WIDTH + DECAY_LORA + ICLR_LORA + GATE_LORA
LNX_EPS = 64e-5
C_HEADS = 4
C_DIM = 128
C_WIDTH = C_HEADS * C_DIM
CONV_W = 3
CHUNK = 64
D_HEADS = 4
D_DIM = 64
D_VDIM = 128
D_QK = D_HEADS * 2 * D_DIM
D_V = D_HEADS * D_VDIM
EVEN_COLS = A_HEADS * A_DIM + 2 * A_KV_HEADS * A_DIM + B_COLS
EVEN_OUT = A_HEADS * A_DIM + B_WIDTH
ODD_COLS = 4 * C_WIDTH + 4 * C_HEADS + 2 * D_QK + D_V
ODD_OUT = C_WIDTH + D_V
N_EXPERTS = 64
TOP_K = 6
N_GROUPS = 8
TOPK_GROUPS = 4
EXPERT_FF = 256
SHARED_FF = 256
ROUTED_SCALE = 1.0
MOE_BLOCK = 128

kernel_name = 'hybrid_prefix_diffusion_step'

def rms_norm(x, g, eps=NORM_EPS):
    xf = x.astype(jnp.float32)
    y = xf * lax.rsqrt(jnp.mean(xf * xf, axis=-1, keepdims=True) + eps)
    return (y * g.astype(jnp.float32)).astype(x.dtype)

def l2_normalize(x, eps=1e-6):
    xf = x.astype(jnp.float32)
    return xf * lax.rsqrt(jnp.sum(xf * xf, axis=-1, keepdims=True) + eps)

def group_norm_heads(y, w, b, eps=LNX_EPS):
    mu = jnp.mean(y, axis=-1, keepdims=True)
    var = jnp.mean(jnp.square(y - mu), axis=-1, keepdims=True)
    return (y - mu) * lax.rsqrt(var + eps) * w + b

def adaln(cond, w, b):
    m = jax.nn.silu(cond) @ w + b
    return m.reshape(cond.shape[0], 6, D_MODEL)

def modulate(x, shift, scale):
    return x * (1 + scale) + shift

def axial_rope_tables(n_tok, dim):
    rows = n_tok // GRID_W
    row = jnp.repeat(jnp.arange(rows, dtype=jnp.float32), GRID_W)
    col = jnp.tile(jnp.arange(GRID_W, dtype=jnp.float32), rows)
    n_freq = dim // 4
    inv = ROPE_THETA ** (-jnp.arange(n_freq, dtype=jnp.float32) / n_freq)
    ang = jnp.concatenate([row[:, None] * inv, col[:, None] * inv], axis=-1)
    return jnp.cos(ang), jnp.sin(ang)

def apply_rope(x, cos, sin):
    xf = x.astype(jnp.float32)
    x1, x2 = xf[..., 0::2], xf[..., 1::2]
    out = jnp.stack([x1 * cos - x2 * sin, x1 * sin + x2 * cos], axis=-1)
    return out.reshape(x.shape).astype(x.dtype)

def block_attention(q, k, v):
    bsz, hk, grp, s, d = q.shape
    nb = s // Q_BLOCK
    qb = jnp.moveaxis(q.reshape(bsz, hk, grp, nb, Q_BLOCK, d), 3, 0)
    scale = d ** -0.5

    def one_block(qblk):
        sc = jnp.einsum('bhgqd,bhkd->bhgqk', qblk, k, preferred_element_type=jnp.float32) * scale
        pr = jax.nn.softmax(sc, axis=-1).astype(v.dtype)
        return jnp.einsum('bhgqk,bhkd->bhgqd', pr, v)

    ob = lax.map(one_block, qb)
    return jnp.moveaxis(ob, 0, 3).reshape(bsz, hk, grp, s, v.shape[-1])

def centred_token_shift(x, mu):
    xp = jnp.pad(x, ((0, 0), (1, 1), (0, 0)))
    neighbours = 0.5 * (xp[:, :-2] + xp[:, 2:])
    return x + mu * (neighbours - x)

def centred_depthwise_conv(x, w):
    ch = x.shape[-1]
    return lax.conv_general_dilated(x, w[:, None, :].astype(x.dtype), window_strides=(1,),
                                    padding=[(CONV_W // 2, CONV_W // 2)],
                                    dimension_numbers=('NWC', 'WIO', 'NWC'), feature_group_count=ch)

def rwkv7_scan(S0, r, w, k, v, a, b):
    def step(S, inp):
        r_t, w_t, k_t, v_t, a_t, b_t = inp
        sa = jnp.einsum('bhij,bhj->bhi', S, a_t)
        S = S * w_t[:, :, None, :] + sa[..., None] * b_t[:, :, None, :] + v_t[..., None] * k_t[:, :, None, :]
        return S, jnp.einsum('bhij,bhj->bhi', S, r_t)

    xs = tuple(jnp.moveaxis(t, 1, 0) for t in (r, w, k, v, a, b))
    S, ys = lax.scan(step, S0, xs)
    return jnp.moveaxis(ys, 0, 1), S

def gated_delta_chunked(q, k, v, g, beta, S0):
    bsz, t_len, nh, dk = k.shape
    n = t_len // CHUNK

    def chunks(t):
        return jnp.moveaxis(t.reshape((bsz, n, CHUNK, nh) + t.shape[3:]), 3, 1)

    q = chunks(q * dk ** -0.5)
    k = chunks(k)
    v = chunks(v)
    g = jnp.cumsum(chunks(g), axis=-1)
    beta = chunks(beta)
    incl = jnp.tril(jnp.ones((CHUNK, CHUNK), bool))
    strict = jnp.tril(jnp.ones((CHUNK, CHUNK), bool), -1)
    gdiff = g[..., :, None] - g[..., None, :]
    decay = jnp.where(incl, jnp.exp(jnp.where(incl, gdiff, 0.0)), 0.0)
    kb = k * beta[..., None]
    L = jnp.where(strict, jnp.einsum('bhnid,bhnjd->bhnij', kb, k) * decay, 0.0)
    eye = jnp.eye(CHUNK, dtype=jnp.float32)
    t_inv = lax.linalg.triangular_solve(eye + L, jnp.broadcast_to(eye, L.shape), left_side=True,
                                        lower=True, unit_diagonal=True)
    u = t_inv @ (v * beta[..., None])
    wk = t_inv @ (kb * jnp.exp(g)[..., None])
    attn = jnp.einsum('bhnid,bhnjd->bhnij', q, k) * decay
    qg = q * jnp.exp(g)[..., None]
    kg = k * jnp.exp(g[..., -1:] - g)[..., None]
    glast = jnp.exp(g[..., -1])

    def step(S, inp):
        u_i, w_i, a_i, qg_i, kg_i, gl_i = inp
        v_new = u_i - jnp.einsum('bhcd,bhde->bhce', w_i, S)
        o = jnp.einsum('bhcd,bhde->bhce', qg_i, S) + jnp.einsum('bhcs,bhse->bhce', a_i, v_new)
        S = S * gl_i[..., None, None] + jnp.einsum('bhcd,bhce->bhde', kg_i, v_new)
        return S, o

    xs = tuple(jnp.moveaxis(t, 2, 0) for t in (u, wk, attn, qg, kg, glast))
    S, o = lax.scan(step, S0, xs)
    o = jnp.moveaxis(jnp.moveaxis(o, 0, 2), 1, 3)
    return o.reshape(bsz, t_len, nh, o.shape[-1]), S

def even_mixer(h, p, ctx=None):
    bsz, t_len, _ = h.shape
    f32 = jnp.float32
    proj = h @ p['w_in']
    a_q = A_HEADS * A_DIM
    a_kv = A_KV_HEADS * A_DIM
    aq, ak, av, xb = jnp.split(proj, [a_q, a_q + a_kv, a_q + 2 * a_kv], axis=-1)
    aq = jnp.transpose(rms_norm(aq.reshape(bsz, t_len, A_HEADS, A_DIM), p['a_qn']), (0, 2, 1, 3))
    ak = jnp.transpose(rms_norm(ak.reshape(bsz, t_len, A_KV_HEADS, A_DIM), p['a_kn']), (0, 2, 1, 3))
    av = jnp.transpose(av.reshape(bsz, t_len, A_KV_HEADS, A_DIM), (0, 2, 1, 3))
    if ctx is None:
        k_all, v_all = ak, av
        S0 = jnp.zeros((bsz, 2, B_HEADS, B_DIM, B_DIM), f32)
    else:
        cache_k, cache_v, S0 = ctx
        cos, sin = axial_rope_tables(t_len, A_DIM)
        aq = apply_rope(aq, cos, sin)
        k_all = jnp.concatenate([cache_k.astype(ak.dtype), apply_rope(ak, cos, sin)], axis=2)
        v_all = jnp.concatenate([cache_v.astype(av.dtype), av], axis=2)
        S0 = S0.astype(f32)
    oa = block_attention(aq.reshape(bsz, A_KV_HEADS, A_GROUP, t_len, A_DIM), k_all, v_all)
    oa = jnp.transpose(oa, (0, 3, 1, 2, 4)).reshape(bsz, t_len, a_q)
    xb = centred_token_shift(xb, p['b_mu'])
    splits = [B_WIDTH, 2 * B_WIDTH, 3 * B_WIDTH, 3 * B_WIDTH + DECAY_LORA, 3 * B_WIDTH + DECAY_LORA + ICLR_LORA]
    r, kb, vb, wd, ad, gd = jnp.split(xb.astype(f32), splits, axis=-1)

    def heads(t):
        return t.astype(f32).reshape(bsz, t_len, B_HEADS, B_DIM)

    r_h, k_h, v_h = heads(r), heads(kb), heads(vb)
    kk = l2_normalize(heads(kb * p['b_kk']))
    y = jnp.zeros_like(v_h)
    finals = []
    for d in range(2):
        w_log = -jax.nn.softplus(-(p['b_w0'][d] + jnp.tanh(wd) @ p['b_w2'][d])) - 0.5
        a = jax.nn.sigmoid(p['b_a0'][d] + ad @ p['b_a2'][d])
        k_d = kb * (1 + (a - 1) * p['b_ka'])
        seqs = (r_h, heads(jnp.exp(-jnp.exp(w_log))), heads(k_d), v_h, -kk, kk * heads(a))
        if d == 1:
            seqs = tuple(jnp.flip(t, axis=1) for t in seqs)
        y_d, S_d = rwkv7_scan(S0[:, d], *seqs)
        y = y + (jnp.flip(y_d, axis=1) if d == 1 else y_d)
        finals.append(S_d)
    y = group_norm_heads(y, p['b_lnx_w'].reshape(B_HEADS, B_DIM), p['b_lnx_b'].reshape(B_HEADS, B_DIM))
    y = y + jnp.sum(r_h * k_h * p['b_rk'], axis=-1, keepdims=True) * v_h
    ob = y.reshape(bsz, t_len, B_WIDTH) * (jax.nn.sigmoid(gd) @ p['b_g2'])
    out = jnp.concatenate([oa, ob.astype(h.dtype)], axis=-1) @ p['w_out']
    new_ctx = (ak, av, jnp.stack(finals, axis=1)) if ctx is None else None
    return out, new_ctx

def odd_mixer(h, p, lam_init, ctx=None):
    bsz, t_len, _ = h.shape
    f32 = jnp.float32
    proj = h @ p['w_in']
    s0 = 4 * C_WIDTH + 4 * C_HEADS
    cqkv, cz, cab, dq, dk, dv = jnp.split(
        proj, [3 * C_WIDTH, 4 * C_WIDTH, s0, s0 + D_QK, s0 + 2 * D_QK], axis=-1)
    cqkv = jax.nn.silu(centred_depthwise_conv(cqkv, p['c_conv']))

    def heads(t):
        return t.astype(f32).reshape(bsz, t_len, C_HEADS, C_DIM)

    cq, ck, cv = (heads(t) for t in jnp.split(cqkv, 3, axis=-1))
    cq, ck = l2_normalize(cq), l2_normalize(ck)
    cab = cab.astype(f32).reshape(bsz, t_len, 4, C_HEADS)
    if ctx is None:
        S0 = jnp.zeros((bsz, 2, C_HEADS, C_DIM, C_DIM), f32)
    else:
        cache_k, cache_v, S0 = ctx
        S0 = S0.astype(f32)
    oc = jnp.zeros_like(cv)
    finals = []
    for d in range(2):
        g = -jnp.exp(p['c_A_log'][d]) * jax.nn.softplus(cab[:, :, d] + p['c_dt_bias'][d])
        beta = jax.nn.sigmoid(cab[:, :, 2 + d])
        seqs = (cq, ck, cv, g, beta)
        if d == 1:
            seqs = tuple(jnp.flip(t, axis=1) for t in seqs)
        o_d, S_d = gated_delta_chunked(*seqs, S0[:, d])
        oc = oc + (jnp.flip(o_d, axis=1) if d == 1 else o_d)
        finals.append(S_d)
    oc = rms_norm(oc, p['c_onorm']) * jax.nn.silu(heads(cz))
    oc = oc.reshape(bsz, t_len, C_WIDTH).astype(h.dtype)
    dq = jnp.transpose(rms_norm(dq.reshape(bsz, t_len, D_HEADS, 2, D_DIM), p['d_qn']), (0, 2, 3, 1, 4))
    dk = jnp.transpose(rms_norm(dk.reshape(bsz, t_len, D_HEADS, 2, D_DIM), p['d_kn']), (0, 2, 3, 1, 4))
    dv = jnp.transpose(dv.reshape(bsz, t_len, D_HEADS, D_VDIM), (0, 2, 1, 3))
    if ctx is None:
        k_all, v_all = dk, dv
    else:
        cos, sin = axial_rope_tables(t_len, D_DIM)
        dq = apply_rope(dq, cos, sin)
        k_all = jnp.concatenate([cache_k.astype(dk.dtype), apply_rope(dk, cos, sin)], axis=3)
        v_all = jnp.concatenate([cache_v.astype(dv.dtype), dv], axis=2)
    o1 = block_attention(dq[:, :, 0:1], k_all[:, :, 0], v_all)
    o2 = block_attention(dq[:, :, 1:2], k_all[:, :, 1], v_all)
    lq1, lk1, lq2, lk2 = p['d_lambda'][0], p['d_lambda'][1], p['d_lambda'][2], p['d_lambda'][3]
    lam = jnp.exp(jnp.sum(lq1 * lk1)) - jnp.exp(jnp.sum(lq2 * lk2)) + lam_init
    od = (o1.astype(f32) - lam * o2.astype(f32))[:, :, 0]
    od = rms_norm(od, p['d_subln']) * (1 - lam_init)
    od = jnp.transpose(od, (0, 2, 1, 3)).reshape(bsz, t_len, D_V).astype(h.dtype)
    out = jnp.concatenate([oc, od], axis=-1) @ p['w_out']
    new_ctx = (dk, dv, jnp.stack(finals, axis=1)) if ctx is None else None
    return out, new_ctx

def swiglu(x, wg, wu, wd):
    return (jax.nn.silu(x @ wg) * (x @ wu)) @ wd

def routed_experts(x, idx, wts, w_gate, w_up, w_down):
    n_tok, dm = x.shape
    n_asg = n_tok * TOP_K
    flat_e = idx.reshape(-1)
    order = jnp.argsort(flat_e)
    e_sorted = flat_e[order]
    tok_sorted = order // TOP_K
    counts = jnp.bincount(flat_e, length=N_EXPERTS)
    padded = (counts + MOE_BLOCK - 1) // MOE_BLOCK * MOE_BLOCK
    pad_end = jnp.cumsum(padded)
    pad_start = pad_end - padded
    seg_start = jnp.cumsum(counts) - counts
    dest = pad_start[e_sorted] + jnp.arange(n_asg) - seg_start[e_sorted]
    n_blocks = -(-n_asg // MOE_BLOCK) + N_EXPERTS
    slot_tok = jnp.full((n_blocks * MOE_BLOCK,), n_tok, jnp.int32).at[dest].set(tok_sorted)
    block_expert = jnp.minimum(
        jnp.searchsorted(pad_end, jnp.arange(n_blocks) * MOE_BLOCK, side='right'), N_EXPERTS - 1)
    x_pad = jnp.concatenate([x, jnp.zeros((1, dm), x.dtype)], axis=0)
    xb = x_pad[slot_tok].reshape(n_blocks, MOE_BLOCK, dm)

    def expert_block(args):
        xblk, e = args
        return swiglu(xblk, w_gate[e], w_up[e], w_down[e])

    yb = lax.map(expert_block, (xb, block_expert)).reshape(-1, dm)
    y_asg = yb[dest].astype(jnp.float32) * wts.reshape(-1)[order][:, None]
    return jnp.zeros((n_tok, dm), jnp.float32).at[tok_sorted].add(y_asg).astype(x.dtype)

def moe(x, router_w, router_bias, w_gate, w_up, w_down, s_gate, s_up, s_down):
    n_tok = x.shape[0]
    scores = jax.nn.sigmoid((x @ router_w).astype(jnp.float32))
    biased = scores + router_bias.astype(jnp.float32)
    per_group = N_EXPERTS // N_GROUPS
    grp_score = jnp.sum(lax.top_k(biased.reshape(n_tok, N_GROUPS, per_group), 2)[0], axis=-1)
    _, grp_idx = lax.top_k(grp_score, TOPK_GROUPS)
    grp_sel = jnp.any(grp_idx[..., None] == jnp.arange(N_GROUPS), axis=1)
    masked = jnp.where(jnp.repeat(grp_sel, per_group, axis=1), biased, -jnp.inf)
    _, idx = lax.top_k(masked, TOP_K)
    wts = jnp.take_along_axis(scores, idx, axis=1)
    wts = wts / (jnp.sum(wts, axis=-1, keepdims=True) + 1e-20) * ROUTED_SCALE
    return routed_experts(x, idx, wts, w_gate, w_up, w_down) + swiglu(x, s_gate, s_up, s_down)

def setup_inputs(seed: int = 0) -> dict:
    key = jax.random.key(seed)
    keys = jax.random.split(key, 64)
    counter = [0]
    f32 = jnp.float32

    def nxt():
        k = keys[counter[0]]
        counter[0] += 1
        return k

    def nrm(shape, scale=1.0):
        return jax.random.normal(nxt(), shape, f32) * scale

    def unif(shape, lo, hi):
        return jax.random.uniform(nxt(), shape, f32, lo, hi)

    def gain(shape):
        return 1.0 + nrm(shape, 0.02)

    D = D_MODEL
    inp = {}
    inp['x_prompt'] = nrm((BATCH, SEQ, D))
    inp['x_sample'] = nrm((DEC_BATCH, DEC_SEQ, D))
    inp['cache_attn_k'] = nrm((DEC_BATCH, N_EVEN, A_KV_HEADS, PAST_LEN, A_DIM))
    inp['cache_attn_v'] = nrm((DEC_BATCH, N_EVEN, A_KV_HEADS, PAST_LEN, A_DIM))
    inp['state_rwkv'] = nrm((DEC_BATCH, N_EVEN, 2, B_HEADS, B_DIM, B_DIM), 0.5)
    inp['state_delta'] = nrm((DEC_BATCH, N_ODD, 2, C_HEADS, C_DIM, C_DIM), 0.1)
    inp['cache_diff_k'] = nrm((DEC_BATCH, N_ODD, D_HEADS, 2, PAST_LEN, D_DIM))
    inp['cache_diff_v'] = nrm((DEC_BATCH, N_ODD, D_HEADS, PAST_LEN, D_VDIM))
    inp['c'] = nrm((DEC_BATCH, D))
    inp['c_ctx'] = nrm((D,))
    inp['mod_w'] = nrm((DEPTH, D, 6 * D), 0.5 * D ** -0.5)
    inp['mod_b'] = nrm((DEPTH, 6 * D), 0.01)
    inp['norm1_g'] = gain((DEPTH, D))
    inp['norm2_g'] = gain((DEPTH, D))
    inp['ev_w_in'] = nrm((N_EVEN, D, EVEN_COLS), D ** -0.5)
    inp['ev_w_out'] = nrm((N_EVEN, EVEN_OUT, D), EVEN_OUT ** -0.5)
    inp['a_qn'] = gain((N_EVEN, A_DIM))
    inp['a_kn'] = gain((N_EVEN, A_DIM))
    inp['b_mu'] = unif((N_EVEN, B_COLS), 0.0, 1.0)
    inp['b_w0'] = unif((N_EVEN, 2, B_WIDTH), -6.0, 1.0)
    inp['b_w2'] = nrm((N_EVEN, 2, DECAY_LORA, B_WIDTH), 0.5 * DECAY_LORA ** -0.5)
    inp['b_a0'] = nrm((N_EVEN, 2, B_WIDTH), 0.1)
    inp['b_a2'] = nrm((N_EVEN, 2, ICLR_LORA, B_WIDTH), 0.5 * ICLR_LORA ** -0.5)
    inp['b_g2'] = nrm((N_EVEN, GATE_LORA, B_WIDTH), GATE_LORA ** -0.5)
    inp['b_kk'] = 0.85 + nrm((N_EVEN, B_WIDTH), 0.02)
    inp['b_ka'] = gain((N_EVEN, B_WIDTH))
    inp['b_rk'] = nrm((N_EVEN, B_HEADS, B_DIM), 0.1)
    inp['b_lnx_w'] = gain((N_EVEN, B_WIDTH))
    inp['b_lnx_b'] = nrm((N_EVEN, B_WIDTH), 0.01)
    inp['od_w_in'] = nrm((N_ODD, D, ODD_COLS), D ** -0.5)
    inp['od_w_out'] = nrm((N_ODD, ODD_OUT, D), ODD_OUT ** -0.5)
    inp['c_conv'] = nrm((N_ODD, CONV_W, 3 * C_WIDTH), CONV_W ** -0.5)
    inp['c_A_log'] = jnp.log(unif((N_ODD, 2, C_HEADS), 1.0, 16.0))
    dt = jnp.exp(unif((N_ODD, 2, C_HEADS), math.log(1e-3), math.log(1e-1)))
    inp['c_dt_bias'] = jnp.log(jnp.expm1(dt))
    inp['c_onorm'] = gain((N_ODD, C_DIM))
    inp['d_qn'] = gain((N_ODD, D_DIM))
    inp['d_kn'] = gain((N_ODD, D_DIM))
    inp['d_lambda'] = nrm((N_ODD, 4, D_DIM), 0.1)
    inp['d_subln'] = gain((N_ODD, D_VDIM))
    inp['router_w'] = nrm((DEPTH, D, N_EXPERTS), D ** -0.5)
    inp['router_bias'] = nrm((DEPTH, N_EXPERTS), 0.01)
    inp['exp_w_gate'] = nrm((DEPTH, N_EXPERTS, D, EXPERT_FF), D ** -0.5)
    inp['exp_w_up'] = nrm((DEPTH, N_EXPERTS, D, EXPERT_FF), D ** -0.5)
    inp['exp_w_down'] = nrm((DEPTH, N_EXPERTS, EXPERT_FF, D), EXPERT_FF ** -0.5)
    inp['sh_w_gate'] = nrm((DEPTH, D, SHARED_FF), D ** -0.5)
    inp['sh_w_up'] = nrm((DEPTH, D, SHARED_FF), D ** -0.5)
    inp['sh_w_down'] = nrm((DEPTH, SHARED_FF, D), SHARED_FF ** -0.5)
    return inp

def reference(x_prompt, x_sample, cache_attn_k, cache_attn_v, state_rwkv, state_delta, cache_diff_k,
              cache_diff_v, c, c_ctx, mod_w, mod_b, norm1_g, norm2_g, ev_w_in, ev_w_out, a_qn, a_kn, b_mu,
              b_w0, b_w2, b_a0, b_a2, b_g2, b_kk, b_ka, b_rk, b_lnx_w, b_lnx_b, od_w_in, od_w_out, c_conv,
              c_A_log, c_dt_bias, c_onorm, d_qn, d_kn, d_lambda, d_subln, router_w, router_bias, exp_w_gate,
              exp_w_up, exp_w_down, sh_w_gate, sh_w_up, sh_w_down):
    xc, xl = x_prompt, x_sample
    n_ctx_tok = xc.shape[0] * xc.shape[1]
    new_ak, new_av, new_sr, new_sd, new_dk, new_dv = [], [], [], [], [], []
    for l in range(DEPTH):
        mc = adaln(c_ctx[None], mod_w[l], mod_b[l])
        ml = adaln(c, mod_w[l], mod_b[l])
        hc = modulate(rms_norm(xc, norm1_g[l]), mc[:, None, 0], mc[:, None, 1]).astype(xc.dtype)
        hl = modulate(rms_norm(xl, norm1_g[l]), ml[:, None, 0], ml[:, None, 1]).astype(xl.dtype)
        j = l // 2
        if l % 2 == 0:
            p = {'w_in': ev_w_in[j], 'w_out': ev_w_out[j], 'a_qn': a_qn[j], 'a_kn': a_kn[j], 'b_mu': b_mu[j],
                 'b_w0': b_w0[j], 'b_w2': b_w2[j], 'b_a0': b_a0[j], 'b_a2': b_a2[j], 'b_g2': b_g2[j],
                 'b_kk': b_kk[j], 'b_ka': b_ka[j], 'b_rk': b_rk[j], 'b_lnx_w': b_lnx_w[j], 'b_lnx_b': b_lnx_b[j]}
            oc, (ak, av, sr) = even_mixer(hc, p)
            ol, _ = even_mixer(hl, p, (cache_attn_k[:, j], cache_attn_v[:, j], state_rwkv[:, j]))
            new_ak.append(ak)
            new_av.append(av)
            new_sr.append(sr)
        else:
            lam_init = 0.8 - 0.6 * math.exp(-0.3 * l)
            p = {'w_in': od_w_in[j], 'w_out': od_w_out[j], 'c_conv': c_conv[j], 'c_A_log': c_A_log[j],
                 'c_dt_bias': c_dt_bias[j], 'c_onorm': c_onorm[j], 'd_qn': d_qn[j], 'd_kn': d_kn[j],
                 'd_lambda': d_lambda[j], 'd_subln': d_subln[j]}
            oc, (dk, dv, sd) = odd_mixer(hc, p, lam_init)
            ol, _ = odd_mixer(hl, p, lam_init, (cache_diff_k[:, j], cache_diff_v[:, j], state_delta[:, j]))
            new_dk.append(dk)
            new_dv.append(dv)
            new_sd.append(sd)
        xc = (xc + mc[:, None, 2] * oc).astype(x_prompt.dtype)
        xl = (xl + ml[:, None, 2] * ol).astype(x_sample.dtype)
        hc2 = modulate(rms_norm(xc, norm2_g[l]), mc[:, None, 3], mc[:, None, 4]).astype(xc.dtype)
        hl2 = modulate(rms_norm(xl, norm2_g[l]), ml[:, None, 3], ml[:, None, 4]).astype(xl.dtype)
        tok = jnp.concatenate([hc2.reshape(-1, D_MODEL), hl2.reshape(-1, D_MODEL)], axis=0)
        f = moe(tok, router_w[l], router_bias[l], exp_w_gate[l], exp_w_up[l], exp_w_down[l],
                sh_w_gate[l], sh_w_up[l], sh_w_down[l])
        xc = (xc + mc[:, None, 5] * f[:n_ctx_tok].reshape(xc.shape)).astype(x_prompt.dtype)
        xl = (xl + ml[:, None, 5] * f[n_ctx_tok:].reshape(xl.shape)).astype(x_sample.dtype)
    st_dtype = x_prompt.dtype
    return (xc, xl, jnp.stack(new_ak, axis=1), jnp.stack(new_av, axis=1),
            jnp.stack(new_sr, axis=1).astype(st_dtype), jnp.stack(new_sd, axis=1).astype(st_dtype),
            jnp.stack(new_dk, axis=1), jnp.stack(new_dv, axis=1))


_drawn_inputs = setup_inputs


def setup_inputs(seed=0):
    import zlib

    import numpy as np

    out = dict(_drawn_inputs(seed))
    spreads = {}
    factors = {'cache_attn_k': 3.522,
     'cache_attn_v': 2.983,
     'state_rwkv': 2.894,
     'a_qn': 8.0,
     'a_kn': 2.871,
     'b_lnx_w': 8.0,
     'b_lnx_b': 8.0,
     'c_onorm': 38.351,
     'd_qn': 8.0,
     'd_kn': 2.763,
     'd_lambda': 5.131,
     'd_subln': 38.312,
     'cache_diff_k': 8.0,
     'cache_diff_v': 8.0}
    for name, (base, spread) in spreads.items():
        noise = np.random.default_rng([zlib.crc32(name.encode()), seed]).standard_normal(out[name].shape)
        drawn = base * np.exp(spread * noise) if base else spread * noise
        out[name] = jnp.asarray(drawn.astype(out[name].dtype))
    for name, factor in factors.items():
        out[name] = (out[name] * factor).astype(out[name].dtype)
    return out
```

```python
import math
from contextlib import ExitStack

import numpy as np
import concourse.bass as bass
from concourse import mybir

F32 = mybir.dt.float32
ALU = mybir.AluOpType
ACT = mybir.ActivationFunctionType
AX = mybir.AxisListType

P = 128
D = 1024
J = D // P
TILES = 3
NTOK = TILES * P
LAYERS = 2
EXPERTS = 64
FF = 256
GROUPS = 8
TOP_GROUPS = 4
TOP_K = 6
HEAD = 64
EVEN_COLS = 2560
ODD_COLS = 3600
EVEN_BLOCKS = [(0, 512), (512, 768), (768, 1280), (1280, 1792), (1792, 2304), (2304, 2560)]
ODD_BLOCKS = [(0, 512), (512, 1024), (1024, 1536), (1536, 2048), (2048, 2064), (2064, 2576), (2576, 3088),
              (3088, 3600)]
XB = 768
XR, XK, XV, XW, XG = 768, 1280, 1792, 2304, 2432
CQ, CK, CV, CZ, CAB, DQ, DV = 0, 512, 1024, 1536, 2048, 2064, 3088
DECAY = math.exp(-0.5)
LAM_INIT = 0.8 - 0.6 * math.exp(-0.3 * 1)
RING = 6
SLOT = 2048
LEVELS = 7

CONSTS = ["ident", "ones", "strict0", "incl0", "strict1", "incl1", "cum_incl0", "cum_excl0", "cum_incl1",
          "cum_excl1", "prev", "next", "both", "from_prev", "from_next"] + [f"join{k}" for k in range(LEVELS)]
NCOL = 72


def constants():
    s = np.arange(P)[:, None]
    t = np.arange(P)[None, :]
    half = P // 2
    m = {"ident": s == t, "ones": s == s, "strict0": s < t, "incl0": s <= t, "strict1": s > t, "incl1": s >= t,
         "prev": s == t - 1, "next": s == t + 1, "both": abs(s - t) == 1,
         "from_prev": (s == P - 1) & (t == 0), "from_next": (s == 0) & (t == P - 1)}
    for d, first in ((0, s < half), (1, s >= half)):
        m[f"cum_incl{d}"] = m[f"incl{d}"].astype(np.float32) - first
        m[f"cum_excl{d}"] = m[f"strict{d}"].astype(np.float32) - first
    for k in range(LEVELS):
        m[f"join{k}"] = (s >> (k + 1) == t >> (k + 1)) & (s >> k != t >> k)
    full = np.zeros((P, len(CONSTS) * P + NCOL), np.float32)
    for i, n in enumerate(CONSTS):
        full[:, i * P:(i + 1) * P] = m[n] * np.ones((P, P), np.float32)
    o = len(CONSTS) * P
    full[:half, o] = 1
    full[half:, o + 1] = 1
    full[:, o + 2] = 1e-6
    full[:, o + 3] = 64e-5
    full[:, o + 4] = 1.0
    full[:, o + 8:o + 72] = (np.arange(GROUPS)[None, :] < np.arange(GROUPS)[:, None]).reshape(-1)
    return full


def rope_rows():
    n = 2 * P
    f = HEAD // 4
    inv = (np.float32(10000.0) ** (-np.arange(f, dtype=np.float32) / f)).astype(np.float32)
    row = (np.arange(n) // 64).astype(np.float32)
    col = (np.arange(n) % 64).astype(np.float32)
    ang = np.concatenate([row[:, None] * inv, col[:, None] * inv], 1)
    c, s = np.cos(ang), np.sin(ang)
    out = np.zeros((n, 2, HEAD), np.float32)
    out[:, 0, 0::2] = c
    out[:, 0, 1::2] = c
    out[:, 1, 0::2] = -s
    out[:, 1, 1::2] = s
    return out


def weight_pieces(w):
    pieces, group = [], []

    def add(srcs):
        g = group[-1] + 1 if group else 0
        for s in srcs:
            pieces.append(s)
            group.append(g)

    starts = []
    for l in range(LAYERS):
        mod = w["mod_w"][l].rearrange("(p c) n -> p c n", c=J)
        for s in range(6):
            add([mod[:, 2 * q:2 * q + 2, s * D:(s + 1) * D] for q in range(4)])
        win = (w["ev_w_in"] if l % 2 == 0 else w["od_w_in"])[0].rearrange("(p c) n -> p c n", c=J)
        for a, b in (EVEN_BLOCKS if l % 2 == 0 else ODD_BLOCKS):
            if b - a > 256:
                add([win[:, 0:4, a:b], win[:, 4:8, a:b]])
            else:
                add([win[:, :, a:b]])
        wout = (w["ev_w_out"] if l % 2 == 0 else w["od_w_out"])[0].rearrange("(p c) n -> p c n", c=J)
        add([wout[:, 2 * q:2 * q + 2, :] for q in range(4)])
        add([w["sh_w_gate"][l].rearrange("(p c) n -> p c n", c=J), w["sh_w_up"][l].rearrange("(p c) n -> p c n", c=J)])
        add([w["sh_w_down"][l].rearrange("(p c) n -> p c n", c=2)])
        starts.append(len(pieces))
        for _ in range(EXPERTS):
            pieces += [None] * 3
            group += [group[-1] + 1, group[-1] + 1, group[-1] + 2]
    return pieces, group, starts


def build(nc, w, outs):
    with ExitStack() as ctx:
        def sb(name, shape):
            return ctx.enter_context(nc.sbuf_tensor(name, shape, F32))

        sems = {}

        def sem(*name):
            n = "_".join(str(x) for x in name)
            if n not in sems:
                sems[n] = ctx.enter_context(nc.semaphore(n))
            return sems[n]

        consts = sb("consts", [P, len(CONSTS) * P + NCOL])
        xT = sb("xT", [P, J, NTOK])
        hT = sb("hT", [P, J, NTOK])
        mixed = sb("mixed", [P, TILES, D])
        params = sb("params", [P, 6176])
        ring = sb("ring", [P, RING, SLOT])
        cond = sb("cond", [P, J, 2])
        cond_exp = sb("cond_exp", [P, J, 2])
        mod_b = sb("mod_b", [P, LAYERS, 6, J])
        gains = sb("gains", [P, LAYERS, 2, J])
        mods = sb("mods", [P, 6, J, 2])
        rope = sb("rope", [P, 2, 2, HEAD])
        rstd = sb("rstd", [P, NTOK])
        stats = sb("stats", [P, 128])
        arena = sb("arena", [P, 21200])
        bank = [ctx.enter_context(nc.psum_tensor(f"bank{i}", [P, 512], F32)) for i in range(8)]
        wt_dram = nc.dram_tensor("routing_rows", [LAYERS, EXPERTS, NTOK], F32).ap()

        C = {n: consts[:, i * P:(i + 1) * P] for i, n in enumerate(CONSTS)}
        c0 = len(CONSTS) * P
        halves = consts[:, c0:c0 + 2]
        eps6, eps_ln, one_col = (consts[:, c0 + i:c0 + i + 1] for i in (2, 3, 4))
        lower_index = consts[:, c0 + 8:c0 + 72].rearrange("p (i j) -> p i j", i=GROUPS)
        masks = [consts[:, (2 + 2 * d) * P:(4 + 2 * d) * P] for d in range(2)]

        def region(*sizes, at=0):
            got = []
            for n in sizes:
                got.append((at, n))
                at += n
            assert at <= 21200, at
            return [arena[:, a:a + n] for a, n in got]

        def hregion(a, n):
            return hT[:, :, :].rearrange("p j n -> p (j n)")[:, a:a + n]

        def heads(ap, n):
            return ap.rearrange("p (h d) -> p h d", h=n)

        def along(ap, n):
            return ap.unsqueeze(len(ap.shape)).broadcast_to(list(ap.shape) + [n])

        pieces, group, loops = weight_pieces(w)

        def slot(n):
            return ring[:, n % RING, :]

        def piece_value(n):
            return 16 * (n // RING + 1)

        first = []
        for l in range(LAYERS):
            s = loops[l - 1] + 3 * EXPERTS if l else 0
            f = {"mod": s, "in": s + 24}
            f["shared"] = loops[l] - 3
            f["out"] = loops[l] - 7
            first.append(f)

        block = ctx.enter_context(nc.Block())

        MEMBERS = ("pe", "act", "dve")

        def phase_end(me, eng, n):
            eng.drain().then_inc(sem("phase_done", me), 1)
            for other in MEMBERS:
                if other != me:
                    eng.wait_ge(sem("phase_done", other), n)

        def proj_of(l):
            cols = EVEN_COLS if l % 2 == 0 else ODD_COLS
            return arena[:, 0:TILES * cols].rearrange("p (t n) -> p t n", t=TILES), TILES * cols

        def projected(l, t, a, b, src):
            dst, src = proj_of(l)[0][:, t, a:b], src[:, 0:b - a]
            if l % 2 == 0 and a == 0:
                return (dst.rearrange("p (j k d) -> p k j d", j=4, k=2), src.rearrange("p (k j d) -> p k j d", j=4, k=2))
            return dst, src

        squares = arena[:, 0:J * NTOK].rearrange("p (j n) -> p j n", j=J)

        def load_experts(sp, l):
            n0 = loops[l]
            with sp.Fori(0, EXPERTS // 2) as i:
                for k in range(6):
                    e = i * 2 + k // 3
                    src = w[("exp_w_gate", "exp_w_up", "exp_w_down")[k % 3]]
                    c = 2 if k % 3 == 2 else J
                    sp.wait_ge(sem("ring_released"), i * 4 + (group[n0 + k - RING] + 1))
                    sp.dma_start(slot(n0 + k).rearrange("p (c k) -> p c k", c=c),
                                 src[l, bass.ds(e, 1)].rearrange("e (p c) n -> (e p) c n", c=c))\
                        .then_inc(sem("ring_loaded", (n0 + k) % RING), 16)

        @block.sync
        def _(sp):
            sp.dma_start(xT[:, :, :], w["xT"]).then_inc(sem("x_loaded"), 16)
            for n, src in enumerate(pieces):
                if src is None:
                    continue
                _, c, k = src.shape
                if n >= RING:
                    sp.wait_ge(sem("ring_released"), group[n - RING] + 1)
                sp.dma_start(slot(n)[:, 0:c * k].rearrange("p (c k) -> p c k", c=c), src)\
                    .then_inc(sem("ring_loaded", n % RING), 16)
                if n + 1 in loops:
                    l = loops.index(n + 1)
                    load_experts(sp, l)
            sp.wait_ge(sem("x_ready"), 2 * LAYERS)
            sp.dma_start(outs["yT"], xT[:, :, :]).then_inc(sem("stored"), 16)
            sp.wait_ge(sem("stored"), 16 * 7)

        RWKV_UNITS = [(0, 0), (0, 1), (1, 0), (2, 1), (2, 0), (1, 1)]
        DELTA_STEPS = [[(0, 0), (0, 1)], [(1, 0), (2, 1)], [(2, 0), (1, 1)]]
        RWKV_KEEPS = (0, 1, 2, 3)
        DELTA_KEEPS = (0, 1)

        class Attention:
            def __init__(self, l):
                self.l = l
                self.even = l % 2 == 0
                self.proj, po = proj_of(l)
                self.base = 0 if self.even else DQ
                self.nh = 10 if self.even else 16
                self.kc = 1 if self.even else 4
                self.vd = 64 if self.even else 128
                self.vbase = 640 if self.even else DV
                nkv = 2 if self.even else 4
                (self.qt, self.kctx, self.klat, self.vc, self.p, self.pt, self.t1, self.t2, self.ss, self.mx,
                 self.sums, self.rinv, self.neg) = region(1536, self.kc * 128, self.kc * 384, nkv * self.vd, 768, 768,
                                                          1024, 1024, 48, 24, 24, 24, 8, at=po)
                self.qt = self.qt.rearrange("p (t c n) -> p t c n", t=TILES, c=4)
                self.kctx = self.kctx.rearrange("p (c n) -> p c n", c=self.kc)
                self.klat = self.klat.rearrange("p (c t n) -> p c t n", c=self.kc, t=TILES)
                self.vc = self.vc.rearrange("p (h d) -> p h d", h=nkv)
                self.p = self.p.rearrange("p (b n) -> p b n", b=2)
                self.pt = self.pt.rearrange("p (b n) -> p b n", b=2)
                self.gain = params[:, 0:640] if self.even else params[:, 4608:5632]
                self.per_bank = 512 // self.vd

            def qk(self, t):
                return self.proj[:, t, self.base:self.base + 64 * self.nh]

            def unit(self, u):
                t, h = divmod(u, 8)
                kt = 1 if t == 0 else 3
                if self.even:
                    return t, kt, h % 4, 64 * (h // 4), 0, h // 4
                return t, kt, h // 2, 64 * (h % 2), h // 2, h // 2

            def values(self, t, kt, vh):
                if t > 0 and kt == 0:
                    return self.vc[:, vh, :]
                src = 0 if t == 0 else kt
                return self.proj[:, src, self.vbase + vh * self.vd:self.vbase + (vh + 1) * self.vd]

        attention = [Attention(l) for l in range(LAYERS)]

        class Inverse:
            def __init__(self, nt, off, t, tt, m1):
                four = lambda aps: [a.rearrange("p (h n) -> p h n", h=4) if len(a.shape) == 2 else a for a in aps]
                self.nt, self.off, self.t, self.tt, self.m1 = nt, four(off), four(t), four(tt), four(m1)

            def sem(self, name, g):
                return sem("inverse", name, g)

        proj0, po0 = proj_of(0)
        (r_ar, r_bt, r_kt, r_tokb, r_tokk, r_toka, r_tokr, r_nr0, r_nr1, r_ak0, r_ak1, *r_inv, r_rs, r_us) = region(
            1024, 512, 512, 512, 512, 512, 512, 1024, 1024, 1024, 1024, *([512] * 8), 512, 512, at=po0)
        r_ar = r_ar.rearrange("p (c k n) -> p c k n", c=4, k=2)
        r_bt, r_kt = (a.rearrange("p (c n) -> p c n", c=4) for a in (r_bt, r_kt))
        r_nr = [a.rearrange("p (c k n) -> p c k n", c=4, k=2) for a in (r_nr0, r_nr1)]
        r_ak = [a.rearrange("p (c k n) -> p c k n", c=4, k=2) for a in (r_ak0, r_ak1)]
        r_inverse = Inverse([a[:, :, 0, :] for a in r_nr], r_inv[0:2], r_inv[2:4], r_inv[4:6], r_inv[6:8])
        r_sig, r_gate, r_ei, r_ev, r_ee, r_x = r_inv[0:6]
        r_rs, r_us = (a.rearrange("p (h d) -> p h d", h=8) for a in (r_rs, r_us))
        r_lora, r_w0, r_a0 = hregion(0, 1024), hregion(1024, 1024), hregion(2048, 1024)
        r_mu = params[:, 640:2432]
        r_kk, r_ka, r_rk, r_lnw, r_lnb, r_g2 = (params[:, 2432 + 512 * i:2944 + 512 * i] for i in range(6))
        state4 = lambda ap: ap.rearrange("p (d j v) -> p d j v", d=2, j=4)
        r_sl = state4(params[:, 5504:6016])
        r_sc = state4(params[:, 640:1152])
        r_sw = params[:, 1152:1408].rearrange("p (j v) -> p j v", j=4)
        r_ec = params[:, 1408:1416].rearrange("p (j h) -> p j h", j=4)
        kk_of = lambda t: proj0[:, t, 0:512]
        lt_of = lambda t: proj0[:, t, 512:640]
        gt_of = lambda t: proj0[:, t, 640:768]
        yacc_of = lambda t: mixed[:, t, 512:1024]

        proj1, po1 = proj_of(1)
        d_buf = [region(*([512] * 10), at=po1 + g * 5120) for g in range(2)]
        d_di, d_at, d_n, d_off, d_t, d_tt, d_m1, d_rs, d_vn, d_kg = (
            [b[i].rearrange("p (h n) -> p h n", h=4) for b in d_buf] for i in range(10))
        d_inverse = Inverse(d_n, d_off, d_t, d_tt, d_m1)
        d_kt = hregion(0, 1536).rearrange("p (t h n) -> p t h n", t=TILES, h=4)
        d_qt = hregion(1536, 1536).rearrange("p (t h n) -> p t h n", t=TILES, h=4)
        d_sl = params[:, 0:1024].rearrange("p (d h v) -> p d h v", d=2, h=4)
        d_sc = params[:, 1024:2048].rearrange("p (d h v) -> p d h v", d=2, h=4)
        small = lambda i: params[:, 2048 + 24 * i:2072 + 24 * i].rearrange("p (t d h) -> p t d h", t=TILES, d=2)
        d_g, d_beta, d_tmp, d_gc, d_eg, d_es, d_et, d_neg = (small(i) for i in range(8))
        conv_w = params[:, 0:4608].rearrange("p (k n) -> p k n", k=3)
        conv_exp = lambda t: arena[:, po1 + 1536 * t:po1 + 1536 * (t + 1)]
        conv_tmp = arena[:, po1 + 4608:po1 + 5632]
        silu_z = arena[:, po1 + 1536:po1 + 3072].rearrange("p (t n) -> p t n", t=TILES)

        m_w, m_sc, m_bi, m_mk, m_eq, m_t0, m_cum = (
            a.rearrange("p (t e) -> p t e", t=TILES) for a in region(*([192] * 7), at=3072))
        m_small, = region(256, at=3072 + 7 * 192)
        m_rank = region(192, 192, at=3072 + 7 * 192 + 256)
        m_bias, m_router, m_wt = region(64, 512, 384, at=3072 + 9 * 192 + 256)
        m_bias_buf = m_bias
        m_bias = m_bias.unsqueeze(1).broadcast_to([P, TILES, EXPERTS])
        m_router = m_router.rearrange("p (c e) -> p c e", c=J)
        m_at = 3072 + 9 * 192 + 256 + 960
        x_bc0, x_bc1, x_e0, x_e1, x_h0, x_h1, x_g, x_one = region(*([NTOK] * 8), at=m_at + 64)
        x_bc, x_e, x_h = [x_bc0, x_bc1], [x_e0, x_e1], [x_h0, x_h1]
        x_y = arena[:, m_at + 64 + 8 * NTOK:m_at + 64 + 8 * NTOK + 3072].rearrange("p (t n) -> p t n", t=TILES)

        @block.tensor
        def _(pe):
            phase = [0]
            used = [0]

            def mm(out, lhsT, rhs, start=True, stop=True, **kw):
                return nc.tensor.matmul(out, lhsT, rhs, start=start, stop=stop, **kw)

            def end_phase():
                phase[0] += 1
                phase_end("pe", pe, phase[0])

            def loaded(n):
                pe.wait_ge(sem("ring_loaded", n % RING), piece_value(n))

            def rows(n, per, width):
                return slot(n)[:, 0:per * width].rearrange("p (c k) -> p c k", c=per)

            def modulation(l):
                pe.wait_ge(sem("cond_ready"), 1)
                n0 = first[l]["mod"]
                for s in range(6):
                    for q in range(4):
                        loaded(n0 + 4 * s + q)
                    for j in range(J):
                        o = (s * J + j) * 2
                        for c in range(J):
                            lhs = rows(n0 + 4 * s + c // 2, 2, D)[:, c % 2, j::J]
                            last = mm(bank[0][:, o:o + 2], lhs, cond[:, c, :], c == 0, c == J - 1)
                    last.then_inc(sem("ring_released"), 1)
                end_phase()

            def norm(n):
                pe.wait_ge(sem("squares_ready"), n)
                for c in range(J):
                    last = mm(bank[1][:, 0:NTOK], C["ones"], squares[:, c, :], c == 0, c == J - 1)
                last.then_inc(sem("sumsq_ready"), 1)

            def projection(l):
                pe.wait_ge(sem("h_ready"), 2 * l + 1)
                n = first[l]["in"]
                k = 0
                for a, b in (EVEN_BLOCKS if l % 2 == 0 else ODD_BLOCKS):
                    wide = b - a > 256
                    loaded(n)
                    if wide:
                        loaded(n + 1)
                    for t in range(TILES):
                        if k >= 6:
                            pe.wait_ge(sem("proj_saved", k % 2), 9 * l + (k - 6) // 2 + 1)
                        for c in range(J):
                            rhs = rows(n + c // 4, 4, b - a)[:, c % 4, :] if wide else rows(n, J, b - a)[:, c, :]
                            last = mm(bank[k % 6][:, 0:b - a], hT[:, c, t * P:(t + 1) * P], rhs, c == 0, c == J - 1)
                        last.then_inc(sem("proj_ready"), 1)
                        k += 1
                    n += 2 if wide else 1
                    pe.drain().then_inc(sem("ring_released"), 1)
                end_phase()

            def token_shift():
                for b in range(4):
                    cols = slice(XB + 448 * b, XB + 448 * (b + 1))
                    if b >= 2:
                        pe.wait_ge(sem("near_saved"), b - 1)
                    for t in range(TILES):
                        out = bank[3 * (b % 2) + t][:, 0:448]
                        last = mm(out, C["both"], proj0[:, t, cols], True, t == 0)
                        if t == 1:
                            last = mm(out, C["from_next"], proj0[:, 2, cols], False, True)
                        if t == 2:
                            last = mm(out, C["from_prev"], proj0[:, 1, cols], False, True)
                    last.then_inc(sem("near_ready"), 1)

            def convolution():
                for b in range(3):
                    cols = slice(512 * b, 512 * (b + 1))
                    if b >= 1:
                        pe.wait_ge(sem("near_saved"), 4 + b)
                    for t in range(TILES):
                        mm(bank[t][:, :], C["prev"], proj1[:, t, cols], True, t != 2)
                        if t == 2:
                            mm(bank[t][:, :], C["from_prev"], proj1[:, 1, cols], False, True)
                        last = mm(bank[3 + t][:, :], C["next"], proj1[:, t, cols], True, t != 1)
                        if t == 1:
                            last = mm(bank[3 + t][:, :], C["from_next"], proj1[:, 2, cols], False, True)
                    last.then_inc(sem("near_ready"), 1)

            def attend(l):
                A = attention[l]
                for t in range(TILES):
                    pe.wait_ge(sem("qk_ready"), TILES * l + t + 1)
                    for c in range(4):
                        src = A.qk(t)[:, 128 * c:128 * (c + 1)]
                        nc.tensor.transpose(bank[2 * t][:, 128 * c:128 * (c + 1)], src, C["ident"])
                    for c in range(A.kc):
                        k0 = 512 + 128 * c
                        last = nc.tensor.transpose(bank[2 * t + 1][:, 128 * c:128 * (c + 1)], A.qk(t)[:, k0:k0 + 128],
                                                   C["ident"])
                    last.then_inc(sem("qkT_ready"), 1)

                def scores(u):
                    t, kt, qc, p0, kc, _ = A.unit(u)
                    if u == 0:
                        pe.wait_ge(sem("keys_loaded"), 32 * l + 32)
                        pe.wait_ge(sem("qT_saved"), TILES * l + TILES)
                        pe.wait_ge(sem("kT_saved"), TILES * l + TILES)
                    if u >= 2:
                        pe.wait_ge(sem("p_ready"), 24 * l + u - 1)
                    rhs = (A.kctx[p0:p0 + 64, kc, :] if kt == 1 else A.klat[p0:p0 + 64, kc, :, :])
                    mm(bank[u % 2][:, 0:kt * P], A.qt[p0:p0 + 64, t, qc, :], rhs).then_inc(sem("s_ready"), 1)

                def turn(u):
                    _, kt, *_ = A.unit(u)
                    pe.wait_ge(sem("p_ready"), 24 * l + u + 1)
                    if u >= 2:
                        pe.wait_ge(sem("pT_saved"), 24 * l + u - 1)
                    for k in range(kt):
                        last = nc.tensor.transpose(bank[2 + u % 2][:, k * P:(k + 1) * P],
                                                   A.p[:, u % 2, k * P:(k + 1) * P], C["ident"])
                    last.then_inc(sem("pT_ready"), 1)

                def weigh(u):
                    t, kt, _, _, _, vh = A.unit(u)
                    g, r = divmod(u, A.per_bank)
                    pe.wait_ge(sem("pT_saved"), 24 * l + u + 1)
                    if r == 0 and g >= 2:
                        pe.wait_ge(sem("o_saved"), 3 * l + g - 1)
                    for k in range(kt):
                        last = mm(bank[4 + g % 2][:, r * A.vd:(r + 1) * A.vd], A.pt[:, u % 2, k * P:(k + 1) * P],
                                  A.values(t, k, vh), k == 0, k == kt - 1)
                    last.then_inc(sem("o_ready"), 1)

                for u in range(26):
                    if u < 24:
                        scores(u)
                    if 1 <= u <= 24:
                        turn(u - 1)
                    if u >= 2:
                        weigh(u - 2)
                end_phase()

            def invert(inv, n, groups=(0, 1)):
                for g in groups:
                    pe.wait_ge(inv.sem("off_ready", g), 7 * n + 1)
                    for h in range(4):
                        last = nc.tensor.transpose(bank[2 + g][:, h * P:(h + 1) * P], inv.off[g][:, h, :], C["ident"])
                    last.then_inc(inv.sem("turned", g), 1)
                for k in range(1, LEVELS):
                    for g in groups:
                        pe.wait_ge(inv.sem("off_ready", g), 7 * n + k + 1)
                        pe.wait_ge(inv.sem("t_ready", g), 7 * n + k)
                        for h in range(4):
                            last = mm(bank[g][:, h * P:(h + 1) * P], inv.off[g][:, h, :], inv.t[g][:, h, :])
                        last.then_inc(inv.sem("m_ready", g), 1)
                    for g in groups:
                        pe.wait_ge(inv.sem("m_saved", g), 6 * n + k)
                        for h in range(4):
                            if k < LEVELS - 1:
                                mm(bank[2 + g][:, h * P:(h + 1) * P], inv.tt[g][:, h, :], inv.m1[g][:, h, :])
                            last = mm(bank[4 + g][:, h * P:(h + 1) * P], inv.m1[g][:, h, :], inv.tt[g][:, h, :])
                        last.then_inc(inv.sem("join_ready", g), 1)

            def rwkv():
                for t in range(TILES):
                    pe.wait_ge(sem("lora_ready"), 1)
                    if t >= 1:
                        pe.wait_ge(sem("lora_saved"), t)
                    nc.tensor.transpose(bank[0][:, 0:P], proj0[:, t, XW:XW + P], C["ident"])
                    nc.tensor.transpose(bank[0][:, P:2 * P], proj0[:, t, XG:XG + P], C["ident"])\
                        .then_inc(sem("lora_turned"), 1)
                pe.wait_ge(sem("rwkv_loaded"), 16 * 6)
                for u, (t, d) in enumerate(RWKV_UNITS):
                    pe.wait_ge(sem("lora_saved"), TILES)
                    if u:
                        pe.wait_ge(sem("unit_saved"), u)
                    mm(bank[0][:, :], lt_of(t)[0:64, :], r_lora[0:64, 512 * d:512 * (d + 1)])
                    mm(bank[1][:, :], lt_of(t)[64:128, :], r_lora[64:128, 512 * d:512 * (d + 1)])\
                        .then_inc(sem("za_ready"), 1)
                    pe.wait_ge(sem("sig_ready"), u + 1)
                    mm(bank[2][:, :], C[f"cum_incl{d}"], r_sig)
                    mm(bank[3][:, :], C[f"cum_excl{d}"], r_sig)
                    for j in range(4):
                        last = mm(bank[4][:, 2 * j:2 * j + 2], r_sig[:, 128 * j:128 * (j + 1)], halves)
                    last.then_inc(sem("cum_ready"), 1)
                    pe.wait_ge(sem("tok_ready"), u + 1)
                    for b, src in enumerate((r_toka, r_tokr, r_tokb, r_tokk)):
                        for j in range(4):
                            last = nc.tensor.transpose(bank[b][:, j * P:(j + 1) * P], src[:, j * P:(j + 1) * P], C["ident"])
                    last.then_inc(sem("tokT_ready"), 1)
                    pe.wait_ge(sem("arT_saved"), u + 1)
                    pe.wait_ge(sem("bkT_saved"), u + 1)
                    for g in range(2):
                        p = slice(64 * g, 64 * g + 64)
                        if g:
                            pe.wait_ge(sem("gram_saved"), 2 * u + g)
                        for j in range(4):
                            mm(bank[4 + j // 2][:, 256 * (j % 2):256 * (j % 2) + 256], r_bt[p, j, :], r_ar[p, j, :, :])
                            last = mm(bank[6 + j // 2][:, 256 * (j % 2):256 * (j % 2) + 256], r_kt[p, j, :],
                                      r_ar[p, j, :, :])
                        last.then_inc(sem("gram_ready"), 1)
                    pe.wait_ge(sem("gram_saved"), 2 * u + 2)
                    for g in range(2):
                        p = slice(64 * g, 64 * g + 64)
                        for j in range(4):
                            h = 2 * j + g
                            v = proj0[:, t, XV + 64 * h:XV + 64 * h + 64]
                            out = bank[6 + g][:, 64 * j:64 * j + 64]
                            if t:
                                mm(out, r_ar[p, j, 0, :], r_sw[p, j, :], True, False)
                            last = mm(out, r_ak[g][:, j, 0, :], v, t == 0, True)
                    last.then_inc(sem("read_ready"), 1)
                    invert(r_inverse, u)
                    pe.wait_ge(sem("read_saved"), u + 1)
                    for g in range(2):
                        pe.wait_ge(r_inverse.sem("t_ready", g), 7 * (u + 1))
                        for j in range(4):
                            last = mm(bank[g][:, 64 * j:64 * j + 64], r_inverse.tt[g][:, j, :], r_rs[:, 2 * j + g, :])
                    last.then_inc(sem("u_ready"), 1)
                    pe.wait_ge(sem("u_saved"), u + 1)
                    for g in range(2):
                        p = slice(64 * g, 64 * g + 64)
                        for j in range(4):
                            h = 2 * j + g
                            v = proj0[:, t, XV + 64 * h:XV + 64 * h + 64]
                            out = bank[2 + g][:, 64 * j:64 * j + 64]
                            if t:
                                mm(out, r_ar[p, j, 1, :], r_sw[p, j, :], True, False)
                            mm(out, r_nr[g][:, j, 1, :], r_us[:, h, :], t == 0, False)
                            last = mm(out, r_ak[g][:, j, 1, :], v, False, True)
                            if u in RWKV_KEEPS:
                                out = bank[4 + g][p, 64 * j:64 * j + 64]
                                mm(out, r_tokb[:, 64 * h:64 * h + 64], r_us[:, h, :], True, False)
                                last = mm(out, r_tokk[:, 64 * h:64 * h + 64], v, False, True)
                    last.then_inc(sem("y_unit_ready"), 1)
                pe.wait_ge(sem("unit_saved"), 6)
                for t in range(TILES):
                    last = mm(bank[t][:, :], gt_of(t), r_g2)
                last.then_inc(sem("gate_ready"), 1)
                end_phase()

            def delta():
                for t in range(TILES):
                    pe.wait_ge(sem("ck_ready"), 1)
                    for h in range(4):
                        nc.tensor.transpose(bank[2 * t][:, h * P:(h + 1) * P], proj1[:, t, CK + h * P:CK + (h + 1) * P],
                                            C["ident"])
                        last = nc.tensor.transpose(bank[2 * t + 1][:, h * P:(h + 1) * P],
                                                   proj1[:, t, CQ + h * P:CQ + (h + 1) * P], C["ident"])
                    last.then_inc(sem("ckT_ready"), 1)
                pe.wait_ge(sem("g_ready"), 1)
                for t in range(TILES):
                    for d in range(2):
                        for i, m in enumerate((f"incl{d}", f"strict{1 - d}", "ones")):
                            o = ((i * TILES + t) * 2 + d) * 4
                            last = mm(bank[6][:, o:o + 4], C[m], d_g[:, t, d, :])
                last.then_inc(sem("gsum_ready"), 1)
                for n, step in enumerate(DELTA_STEPS):
                    if n:
                        pe.wait_ge(sem("step_saved"), 2 * n)
                    else:
                        pe.wait_ge(sem("ckT_saved"), TILES)
                        pe.wait_ge(sem("cqT_saved"), TILES)
                        pe.wait_ge(sem("decay_cols_ready"), 1)
                    for g, (t, d) in enumerate(step):
                        pe.wait_ge(sem("gi_ready", g), n + 1)
                        mm(bank[g][:, :], C["ones"], d_t[g].rearrange("p h n -> p (h n)"))
                        for h in range(4):
                            mm(bank[2 + g][:, h * P:(h + 1) * P], d_kt[:, t, h, :], d_kt[:, t, h, :])
                            last = mm(bank[4 + g][:, h * P:(h + 1) * P], d_qt[:, t, h, :], d_kt[:, t, h, :])
                        last.then_inc(sem("dgram_ready", g), 1)
                    for g, (t, d) in enumerate(step):
                        pe.wait_ge(sem("na_ready", g), n + 1)
                        for h in range(4):
                            nc.tensor.transpose(bank[g][:, h * P:(h + 1) * P], d_m1[g][:, h, :], C["ident"])
                            last = nc.tensor.transpose(bank[2 + g][:, h * P:(h + 1) * P], d_tt[g][:, h, :], C["ident"])
                        last.then_inc(sem("naT_ready", g), 1)
                    if n:
                        pe.wait_ge(sem("delta_loaded"), 16)
                        for g, (t, d) in enumerate(step):
                            for h in range(4):
                                last = mm(bank[6 + g][:, h * P:(h + 1) * P], d_kt[:, t, h, :], d_sl[:, d, h, :])
                        last.then_inc(sem("ks_ready"), 1)
                    for g in range(2):
                        pe.wait_ge(sem("naT_saved", g), n + 1)
                    invert(d_inverse, len(RWKV_UNITS) + n)
                    for g in range(2):
                        pe.wait_ge(sem("rs_ready", g), n + 1)
                        pe.wait_ge(d_inverse.sem("t_ready", g), LEVELS * (len(RWKV_UNITS) + n + 1))
                        for h in range(4):
                            last = mm(bank[g][:, h * P:(h + 1) * P], d_tt[g][:, h, :], d_rs[g][:, h, :])
                        last.then_inc(sem("vn_ready", g), 1)
                    for g, (t, d) in enumerate(step):
                        pe.wait_ge(sem("vn_saved", g), n + 1)
                        for h in range(4):
                            last = mm(bank[2 + g][:, h * P:(h + 1) * P], d_at[g][:, h, :], d_vn[g][:, h, :])
                            if n:
                                last = mm(bank[6 + g][:, h * P:(h + 1) * P], d_qt[:, t, h, :], d_sl[:, d, h, :])
                            if n in DELTA_KEEPS:
                                last = mm(bank[4 + g][:, h * P:(h + 1) * P], d_kg[g][:, h, :], d_vn[g][:, h, :])
                        last.then_inc(sem("od_ready", g), 1)
                end_phase()

            def output_projection(l):
                pe.wait_ge(sem("mixed_ready"), l + 1)
                for k in range(6):
                    t, half = divmod(k, 2)
                    for i in range(4):
                        last = nc.tensor.transpose(bank[k][:, i * P:(i + 1) * P], mixed[:, t, 4 * half + i::J], C["ident"])
                    last.then_inc(sem("mixedT_ready"), 1)
                pe.wait_ge(sem("mixedT_saved", 0), 3 * (l + 1))
                pe.wait_ge(sem("mixedT_saved", 1), 3 * (l + 1))
                n = first[l]["out"]
                for q in range(4):
                    loaded(n + q)
                for j in range(J):
                    for c in range(J):
                        last = mm(bank[j][:, 0:NTOK], rows(n + c // 2, 2, D)[:, c % 2, j::J], hT[:, c, :], c == 0,
                                  c == J - 1)
                    last.then_inc(sem("out_ready"), 1)
                pe.drain().then_inc(sem("ring_released"), 1)
                end_phase()

            def router(l):
                pe.wait_ge(sem("h_ready"), 2 * l + 2)
                pe.wait_ge(sem("router_loaded"), 32 * (l + 1))
                for t in range(TILES):
                    for c in range(J):
                        last = mm(bank[2][:, 64 * t:64 * t + 64], hT[:, c, t * P:(t + 1) * P], m_router[:, c, :], c == 0,
                                  c == J - 1)
                last.then_inc(sem("logits_ready"), 1)
                pe.wait_ge(sem("routing_ready"), l + 1)
                for t in range(TILES):
                    last = nc.tensor.transpose(bank[3][0:EXPERTS, t * P:(t + 1) * P], m_w[:, t, :], C["ident"])
                last.then_inc(sem("routingT_ready"), 1)
                end_phase()

            def gate_up(gate, up, half):
                for w_, b in ((gate, 6), (up, 7)):
                    for c in range(J):
                        last = mm(bank[b][:, 0:NTOK], w_[:, c, half::2], hT[:, c, :], c == 0, c == J - 1)
                return last

            def down(wd, half, hid, opens):
                for t in range(TILES):
                    for b in range(2):
                        last = mm(bank[2 * t + b][:, :], hid[:, t * P:(t + 1) * P], wd[:, half, b * 512:(b + 1) * 512],
                                  opens, True, skip_group_check=True)
                return last

            def experts(l):
                q0 = 2 * (EXPERTS + 1) * l
                n = first[l]["shared"]
                gate, up, dn = (rows(n, J, FF), rows(n + 1, J, FF), rows(n + 2, 2, D))
                loaded(n)
                loaded(n + 1)
                gate_up(gate, up, 0).then_inc(sem("gu_ready"), 1)
                pe.wait_ge(sem("gu_saved"), q0 + 1)
                gate_up(gate, up, 1).then_inc(sem("gu_ready"), 1)
                pe.drain().then_inc(sem("ring_released"), 1)
                loaded(n + 2)
                pe.wait_ge(sem("hid_ready"), q0 + 1)
                down(dn, 0, x_h[0], True).then_inc(sem("down_done"), 1)
                pe.wait_ge(sem("hid_ready"), q0 + 2)
                down(dn, 1, x_h[1], False).then_inc(sem("down_done"), 1)
                pe.drain().then_inc(sem("ring_released"), 1)
                n0 = loops[l]
                with pe.Fori(0, EXPERTS // 2) as i:
                    for e in range(2):
                        m = n0 + 3 * e
                        q = q0 + 2 + 2 * e
                        gate, up, dn = (rows(m, J, FF), rows(m + 1, J, FF), rows(m + 2, 2, D))
                        for k in range(2):
                            pe.wait_ge(sem("ring_loaded", (m + k) % RING), i * 16 + piece_value(m + k))
                        pe.wait_ge(sem("gu_saved"), i * 4 + q)
                        gate_up(gate, up, 0).then_inc(sem("gu_ready"), 1)
                        pe.wait_ge(sem("gu_saved"), i * 4 + (q + 1))
                        gate_up(gate, up, 1).then_inc(sem("gu_ready"), 1)
                        pe.drain().then_inc(sem("ring_released"), 1)
                        pe.wait_ge(sem("ring_loaded", (m + 2) % RING), i * 16 + piece_value(m + 2))
                        pe.wait_ge(sem("hid_ready"), i * 4 + (q + 1))
                        down(dn, 0, x_h[0], False).then_inc(sem("down_done"), 1)
                        pe.wait_ge(sem("hid_ready"), i * 4 + (q + 2))
                        down(dn, 1, x_h[1], False).then_inc(sem("down_done"), 1)
                        pe.drain().then_inc(sem("ring_released"), 1)
                pe.drain().then_inc(sem("y_sums_ready"), 1)
                pe.wait_ge(sem("y_sums_saved"), 6 * (l + 1))
                for k in range(6):
                    t, half = divmod(k, 2)
                    for i in range(4):
                        last = nc.tensor.transpose(bank[k][:, i * P:(i + 1) * P], x_y[:, t, 4 * half + i::J], C["ident"])
                    last.then_inc(sem("yT_ready"), 1)
                end_phase()

            for l in range(LAYERS):
                modulation(l)
                norm(2 * l + 1)
                projection(l)
                (token_shift if l % 2 == 0 else convolution)()
                end_phase()
                attend(l)
                (rwkv if l % 2 == 0 else delta)()
                output_projection(l)
                norm(2 * l + 2)
                router(l)
                experts(l)

        @block.scalar
        def _(act):
            phase = [0]
            chain = [0]

            def link(ins):
                chain[0] += 1
                ins.then_inc(sem("act_chain"), 1)
                act.wait_ge(sem("act_chain"), chain[0])

            def f(out, in_, func, **kw):
                return nc.scalar.activation(out, in_, func, **kw)

            def rsqrt(ap, scale, eps):
                link(f(ap, ap, ACT.Ln, scale=scale, bias=eps))
                return f(ap, ap, ACT.Exp, scale=-0.5)

            def end_phase():
                phase[0] += 1
                phase_end("act", act, phase[0])

            def load(out, in_, s):
                act.dma_start(out, in_).then_inc(s, 16)

            def rows_of(ap, n=P):
                return ap.unsqueeze(0).broadcast_to([n] + list(ap.shape))

            def load_params(l):
                s = sem("params_loaded")
                if l % 2 == 0:
                    load(heads(params[:, 0:512], 8), w["a_qn"][0].unsqueeze(0).unsqueeze(0).broadcast_to([P, 8, 64]), s)
                    load(heads(params[:, 512:640], 2), w["a_kn"][0].unsqueeze(0).unsqueeze(0).broadcast_to([P, 2, 64]), s)
                    load(r_mu, rows_of(w["b_mu"][0]), s)
                    for dst, name in ((r_kk, "b_kk"), (r_ka, "b_ka"), (r_lnw, "b_lnx_w"), (r_lnb, "b_lnx_b")):
                        load(dst, rows_of(w[name][0]), s)
                    load(r_rk, rows_of(w["b_rk"][0].rearrange("h d -> (h d)")), s)
                else:
                    load(conv_w, rows_of(w["c_conv"][0]), s)
                    load(heads(params[:, 4608:5120], 8), w["d_qn"][0].unsqueeze(0).unsqueeze(0).broadcast_to([P, 8, 64]), s)
                    load(heads(params[:, 5120:5632], 8), w["d_kn"][0].unsqueeze(0).unsqueeze(0).broadcast_to([P, 8, 64]), s)
                    load(params[:, 5632:5760], rows_of(w["c_onorm"][0]), s)
                    load(params[:, 5760:5888], rows_of(w["d_subln"][0]), s)
                    load(params[:, 5888:6144], rows_of(w["d_lambda"][0].rearrange("k d -> (k d)")), s)
                    load(params[:, 6144:6152], rows_of(w["c_A_log"][0].rearrange("d h -> (d h)")), s)
                    load(params[:, 6152:6160], rows_of(w["c_dt_bias"][0].rearrange("d h -> (d h)")), s)

            def norm(n):
                if n == 1:
                    act.wait_ge(sem("x_loaded"), 16)
                else:
                    act.wait_ge(sem("x_ready"), n - 1)
                f(squares, xT[:, :, :], ACT.Square).then_inc(sem("squares_ready"), 1)
                act.wait_ge(sem("sumsq_ready"), n)
                link(f(rstd[:, :], bank[1][:, 0:NTOK], ACT.Ln, scale=1.0 / D, bias=eps6))
                f(rstd[:, :], rstd[:, :], ACT.Exp, scale=-0.5).then_inc(sem("rstd_ready"), 1)

            def projection(l):
                proj, _ = proj_of(l)
                k = 0
                for a, b in (EVEN_BLOCKS if l % 2 == 0 else ODD_BLOCKS):
                    for t in range(TILES):
                        if k % 2 == 1:
                            act.wait_ge(sem("proj_ready"), 18 * l + k + 1)
                            nc.scalar.copy(*projected(l, t, a, b, bank[k % 6])).then_inc(sem("proj_saved", 1), 1)
                        k += 1
                end_phase()

            def load_cached(l):
                A = attention[l]
                s = sem("keys_loaded")
                load(A.klat[:, :, 0, :], w["keys_a"].unsqueeze(1) if A.even else w["keys_d"], s)
                load(A.vc, w["values_a"] if A.even else w["values_d"], s)
                if not A.even:
                    load(d_sl, w["state_d"], sem("delta_loaded"))
                else:
                    s = sem("rwkv_loaded")
                    load(r_lora[0:64, :].rearrange("p (d n) -> p d n", d=2), w["b_w2"][0].rearrange("d k n -> k d n"), s)
                    load(r_lora[64:128, :].rearrange("p (d n) -> p d n", d=2), w["b_a2"][0].rearrange("d k n -> k d n"), s)
                    load(r_w0.rearrange("p (d n) -> p d n", d=2), rows_of(w["b_w0"][0]), s)
                    load(r_a0.rearrange("p (d n) -> p d n", d=2), rows_of(w["b_a0"][0]), s)
                    load(r_sl, w["state_r"], s)
                    load(r_g2, w["b_g2"][0], s)

            def conv_silu():
                for t in range(TILES):
                    act.wait_ge(sem("conv_done"), t + 1)
                    f(conv_exp(t), proj1[:, t, 0:1536], ACT.Exp, scale=-1.0).then_inc(sem("conv_exp_ready"), 1)

            def attend(l):
                A = attention[l]
                for t in range(TILES):
                    act.wait_ge(sem("qk_sumsq"), TILES * l + t + 1)
                    rsqrt(A.ss[:, 16 * t:16 * t + A.nh], 1.0 / HEAD, eps6).then_inc(sem("qk_rstd"), 1)
                if not A.even:
                    act.wait_ge(sem("lam_sums"), 1)
                    f(A.neg[:, 0:2], A.neg[:, 0:2], ACT.Exp).then_inc(sem("lam_exps"), 1)
                act.wait_ge(sem("qk_ready"), TILES * l + 1)
                k0 = A.base + 512
                nk = 64 * (A.nh - 8)
                load(outs["k_a"] if A.even else outs["k_d"], A.proj[:, 0, k0:k0 + nk], sem("stored"))
                load(outs["v_a"] if A.even else outs["v_d"],
                     A.proj[:, 0, A.vbase:A.vbase + (128 if A.even else 512)], sem("stored"))
                for t in range(TILES):
                    act.wait_ge(sem("qkT_ready"), TILES * l + t + 1)
                    nc.scalar.copy(A.qt[:, t, :, :], bank[2 * t][:, :].rearrange("p (c n) -> p c n", c=4))\
                        .then_inc(sem("qT_saved"), 1)
                for u in range(25):
                    if u < 24:
                        kt = A.unit(u)[1]
                        act.wait_ge(sem("max_ready"), 24 * l + u + 1)
                        if u >= 2:
                            act.wait_ge(sem("pT_ready"), 24 * l + u - 1)
                        f(A.p[:, u % 2, 0:kt * P], bank[u % 2][:, 0:kt * P], ACT.Exp, bias=A.mx[:, u:u + 1],
                          accum_out=A.sums[:, u:u + 1]).then_inc(sem("p_ready"), 1)
                    if u >= 1:
                        v = u - 1
                        kt = A.unit(v)[1]
                        act.wait_ge(sem("pT_ready"), 24 * l + v + 1)
                        if v >= 2:
                            act.wait_ge(sem("o_ready"), 24 * l + v - 1)
                        nc.scalar.copy(A.pt[:, v % 2, 0:kt * P], bank[2 + v % 2][:, 0:kt * P])\
                            .then_inc(sem("pT_saved"), 1)
                if not A.even:
                    act.wait_ge(sem("head_sumsq"), 3)
                    rsqrt(stats[:, 0:12], 1.0 / P, eps6).then_inc(sem("head_rstd"), 1)
                end_phase()

            def invert(inv, n, groups=(0, 1)):
                for k in range(1, LEVELS):
                    for g in groups:
                        act.wait_ge(inv.sem("m_ready", g), 6 * n + k)
                        nc.scalar.copy(inv.m1[g], bank[g][:, :].rearrange("p (h n) -> p h n", h=4))\
                            .then_inc(inv.sem("m_saved", g), 1)

            def rwkv():
                act.wait_ge(sem("stored"), 32)
                f(proj0[:, :, XW:XW + 64], proj0[:, :, XW:XW + 64], ACT.Exp, scale=2.0)
                f(proj0[:, :, XG:XG + P], proj0[:, :, XG:XG + P], ACT.Exp, scale=-1.0).then_inc(sem("lora_exp"), 1)
                for t in range(TILES):
                    act.wait_ge(sem("lora_turned"), t + 1)
                    nc.scalar.copy(proj0[:, t, 512:768], bank[0][:, 0:2 * P]).then_inc(sem("lora_saved"), 1)
                act.wait_ge(sem("head_sumsq"), 1)
                rsqrt(stats[:, 0:24], 1.0, eps6).then_inc(sem("head_rstd"), 1)
                for u, (t, d) in enumerate(RWKV_UNITS):
                    act.wait_ge(sem("zw_sum"), u + 1)
                    f(r_sig, r_sig, ACT.Exp, scale=-1.0)
                    f(r_gate, r_gate, ACT.Exp, scale=-1.0).then_inc(sem("z_exp"), 1)
                    act.wait_ge(sem("cum_ready"), u + 1)
                    f(r_ei, bank[2][:, :], ACT.Exp, scale=-DECAY)
                    f(r_ev, bank[2][:, :], ACT.Exp, scale=DECAY)
                    f(r_ee, bank[3][:, :], ACT.Exp, scale=-DECAY)
                    f(r_ec, bank[4][:, 0:8].rearrange("p (j h) -> p j h", j=4), ACT.Exp, scale=-DECAY)\
                        .then_inc(sem("exps_ready"), 1)
                    act.wait_ge(sem("tokT_ready"), u + 1)
                    nc.scalar.copy(r_ar[:, :, 0, :], bank[0][:, :].rearrange("p (c n) -> p c n", c=4))
                    nc.scalar.copy(r_ar[:, :, 1, :], bank[1][:, :].rearrange("p (c n) -> p c n", c=4))\
                        .then_inc(sem("arT_saved"), 1)
                    act.wait_ge(sem("read_ready"), u + 1)
                    for g in range(2):
                        last = nc.scalar.copy(r_rs[:, g::2, :], heads(bank[6 + g][:, 0:256], 4))
                    last.then_inc(sem("read_saved"), 1)
                    invert(r_inverse, u)
                    act.wait_ge(sem("u_ready"), u + 1)
                    for g in range(2):
                        last = nc.scalar.copy(r_us[:, g::2, :], heads(bank[g][:, 0:256], 4))
                    last.then_inc(sem("u_saved"), 1)
                    if u == 2:
                        load(outs["state_r"], r_sc, sem("stored"))
                act.wait_ge(sem("head_sumsq"), 2)
                rsqrt(stats[:, 24:48], 1.0 / HEAD, eps_ln).then_inc(sem("head_rstd"), 1)
                act.wait_ge(sem("stored"), 48)
                end_phase()

            def delta():
                act.wait_ge(sem("head_sumsq"), 4)
                rsqrt(stats[:, 0:24], 1.0, eps6).then_inc(sem("head_rstd"), 1)
                act.wait_ge(sem("softplus_in"), 1)
                link(f(d_tmp, d_tmp, ACT.Exp))
                f(d_tmp, d_tmp, ACT.Ln, bias=one_col)
                f(params[:, 6144:6152], params[:, 6144:6152], ACT.Exp)
                f(d_beta, proj1[:, :, CAB + 8:CAB + 16].rearrange("p t (d h) -> p t d h", d=2), ACT.Exp, scale=-1.0)\
                    .then_inc(sem("softplus_ln"), 1)
                for t in range(TILES):
                    act.wait_ge(sem("ckT_ready"), t + 1)
                    nc.scalar.copy(d_kt[:, t, :, :], heads(bank[2 * t][:, :], 4)).then_inc(sem("ckT_saved"), 1)
                act.wait_ge(sem("gsum_ready"), 1)
                for i, dst in enumerate((d_eg, d_es, d_et)):
                    last = f(dst, bank[6][:, 24 * i:24 * i + 24].rearrange("p (t d h) -> p t d h", t=TILES, d=2), ACT.Exp)
                last.then_inc(sem("decay_exps"), 1)
                for n, step in enumerate(DELTA_STEPS):
                    for g in range(2):
                        act.wait_ge(sem("dneg_ready", g), n + 1)
                        f(d_off[g], d_off[g], ACT.Exp, scale=-1.0).then_inc(sem("dexp_ready", g), 1)
                    invert(d_inverse, len(RWKV_UNITS) + n)
                    for g in range(2):
                        act.wait_ge(sem("vn_ready", g), n + 1)
                        nc.scalar.copy(d_vn[g], heads(bank[g][:, :], 4)).then_inc(sem("vn_saved", g), 1)
                    if n == 1:
                        load(outs["state_d"], d_sc, sem("stored"))
                act.wait_ge(sem("head_sumsq"), 5)
                rsqrt(stats[:, 12:24], 1.0 / P, eps6)
                f(silu_z, proj1[:, :, CZ:CZ + 512], ACT.Exp, scale=-1.0).then_inc(sem("head_rstd"), 1)
                act.wait_ge(sem("stored"), 96)
                end_phase()

            def output_projection(l):
                act.wait_ge(sem("mixed_ready"), l + 1)
                for k in (0, 2, 4):
                    t, half = divmod(k, 2)
                    act.wait_ge(sem("mixedT_ready"), 6 * l + k + 1)
                    nc.scalar.copy(hT[:, 4 * half:4 * half + 4, t * P:(t + 1) * P], heads(bank[k][:, :], 4))\
                        .then_inc(sem("mixedT_saved", 0), 1)
                end_phase()

            def router(l):
                act.wait_ge(sem("logits_ready"), l + 1)
                f(m_sc, heads(bank[2][:, 0:192], 3), ACT.Exp, scale=-1.0).then_inc(sem("logit_exps"), 1)
                act.wait_ge(sem("routingT_saved"), l + 1)
                load(wt_dram[l], m_wt[0:EXPERTS, :], sem("routing_stored"))
                end_phase()

            def experts(l):
                q0 = 2 * (EXPERTS + 1) * l

                def gate_exp(half, q, i=None):
                    v = lambda n: n if i is None else i * 4 + n
                    act.wait_ge(sem("gu_ready"), v(q + 1))
                    if i is not None:
                        act.wait_ge(sem("gated"), v(q - 1))
                    f(x_e[half], bank[6][:, 0:NTOK], ACT.Exp, scale=-1.0).then_inc(sem("gate_exp"), 1)

                gate_exp(0, q0)
                gate_exp(1, q0 + 1)
                with act.Fori(0, EXPERTS // 2) as i:
                    for e in range(2):
                        for half in range(2):
                            gate_exp(half, q0 + 2 + 2 * e + half, i)
                act.wait_ge(sem("y_sums_ready"), l + 1)
                for k in (0, 2, 4):
                    nc.scalar.copy(x_y[:, k // 2, 0:512], bank[k][:, :]).then_inc(sem("y_sums_saved"), 1)
                end_phase()

            nc.scalar.preload_act_table_set("natural_log_exp_and_others")
            for dst, name in ((consts[:, :], "consts"), (cond[:, :, :], "cond"), (mod_b[:, :, :, :], "mod_b"),
                              (gains[:, :, :, :], "gains"), (rope[:, :, :, :], "rope")):
                load(dst, w[name], sem("start_loaded"))
            load_params(0)
            act.wait_ge(sem("start_loaded"), 80)
            f(cond_exp[:, :, :], cond[:, :, :], ACT.Exp, scale=-1.0).then_inc(sem("cond_exps"), 1)
            for l in range(LAYERS):
                end_phase()
                norm(2 * l + 1)
                projection(l)
                if l % 2:
                    conv_silu()
                end_phase()
                load_cached(l)
                attend(l)
                (rwkv if l % 2 == 0 else delta)()
                if l + 1 < LAYERS:
                    load_params(l + 1)
                load(m_router, w["router_w"][l].rearrange("(p c) e -> p c e", c=J), sem("router_loaded"))
                load(m_bias_buf, rows_of(w["router_bias"][l]), sem("router_loaded"))
                output_projection(l)
                norm(2 * l + 2)
                router(l)
                experts(l)

        @block.vector
        def _(dve):
            phase = [0]
            chain = [0]

            def link(ins):
                chain[0] += 1
                ins.then_inc(sem("dve_chain"), 1)
                dve.wait_ge(sem("dve_chain"), chain[0])

            def tt(out, a, b, op):
                return nc.vector.tensor_tensor(out, a, b, op)

            def ts(out, a, s1, op0, s2=None, op1=None):
                if op1 is None:
                    return nc.vector.tensor_scalar(out, a, s1, None, op0)
                return nc.vector.tensor_scalar(out, a, s1, s2, op0, op1)

            def stt(out, a, s, b, op0, op1):
                return nc.vector.scalar_tensor_tensor(out=out, in0=a, scalar=s, in1=b, op0=op0, op1=op1)

            def total(out, a, op=ALU.add, **kw):
                return nc.vector.tensor_reduce(out, a, AX.X, op, **kw)

            def copy(out, a):
                return nc.vector.tensor_copy(out, a)

            def recip(ap):
                return nc.vector.reciprocal(ap, ap)

            def sigmoid_of(ap):
                link(ts(ap, ap, 1.0, ALU.add))
                return recip(ap)

            def end_phase():
                phase[0] += 1
                phase_end("dve", dve, phase[0])

            def modulation(l):
                if l == 0:
                    dve.wait_ge(sem("cond_exps"), 1)
                    link(sigmoid_of(cond_exp[:, :, :]))
                    tt(cond[:, :, :], cond[:, :, :], cond_exp[:, :, :], ALU.mult).then_inc(sem("cond_ready"), 1)
                end_phase()
                link(tt(mods[:, :, :, :].rearrange("p s j c -> p (s j) c"),
                        bank[0][:, 0:96].rearrange("p (k c) -> p k c", c=2),
                        along(mod_b[:, l, :, :].rearrange("p s j -> p (s j)"), 2), ALU.add))
                for which, s in ((0, 1), (1, 4)):
                    link(stt(mods[:, s, :, :], mods[:, s, :, :], 1.0, along(gains[:, l, which, :], 2), ALU.add, ALU.mult))

            def norm(n):
                l, which = divmod(n - 1, 2)
                if n == 1:
                    dve.wait_ge(sem("x_loaded"), 16)
                dve.wait_ge(sem("rstd_ready"), n)
                link(tt(squares, xT[:, :, :], rstd[:, :].unsqueeze(1).broadcast_to([P, J, NTOK]), ALU.mult))
                for j in range(J):
                    for c, a, b in ((0, 0, P), (1, P, NTOK)):
                        last = ts(hT[:, j, a:b], squares[:, j, a:b], mods[:, 3 * which + 1, j, c:c + 1], ALU.mult,
                                  mods[:, 3 * which, j, c:c + 1], ALU.add)
                last.then_inc(sem("h_ready"), 1)

            def projection(l):
                proj, _ = proj_of(l)
                k = 0
                for a, b in (EVEN_BLOCKS if l % 2 == 0 else ODD_BLOCKS):
                    for t in range(TILES):
                        if k % 2 == 0:
                            dve.wait_ge(sem("proj_ready"), 18 * l + k + 1)
                            copy(*projected(l, t, a, b, bank[k % 6])).then_inc(sem("proj_saved", 0), 1)
                        k += 1
                end_phase()
                dve.wait_ge(sem("params_loaded"), 128 * l + 16 * 8)

            def token_shift():
                tmp = attention[0].t1[:, 0:448]
                for b in range(4):
                    dve.wait_ge(sem("near_ready"), b + 1)
                    for t in range(TILES):
                        x = proj0[:, t, XB + 448 * b:XB + 448 * (b + 1)]
                        link(stt(tmp, bank[3 * (b % 2) + t][:, 0:448], 0.5, x, ALU.mult, ALU.subtract))
                        link(tt(tmp, tmp, r_mu[:, 448 * b:448 * (b + 1)], ALU.mult))
                        link(tt(x, x, tmp, ALU.add))
                    dve.drain().then_inc(sem("near_saved"), 1)

            def convolution():
                tmp, tmp2 = conv_tmp[:, 0:512], conv_tmp[:, 512:1024]
                for b in range(3):
                    cols = slice(512 * b, 512 * (b + 1))
                    dve.wait_ge(sem("near_ready"), 4 + b + 1)
                    for t in range(TILES):
                        x = proj1[:, t, cols]
                        tt(tmp, bank[t][:, :], conv_w[:, 0, cols], ALU.mult)
                        tt(tmp2, bank[3 + t][:, :], conv_w[:, 2, cols], ALU.mult)
                        link(tt(x, x, conv_w[:, 1, cols], ALU.mult))
                        link(tt(x, x, tmp, ALU.add))
                        link(tt(x, x, tmp2, ALU.add))
                    dve.drain().then_inc(sem("near_saved"), 1)
                for t in range(TILES):
                    dve.drain().then_inc(sem("conv_done"), 1)
                for t in range(TILES):
                    x = proj1[:, t, 0:1536]
                    dve.wait_ge(sem("conv_exp_ready"), t + 1)
                    link(sigmoid_of(conv_exp(t)))
                    link(tt(x, x, conv_exp(t), ALU.mult))

            def attend(l):
                A = attention[l]
                n = 64 * A.nh
                link(ts(A.gain[:, 0:512], A.gain[:, 0:512], HEAD ** -0.5, ALU.mult))
                for t in range(TILES):
                    link(tt(A.t1[:, 0:n], A.qk(t), A.qk(t), ALU.mult))
                    total(A.ss[:, 16 * t:16 * t + A.nh], heads(A.t1[:, 0:n], A.nh)).then_inc(sem("qk_sumsq"), 1)
                    dve.wait_ge(sem("qk_sumsq"), TILES * l + t + 1)
                if not A.even:
                    lam = params[:, 5888:6144].rearrange("p (k d) -> p k d", k=4)
                    link(tt(heads(A.t1[:, 0:128], 2), lam[:, 0::2, :], lam[:, 1::2, :], ALU.mult))
                    total(A.neg[:, 0:2], heads(A.t1[:, 0:128], 2)).then_inc(sem("lam_sums"), 1)
                    dve.wait_ge(sem("lam_exps"), 1)
                    link(stt(A.neg[:, 2:3], A.neg[:, 1:2], LAM_INIT, A.neg[:, 0:1], ALU.subtract, ALU.subtract))
                for t in range(TILES):
                    qk = heads(A.qk(t), A.nh)
                    dve.wait_ge(sem("qk_rstd"), TILES * l + t + 1)
                    link(tt(qk, qk, along(A.ss[:, 16 * t:16 * t + A.nh], 64), ALU.mult))
                    scaled = tt(A.qk(t), A.qk(t), A.gain, ALU.mult)
                    if t == 0:
                        scaled.then_inc(sem("qk_ready"), 1)
                        continue
                    link(scaled)
                    cos, sin = (rope[:, t - 1, i, :] for i in range(2))
                    wide = lambda ap: ap.unsqueeze(1).broadcast_to([P, A.nh, ap.shape[-1]])
                    t1, t2 = heads(A.t1[:, 0:n], A.nh), heads(A.t2[:, 0:n], A.nh)
                    tt(t2[:, :, 0::2], qk[:, :, 1::2], wide(sin[:, 0::2]), ALU.mult)
                    tt(t2[:, :, 1::2], qk[:, :, 0::2], wide(sin[:, 1::2]), ALU.mult)
                    link(tt(t1, qk, wide(cos), ALU.mult))
                    tt(qk, t1, t2, ALU.add).then_inc(sem("qk_ready"), 1)
                    dve.wait_ge(sem("qk_ready"), TILES * l + t + 1)
                for t in range(TILES):
                    dve.wait_ge(sem("qkT_ready"), TILES * l + t + 1)
                    dst = A.kctx if t == 0 else A.klat[:, :, t, :]
                    copy(dst, heads(bank[2 * t + 1][:, 0:A.kc * P], A.kc)).then_inc(sem("kT_saved"), 1)

                def normalise(g):
                    n = A.per_bank
                    units = slice(n * g, n * (g + 1))
                    dve.wait_ge(sem("o_ready"), 24 * l + n * (g + 1))
                    link(nc.vector.reciprocal(A.rinv[:, units], A.sums[:, units]))
                    src = heads(bank[4 + g % 2][:, :], n)
                    if A.even:
                        tt(heads(mixed[:, g, 0:512], 8), src, along(A.rinv[:, units], 64), ALU.mult)\
                            .then_inc(sem("o_saved"), 1)
                        return
                    t, half = divmod(g, 2)
                    r2 = A.rinv[:, n * g + 1:n * (g + 1):2]
                    link(ts(r2, r2, A.neg[:, 2:3], ALU.mult))
                    t1, t2 = heads(A.t1[:, 0:256], 2), heads(A.t2[:, 0:256], 2)
                    tt(t1, src[:, 0::2, :], along(A.rinv[:, n * g:n * (g + 1):2], P), ALU.mult)
                    link(tt(t2, src[:, 1::2, :], along(r2, P), ALU.mult))
                    out = heads(mixed[:, t, 512 + 256 * half:768 + 256 * half], 2)
                    tt(out, t1, t2, ALU.add).then_inc(sem("o_saved"), 1)
                    dve.wait_ge(sem("o_saved"), 3 * l + g + 1)

                n_groups = 24 // A.per_bank
                done = 0
                for u in range(24):
                    kt = A.unit(u)[1]
                    dve.wait_ge(sem("s_ready"), 24 * l + u + 1)
                    total(A.mx[:, u:u + 1], bank[u % 2][:, 0:kt * P], ALU.max, negate=True)\
                        .then_inc(sem("max_ready"), 1)
                    if done < n_groups and u >= A.per_bank * (done + 1) + 2:
                        normalise(done)
                        done += 1
                while done < n_groups:
                    normalise(done)
                    done += 1
                if not A.even:
                    od = mixed[:, :, 512:1024].rearrange("p t (h d) -> p t h d", h=4)
                    tmp = arena[:, po1:po1 + 1536].rearrange("p (t h d) -> p t h d", t=TILES, h=4)
                    st = stats[:, 0:12].rearrange("p (t h) -> p t h", t=TILES)
                    link(tt(tmp, od, od, ALU.mult))
                    total(st, tmp).then_inc(sem("head_sumsq"), 1)
                    dve.wait_ge(sem("head_rstd"), 3)
                    link(ts(st, st, 1.0 - LAM_INIT, ALU.mult))
                    link(tt(od, od, along(st, P), ALU.mult))
                    sub = params[:, 5760:5888].unsqueeze(1).unsqueeze(1).broadcast_to([P, TILES, 4, P])
                    link(tt(od, od, sub, ALU.mult))
                end_phase()

            def join(inv, n, groups=(0, 1)):
                ident = C["ident"].unsqueeze(1).broadcast_to([P, 4, P])
                for g in groups:
                    dve.wait_ge(inv.sem("off_ready", g), 7 * n + 1)
                    tt(inv.tt[g], inv.off[g], ident, ALU.add)
                for g in groups:
                    dve.wait_ge(inv.sem("turned", g), n + 1)
                    tt(inv.t[g], heads(bank[2 + g][:, :], 4), ident, ALU.add).then_inc(inv.sem("t_ready", g), 1)
                for k in range(1, LEVELS):
                    for g in groups:
                        dve.wait_ge(inv.sem("join_ready", g), 6 * n + k)
                        dve.wait_ge(inv.sem("t_ready", g), 7 * n + k)
                        if k < LEVELS - 1:
                            tt(inv.t[g], inv.t[g], heads(bank[2 + g][:, :], 4), ALU.add)
                        tt(inv.tt[g], inv.tt[g], heads(bank[4 + g][:, :], 4), ALU.add)\
                            .then_inc(inv.sem("t_ready", g), 1)

            def rwkv():
                dve.wait_ge(sem("lora_exp"), 1)
                th, sg = proj0[:, :, XW:XW + 64], proj0[:, :, XG:XG + P]
                ts(sg, sg, 1.0, ALU.add)
                link(ts(th, th, 1.0, ALU.add))
                recip(sg)
                link(recip(th))
                ts(th, th, -2.0, ALU.mult, 1.0, ALU.add).then_inc(sem("lora_ready"), 1)
                wide = lambda ap: ap.unsqueeze(1).broadcast_to([P, TILES, 512])
                kk = proj0[:, :, 0:512]
                tmp = arena[:, po0:po0 + 1536].rearrange("p (t n) -> p t n", t=TILES)
                h4 = lambda ap: ap.rearrange("p t (h d) -> p t h d", h=8)
                st = stats[:, 0:24].rearrange("p (t h) -> p t h", t=TILES)
                link(tt(kk, proj0[:, :, XK:XK + 512], wide(r_kk), ALU.mult))
                link(tt(tmp, kk, kk, ALU.mult))
                total(st, h4(tmp)).then_inc(sem("head_sumsq"), 1)
                dve.wait_ge(sem("head_rstd"), 1)
                link(tt(h4(kk), h4(kk), along(st, 64), ALU.mult))
                dve.wait_ge(sem("rwkv_loaded"), 16 * 6)
                for u, (t, d) in enumerate(RWKV_UNITS):
                    dve.wait_ge(sem("za_ready"), u + 1)
                    tt(r_sig, bank[0][:, :], r_w0[:, 512 * d:512 * (d + 1)], ALU.add)
                    tt(r_gate, bank[1][:, :], r_a0[:, 512 * d:512 * (d + 1)], ALU.add).then_inc(sem("zw_sum"), 1)
                    dve.wait_ge(sem("z_exp"), u + 1)
                    ts(r_gate, r_gate, 1.0, ALU.add)
                    link(ts(r_sig, r_sig, 1.0, ALU.add))
                    recip(r_sig).then_inc(sem("sig_ready"), 1)
                    link(recip(r_gate))
                    tt_k = proj0[:, t, XK:XK + 512]
                    stt(r_tokb, kk_of(t), -1.0, r_gate, ALU.mult, ALU.mult)
                    link(stt(r_tokk, r_gate, 1.0, r_ka, ALU.subtract, ALU.mult))
                    link(stt(r_tokk, r_tokk, 1.0, tt_k, ALU.add, ALU.mult))
                    dve.wait_ge(sem("exps_ready"), u + 1)
                    if t:
                        tt(r_sw, r_sl[:, d, :, :], along(r_ec[:, :, d], 64), ALU.mult)
                    tt(r_toka, kk_of(t), r_ee, ALU.mult)
                    tt(r_tokr, proj0[:, t, XR:XR + 512], r_ei, ALU.mult)
                    tt(r_tokb, r_tokb, r_ev, ALU.mult)
                    tt(r_tokk, r_tokk, r_ev, ALU.mult).then_inc(sem("tok_ready"), 1)
                    dve.wait_ge(sem("tokT_ready"), u + 1)
                    copy(r_bt, heads(bank[2][:, :], 4))
                    copy(r_kt, heads(bank[3][:, :], 4)).then_inc(sem("bkT_saved"), 1)
                    mask = masks[d].unsqueeze(1).broadcast_to([P, 2, 256])
                    for g in range(2):
                        dve.wait_ge(sem("gram_ready"), 2 * u + g + 1)
                        two = lambda ap, i: ap[:, 2 * i:2 * i + 2, :, :].rearrange("p c k n -> p c (k n)")
                        for i in range(2):
                            last = tt(two(r_nr[g], i), heads(bank[4 + i][:, :], 2), mask, ALU.mult)
                        last.then_inc(r_inverse.sem("nt_ready", g), 1)
                        for i in range(2):
                            last = tt(two(r_ak[g], i), heads(bank[6 + i][:, :], 2), mask, ALU.mult)
                        last.then_inc(sem("gram_saved"), 1)
                    join(r_inverse, u)
                    dve.wait_ge(sem("y_unit_ready"), u + 1)
                    first_visit = u in (0, 2, 3)
                    for g in range(2):
                        y = heads(yacc_of(t), 8)[:, g::2, :]
                        src = heads(bank[2 + g][:, 0:256], 4)
                        last = copy(y, src) if first_visit else tt(y, y, src, ALU.add)
                        if u in RWKV_KEEPS:
                            p = slice(64 * g, 64 * g + 64)
                            src = heads(bank[4 + g][p, 0:256], 4)
                            end = along(r_ec[p, :, 1 - d], 64)
                            if t:
                                link(tt(r_sw[p, :, :], r_sw[p, :, :], src, ALU.add))
                                last = tt(r_sl[p, d, :, :], r_sw[p, :, :], end, ALU.mult)
                            else:
                                last = tt(r_sc[p, d, :, :], src, end, ALU.mult)
                    last.then_inc(sem("unit_saved"), 1)
                    dve.wait_ge(sem("unit_saved"), u + 1)
                y = mixed[:, :, 512:1024]
                mean = stats[:, 0:24].rearrange("p (t h) -> p t h", t=TILES)
                var = stats[:, 24:48].rearrange("p (t h) -> p t h", t=TILES)
                link(total(mean, h4(y)))
                link(ts(mean, mean, 1.0 / HEAD, ALU.mult))
                link(tt(h4(y), h4(y), along(mean, 64), ALU.subtract))
                link(tt(tmp, y, y, ALU.mult))
                total(var, h4(tmp)).then_inc(sem("head_sumsq"), 1)
                dve.wait_ge(sem("head_sumsq"), 2)
                link(tt(tmp, proj0[:, :, XR:XR + 512], proj0[:, :, XK:XK + 512], ALU.mult))
                link(tt(tmp, tmp, wide(r_rk), ALU.mult))
                link(total(mean, h4(tmp)))
                link(tt(h4(tmp), h4(proj0[:, :, XV:XV + 512]), along(mean, 64), ALU.mult))
                dve.wait_ge(sem("head_rstd"), 2)
                link(tt(h4(y), h4(y), along(var, 64), ALU.mult))
                link(tt(y, y, wide(r_lnw), ALU.mult))
                link(tt(y, y, wide(r_lnb), ALU.add))
                link(tt(y, y, tmp, ALU.add))
                dve.wait_ge(sem("gate_ready"), 1)
                for t in range(TILES):
                    last = tt(mixed[:, t, 512:1024], mixed[:, t, 512:1024], bank[t][:, :], ALU.mult)
                last.then_inc(sem("mixed_ready"), 1)
                end_phase()

            def delta():
                h8 = lambda ap: ap.rearrange("p t (h d) -> p t h d", h=8)
                qk = proj1[:, :, 0:1024]
                tmp = arena[:, po1:po1 + 3072].rearrange("p (t n) -> p t n", t=TILES)
                st = stats[:, 0:24].rearrange("p (t h) -> p t h", t=TILES)
                link(tt(tmp, qk, qk, ALU.mult))
                total(st, h8(tmp)).then_inc(sem("head_sumsq"), 1)
                td = lambda ap: ap.rearrange("p (d h) -> p d h", d=2).unsqueeze(1).broadcast_to([P, TILES, 2, 4])
                flat = lambda ap: ap.rearrange("p t d h -> p (t d h)")
                a_in = proj1[:, :, CAB:CAB + 8].rearrange("p t (d h) -> p t d h", d=2)
                link(tt(d_g, a_in, td(params[:, 6152:6160]), ALU.add))
                stt(flat(d_tmp), flat(d_g), -1.0, flat(d_g), ALU.mult, ALU.min).then_inc(sem("softplus_in"), 1)
                dve.wait_ge(sem("softplus_in"), 1)
                link(ts(d_g, d_g, 0.0, ALU.max))
                dve.wait_ge(sem("head_rstd"), 4)
                link(ts(st[:, :, 0:4], st[:, :, 0:4], P ** -0.5, ALU.mult))
                tt(h8(qk), h8(qk), along(st, P), ALU.mult).then_inc(sem("ck_ready"), 1)
                dve.wait_ge(sem("softplus_ln"), 1)
                link(tt(d_g, d_g, d_tmp, ALU.add))
                link(tt(d_g, d_g, td(params[:, 6144:6152]), ALU.mult))
                ts(d_g, d_g, -1.0, ALU.mult).then_inc(sem("g_ready"), 1)
                link(sigmoid_of(d_beta))
                link(ts(d_neg, d_beta, -1.0, ALU.mult))
                for t in range(TILES):
                    dve.wait_ge(sem("ckT_ready"), t + 1)
                    copy(d_qt[:, t, :, :], heads(bank[2 * t + 1][:, :], 4)).then_inc(sem("cqT_saved"), 1)
                dve.wait_ge(sem("gsum_ready"), 1)
                dve.wait_ge(sem("decay_exps"), 1)
                copy(d_gc, bank[6][:, 0:24].rearrange("p (t d h) -> p t d h", t=TILES, d=2))
                dve.drain().then_inc(sem("decay_cols_ready"), 1)
                dve.wait_ge(sem("decay_cols_ready"), 1)
                dve.wait_ge(sem("g_ready"), 1)
                dve.wait_ge(sem("ck_ready"), 1)
                dve.wait_ge(sem("delta_loaded"), 16)
                for n, step in enumerate(DELTA_STEPS):
                    for g, (t, d) in enumerate(step):
                        for h in range(4):
                            last = ts(d_t[g][:, h, :], C[f"incl{d}"], d_g[:, t, d, h:h + 1], ALU.mult)
                        last.then_inc(sem("gi_ready", g), 1)
                    for g, (t, d) in enumerate(step):
                        dve.wait_ge(sem("dgram_ready", g), n + 1)
                        for h in range(4):
                            last = ts(d_off[g][:, h, :], bank[g][:, h * P:(h + 1) * P], d_gc[:, t, d, h:h + 1],
                                      ALU.subtract, 0.0, ALU.max)
                        last.then_inc(sem("dneg_ready", g), 1)
                    for g, (t, d) in enumerate(step):
                        strict, incl = (masks[1 - d][:, 128 * i:128 * (i + 1)].unsqueeze(1).broadcast_to([P, 4, P])
                                        for i in range(2))
                        dve.wait_ge(sem("dexp_ready", g), n + 1)
                        tt(d_m1[g], d_off[g], strict, ALU.mult)
                        link(tt(d_tt[g], d_off[g], incl, ALU.mult))
                        tt(d_tt[g], d_tt[g], heads(bank[4 + g][:, :], 4), ALU.mult)
                        link(tt(d_m1[g], d_m1[g], heads(bank[2 + g][:, :], 4), ALU.mult))
                        tt(d_m1[g], d_m1[g], along(d_neg[:, t, d, :], P), ALU.mult).then_inc(sem("na_ready", g), 1)
                    for g, (t, d) in enumerate(step):
                        dve.wait_ge(sem("naT_ready", g), n + 1)
                        copy(d_n[g], heads(bank[g][:, :], 4)).then_inc(d_inverse.sem("nt_ready", g), 1)
                        copy(d_at[g], heads(bank[2 + g][:, :], 4)).then_inc(sem("naT_saved", g), 1)
                    for g, (t, d) in enumerate(step):
                        v = heads(proj1[:, t, CV:CV + 512], 4)
                        k = heads(proj1[:, t, CK:CK + 512], 4)
                        beta = along(d_beta[:, t, d, :], P)
                        tt(d_kg[g], k, along(d_es[:, t, d, :], P), ALU.mult)
                        if n:
                            dve.wait_ge(sem("ks_ready"), n)
                            link(tt(d_rs[g], heads(bank[6 + g][:, :], 4), along(d_eg[:, t, d, :], P), ALU.mult))
                            link(tt(d_rs[g], v, d_rs[g], ALU.subtract))
                            tt(d_rs[g], d_rs[g], beta, ALU.mult).then_inc(sem("rs_ready", g), 1)
                        else:
                            tt(d_rs[g], v, beta, ALU.mult).then_inc(sem("rs_ready", g), 1)
                    join(d_inverse, len(RWKV_UNITS) + n)
                    for g, (t, d) in enumerate(step):
                        dve.wait_ge(sem("od_ready", g), n + 1)
                        o = heads(mixed[:, t, 0:512], 4)
                        src = heads(bank[2 + g][:, :], 4)
                        first_visit = (n, g) in ((0, 0), (1, 0), (1, 1))
                        if n:
                            link(tt(d_rs[g], heads(bank[6 + g][:, :], 4), along(d_eg[:, t, d, :], P), ALU.mult))
                            link(tt(d_rs[g], d_rs[g], src, ALU.add))
                            src = d_rs[g]
                        link(copy(o, src) if first_visit else tt(o, o, src, ALU.add))
                        if n == 0:
                            link(copy(d_sc[:, d, :, :], heads(bank[4 + g][:, :], 4)))
                        if n == 1:
                            s = d_sl[:, d, :, :]
                            link(tt(s, s, along(d_et[:, t, d, :], P), ALU.mult))
                            link(tt(s, s, heads(bank[4 + g][:, :], 4), ALU.add))
                        dve.drain().then_inc(sem("step_saved"), 1)
                oc = mixed[:, :, 0:512].rearrange("p t (h d) -> p t h d", h=4)
                tmp = arena[:, po1:po1 + 1536].rearrange("p (t h d) -> p t h d", t=TILES, h=4)
                st = stats[:, 12:24].rearrange("p (t h) -> p t h", t=TILES)
                link(tt(tmp, oc, oc, ALU.mult))
                total(st, tmp).then_inc(sem("head_sumsq"), 1)
                dve.wait_ge(sem("head_rstd"), 5)
                link(tt(oc, oc, along(st, P), ALU.mult))
                link(tt(oc, oc, params[:, 5632:5760].unsqueeze(1).unsqueeze(1).broadcast_to([P, TILES, 4, P]), ALU.mult))
                link(sigmoid_of(silu_z))
                link(tt(silu_z, silu_z, proj1[:, :, CZ:CZ + 512], ALU.mult))
                tt(mixed[:, :, 0:512], mixed[:, :, 0:512], silu_z, ALU.mult).then_inc(sem("mixed_ready"), 1)
                end_phase()

            def output_projection(l):
                for k in (1, 3, 5):
                    t, half = divmod(k, 2)
                    dve.wait_ge(sem("mixedT_ready"), 6 * l + k + 1)
                    copy(hT[:, 4 * half:4 * half + 4, t * P:(t + 1) * P], heads(bank[k][:, :], 4))\
                        .then_inc(sem("mixedT_saved", 1), 1)
                for j in range(J):
                    dve.wait_ge(sem("out_ready"), J * l + j + 1)
                    for c, a, b in ((0, 0, P), (1, P, NTOK)):
                        last = stt(xT[:, j, a:b], bank[j][:, a:b], mods[:, 2, j, c:c + 1], xT[:, j, a:b], ALU.mult,
                                   ALU.add)
                last.then_inc(sem("x_ready"), 1)
                dve.wait_ge(sem("x_ready"), 2 * l + 1)
                end_phase()

            def router(l):
                dve.wait_ge(sem("logit_exps"), l + 1)
                dve.wait_ge(sem("router_loaded"), 32 * (l + 1))
                link(sigmoid_of(m_sc))
                link(tt(m_bi, m_sc, m_bias, ALU.add))
                top = m_t0.rearrange("p t e -> p (t e)").rearrange("p (k e) -> p k e", e=8)
                bi = m_bi.rearrange("p t e -> p (t e)").rearrange("p (k e) -> p k e", e=8)
                for k in range(TILES * GROUPS):
                    last = nc.vector.max(top[:, k, :], bi[:, k, :])
                link(last)
                gs, sel, pen = (m_small[:, 24 * i:24 * i + 24] for i in range(3))
                link(tt(gs, top[:, :, 0], top[:, :, 1], ALU.add))
                g3 = heads(gs, TILES)
                gj = g3.unsqueeze(2).broadcast_to([P, TILES, GROUPS, GROUPS])
                gi = along(g3, GROUPS)
                above, equal = (a.rearrange("p (t i j) -> p t i j", t=TILES, i=GROUPS) for a in m_rank)
                tt(above, gj, gi, ALU.is_gt)
                link(tt(equal, gj, gi, ALU.is_equal))
                link(tt(equal, equal, lower_index.unsqueeze(1).broadcast_to([P, TILES, GROUPS, GROUPS]), ALU.mult))
                link(tt(above, above, equal, ALU.add))
                link(total(heads(sel, TILES), above))
                link(ts(sel, sel, float(TOP_GROUPS), ALU.is_lt))
                link(ts(pen, sel, 1.0, ALU.subtract, 1e30, ALU.mult))
                mk = m_mk.rearrange("p t e -> p (t e)").rearrange("p (k e) -> p k e", e=8)
                link(tt(mk, bi, along(sel, 8), ALU.mult))
                link(tt(mk, mk, along(pen, 8), ALU.add))
                best = m_small[:, 72:96].rearrange("p (t k) -> p t k", t=TILES)
                for t in range(TILES):
                    last = nc.vector.max(best[:, t, :], m_mk[:, t, :])
                link(last)
                for t in range(TILES):
                    ts(m_t0[:, t, :], m_mk[:, t, :], best[:, t, TOP_K - 1:TOP_K], ALU.is_gt)
                    last = ts(m_eq[:, t, :], m_mk[:, t, :], best[:, t, TOP_K - 1:TOP_K], ALU.is_equal)
                link(last)
                for t in range(TILES):
                    nc.vector.tensor_tensor_scan(m_cum[:, t, :], C["ones"][:, 0:EXPERTS], m_eq[:, t, :], 0.0, ALU.mult,
                                                 ALU.add)
                room = m_small[:, 96:99]
                link(total(room, m_t0))
                link(ts(room, room, -1.0, ALU.mult, float(TOP_K), ALU.add))
                for t in range(TILES):
                    last = ts(m_cum[:, t, :], m_cum[:, t, :], room[:, t:t + 1], ALU.is_le)
                link(last)
                link(tt(m_eq, m_eq, m_cum, ALU.mult))
                link(tt(m_t0, m_t0, m_eq, ALU.add))
                link(tt(m_w, m_t0, m_sc, ALU.mult))
                norm_ = m_small[:, 99:102]
                link(total(norm_, m_w))
                link(ts(norm_, norm_, 1e-20, ALU.add))
                link(recip(norm_))
                tt(m_w, m_w, along(norm_, EXPERTS), ALU.mult).then_inc(sem("routing_ready"), 1)
                dve.wait_ge(sem("routingT_ready"), l + 1)
                copy(m_wt[0:EXPERTS, :], bank[3][0:EXPERTS, 0:NTOK]).then_inc(sem("routingT_saved"), 1)
                end_phase()

            def experts(l):
                q0 = 2 * (EXPERTS + 1) * l

                def hidden(half, q, i=None, e=0):
                    v = lambda n: n if i is None else i * 4 + n
                    dve.wait_ge(sem("gate_exp"), v(q + 1))
                    ts(x_e[half], x_e[half], 1.0, ALU.add).then_inc(sem("plus_one"), 1)
                    dve.wait_ge(sem("plus_one"), v(q + 1))
                    recip(x_e[half]).then_inc(sem("gate_sig"), 1)
                    dve.wait_ge(sem("gate_sig"), v(q + 1))
                    tt(x_g, bank[6][:, 0:NTOK], x_e[half], ALU.mult).then_inc(sem("gated"), 1)
                    dve.wait_ge(sem("gated"), v(q + 1))
                    if i is not None:
                        dve.wait_ge(sem("down_done"), v(q - 1))
                    tt(x_h[half], bank[7][:, 0:NTOK], x_g, ALU.mult).then_inc(sem("gu_saved"), 1)
                    dve.wait_ge(sem("gu_saved"), v(q + 1))
                    if i is None:
                        dve.drain().then_inc(sem("hid_ready"), 1)
                        return
                    if half == 0:
                        dve.wait_ge(sem("rows_loaded", e), i * 16 + 16 * (l * EXPERTS // 2 + 1))
                    tt(x_h[half], x_h[half], x_bc[e], ALU.mult).then_inc(sem("hid_ready"), 1)

                hidden(0, q0)
                hidden(1, q0 + 1)
                with dve.Fori(0, EXPERTS // 2) as i:
                    for e in range(2):
                        for half in range(2):
                            hidden(half, q0 + 2 + 2 * e + half, i, e)
                dve.wait_ge(sem("y_sums_ready"), l + 1)
                for k in (1, 3, 5):
                    copy(x_y[:, k // 2, 512:1024], bank[k][:, :]).then_inc(sem("y_sums_saved"), 1)
                for k in range(6):
                    t, half = divmod(k, 2)
                    c = min(t, 1)
                    dve.wait_ge(sem("yT_ready"), 6 * l + k + 1)
                    for i in range(4):
                        j = 4 * half + i
                        x = xT[:, j, t * P:(t + 1) * P]
                        last = stt(x, bank[k][:, i * P:(i + 1) * P], mods[:, 5, j, c:c + 1], x, ALU.mult, ALU.add)
                last.then_inc(sem("x_ready"), 1)
                dve.wait_ge(sem("x_ready"), 2 * l + 2)
                end_phase()

            for l in range(LAYERS):
                modulation(l)
                norm(2 * l + 1)
                projection(l)
                (token_shift if l % 2 == 0 else convolution)()
                end_phase()
                attend(l)
                (rwkv if l % 2 == 0 else delta)()
                output_projection(l)
                norm(2 * l + 2)
                router(l)
                experts(l)

        @block.gpsimd
        def _(pool):
            def masked_parts(inv, n, groups=(0, 1)):
                for k in range(LEVELS):
                    mask = C[f"join{k}"].unsqueeze(1).broadcast_to([P, 4, P])
                    for g in groups:
                        if k == 0:
                            pool.wait_ge(inv.sem("nt_ready", g), n + 1)
                            if n:
                                pool.wait_ge(inv.sem("m_ready", g), 6 * n)
                        elif k == 1:
                            pool.wait_ge(inv.sem("t_ready", g), 7 * n + 1)
                        else:
                            pool.wait_ge(inv.sem("m_ready", g), 6 * n + k - 1)
                        nc.gpsimd.tensor_tensor(inv.off[g], inv.nt[g], mask, ALU.mult)\
                            .then_inc(inv.sem("off_ready", g), 1)

            def routing_rows(l):
                pool.wait_ge(sem("routing_stored"), 16 * (l + 1))
                pool.wait_ge(sem("phase_done_dve"), 8 * l + 7)
                q0 = 2 * (EXPERTS + 1) * l
                with pool.Fori(0, EXPERTS // 2) as i:
                    for e in range(2):
                        pool.wait_ge(sem("hid_ready"), i * 4 + max(q0 + 2 * e, 1))
                        pool.dma_start(x_bc[e], wt_dram[l, bass.ds(i * 2 + e, 1), :].broadcast_to([P, NTOK]))\
                            .then_inc(sem("rows_loaded", e), 16)

            for u in range(len(RWKV_UNITS)):
                masked_parts(r_inverse, u)
            routing_rows(0)
            for n in range(len(DELTA_STEPS)):
                masked_parts(d_inverse, len(RWKV_UNITS) + n)
            routing_rows(1)


_PLAIN = ["mod_w", "ev_w_in", "ev_w_out", "a_qn", "a_kn", "b_mu", "b_w0", "b_w2", "b_a0", "b_a2", "b_g2", "b_kk", "b_ka",
          "b_rk", "b_lnx_w", "b_lnx_b", "od_w_in", "od_w_out", "c_conv", "c_A_log", "c_dt_bias", "c_onorm", "d_qn",
          "d_kn", "d_lambda", "d_subln", "router_w", "router_bias", "exp_w_gate", "exp_w_up", "exp_w_down",
          "sh_w_gate", "sh_w_up", "sh_w_down"]
_OUTS = {"yT": (P, J, NTOK), "k_a": (P, 128), "v_a": (P, 128), "state_r": (P, 2, 4, 64), "state_d": (P, 2, 4, 128),
         "k_d": (P, 512), "v_d": (P, 512)}


def kernel(**inputs):
    import numpy as _np
    import concourse.bacc as _bacc
    from concourse import mybir as _mybir
    from concourse.bass_utils import run_bass_kernel_spmd as _run

    x = {k: _np.asarray(v) for k, v in inputs.items()}
    lay = {n: x[n] for n in _PLAIN}
    lay["xT"] = _np.concatenate([x["x_prompt"][0], x["x_sample"][0]], 0).T.reshape(P, J, NTOK)
    lay["cond"] = _np.stack([x["c_ctx"], x["c"][0]], 1).reshape(P, J, 2)
    lay["mod_b"] = x["mod_b"].reshape(LAYERS, 6, P, J).transpose(2, 0, 1, 3)
    lay["gains"] = _np.stack([x["norm1_g"], x["norm2_g"]], 1).reshape(LAYERS, 2, P, J).transpose(2, 0, 1, 3)
    lay["keys_a"] = x["cache_attn_k"][0, 0].transpose(0, 2, 1).reshape(P, P)
    lay["values_a"] = x["cache_attn_v"][0, 0].transpose(1, 0, 2)
    lay["keys_d"] = x["cache_diff_k"][0, 0].transpose(1, 3, 0, 2).reshape(P, 4, P)
    lay["values_d"] = x["cache_diff_v"][0, 0].transpose(1, 0, 2)
    lay["state_r"] = x["state_rwkv"][0, 0].reshape(2, 4, 2, 64, 64).transpose(2, 4, 0, 1, 3).reshape(P, 2, 4, 64)
    lay["state_d"] = x["state_delta"][0, 0].transpose(2, 0, 1, 3)
    lay["consts"] = constants()
    lay["rope"] = rope_rows().reshape(2, P, 2, HEAD).transpose(1, 0, 2, 3)

    nc = _bacc.Bacc("TRN2", target_bir_lowering=False, num_devices=1)
    arrays, aps = {}, {}
    for n, a in lay.items():
        a = _np.ascontiguousarray(a)
        arrays[f"in_{n}"] = a
        aps[n] = nc.dram_tensor(f"in_{n}", a.shape, _mybir.dt.from_np(a.dtype), kind="ExternalInput").ap()
    outs = {n: nc.dram_tensor(f"out_{n}", s, _mybir.dt.float32, kind="ExternalOutput").ap() for n, s in _OUTS.items()}
    build(nc, aps, outs)
    r = _run(nc, [arrays], core_ids=[0]).results[0]
    got = {n: r[f"out_{n}"] for n in _OUTS}
    y = got["yT"].reshape(D, NTOK).T
    return (y[None, :P], y[None, P:],
            got["k_a"].reshape(P, 2, 64).transpose(1, 0, 2)[None, None],
            got["v_a"].reshape(P, 2, 64).transpose(1, 0, 2)[None, None],
            got["state_r"].reshape(2, 64, 2, 4, 64).transpose(2, 3, 0, 4, 1).reshape(1, 1, 2, 8, 64, 64),
            got["state_d"].transpose(1, 2, 0, 3)[None, None],
            got["k_d"].reshape(P, 4, 2, 64).transpose(1, 2, 0, 3)[None, None],
            got["v_d"].reshape(P, 4, P).transpose(1, 0, 2)[None, None])
```

```python
import math
from contextlib import ExitStack

import numpy as np
import concourse.bass as bass
from concourse import mybir

F32 = mybir.dt.float32
BF16 = mybir.dt.bfloat16
I32 = mybir.dt.int32
ALU = mybir.AluOpType
ACT = mybir.ActivationFunctionType
AX = mybir.AxisListType

P = 128
D = 1024
J = D // P
TILES = 3
NTOK = TILES * P
LAYERS = 2
EXPERTS = 64
FF = 256
GROUPS = 8
TOP_GROUPS = 4
TOP_K = 6
HEAD = 64
EVEN_COLS = 2560
ODD_COLS = 3600
EVEN_BLOCKS = [(0, 512), (512, 768), (768, 1280), (1280, 1792), (1792, 2304), (2304, 2560)]
ODD_BLOCKS = [(0, 512), (512, 1024), (1024, 1536), (1536, 2048), (2048, 2064), (2064, 2576), (2576, 3088),
              (3088, 3600)]
XB = 768
XR, XK, XV, XW, XG = 768, 1280, 1792, 2304, 2432
CQ, CK, CV, CZ, CAB, DQ, DV = 0, 512, 1024, 1536, 2048, 2064, 3088
DECAY = math.exp(-0.5)
LAM_INIT = 0.8 - 0.6 * math.exp(-0.3 * 1)
SLOTS = 128
NOWHERE = 4096
RING = 6
SLOT = 2048
LEVELS = 7

CONSTS = ["ident", "ones", "strict0", "incl0", "strict1", "incl1", "cum_incl0", "cum_excl0", "cum_incl1",
          "cum_excl1", "prev", "next", "both", "from_prev", "from_next", "slot_index"] + [f"join{k}" for k in range(LEVELS)]
NCOL = 80


def constants():
    s = np.arange(P)[:, None]
    t = np.arange(P)[None, :]
    half = P // 2
    m = {"ident": s == t, "ones": s == s, "strict0": s < t, "incl0": s <= t, "strict1": s > t, "incl1": s >= t,
         "prev": s == t - 1, "next": s == t + 1, "both": abs(s - t) == 1,
         "from_prev": (s == P - 1) & (t == 0), "from_next": (s == 0) & (t == P - 1)}
    m["slot_index"] = np.broadcast_to(t, (P, P)).astype(np.float32)
    for d, first in ((0, s < half), (1, s >= half)):
        m[f"cum_incl{d}"] = m[f"incl{d}"].astype(np.float32) - first
        m[f"cum_excl{d}"] = m[f"strict{d}"].astype(np.float32) - first
    for k in range(LEVELS):
        m[f"join{k}"] = (s >> (k + 1) == t >> (k + 1)) & (s >> k != t >> k)
    full = np.zeros((P, len(CONSTS) * P + NCOL), np.float32)
    for i, n in enumerate(CONSTS):
        full[:, i * P:(i + 1) * P] = m[n] * np.ones((P, P), np.float32)
    o = len(CONSTS) * P
    full[:half, o] = 1
    full[half:, o + 1] = 1
    full[:, o + 2] = 1e-6
    full[:, o + 3] = 64e-5
    full[:, o + 4] = 1.0
    full[:, o + 5] = np.arange(P)
    for k in range(TILES):
        full[:, o + 72 + k] = P * k - NOWHERE
    full[:, o + 8:o + 72] = (np.arange(GROUPS)[None, :] < np.arange(GROUPS)[:, None]).reshape(-1)
    return full


def rope_rows():
    n = 2 * P
    f = HEAD // 4
    inv = (np.float32(10000.0) ** (-np.arange(f, dtype=np.float32) / f)).astype(np.float32)
    row = (np.arange(n) // 64).astype(np.float32)
    col = (np.arange(n) % 64).astype(np.float32)
    ang = np.concatenate([row[:, None] * inv, col[:, None] * inv], 1)
    c, s = np.cos(ang), np.sin(ang)
    out = np.zeros((n, 2, HEAD), np.float32)
    out[:, 0, 0::2] = c
    out[:, 0, 1::2] = c
    out[:, 1, 0::2] = -s
    out[:, 1, 1::2] = s
    return out


def weight_pieces(w):
    pieces, group = [], []

    def add(srcs):
        g = group[-1] + 1 if group else 0
        for s in srcs:
            pieces.append(s)
            group.append(g)

    starts = []
    for l in range(LAYERS):
        mod = w["mod_w"][l].rearrange("(p c) n -> p c n", c=J)
        for s in range(6):
            add([mod[:, 2 * q:2 * q + 2, s * D:(s + 1) * D] for q in range(4)])
        win = (w["ev_w_in"] if l % 2 == 0 else w["od_w_in"])[0].rearrange("(p c) n -> p c n", c=J)
        for a, b in (EVEN_BLOCKS if l % 2 == 0 else ODD_BLOCKS):
            if b - a > 256:
                add([win[:, 0:4, a:b], win[:, 4:8, a:b]])
            else:
                add([win[:, :, a:b]])
        wout = (w["ev_w_out"] if l % 2 == 0 else w["od_w_out"])[0].rearrange("(p c) n -> p c n", c=J)
        add([wout[:, 2 * q:2 * q + 2, :] for q in range(4)])
        add([w["sh_w_gate"][l].rearrange("(p c) n -> p c n", c=J), w["sh_w_up"][l].rearrange("(p c) n -> p c n", c=J)])
        add([w["sh_w_down"][l].rearrange("(p c) n -> p c n", c=2)])
        starts.append(len(pieces))
        pieces += [None] * (3 * EXPERTS)
        group += [group[-1]] * (3 * EXPERTS)
    return pieces, group, starts


def build(nc, w, outs):
    with ExitStack() as ctx:
        def sb(name, shape):
            return ctx.enter_context(nc.sbuf_tensor(name, shape, F32))

        sems = {}

        def sem(*name):
            n = "_".join(str(x) for x in name)
            if n not in sems:
                sems[n] = ctx.enter_context(nc.semaphore(n))
            return sems[n]

        consts = sb("consts", [P, len(CONSTS) * P + NCOL])
        xT = sb("xT", [P, J, NTOK])
        hT = sb("hT", [P, J, NTOK])
        mixed = sb("mixed", [P, TILES, D])
        params = sb("params", [P, 6176])
        ring = sb("ring", [P, RING, SLOT])
        cond = sb("cond", [P, J, 2])
        cond_exp = sb("cond_exp", [P, J, 2])
        mod_b = sb("mod_b", [P, LAYERS, 6, J])
        gains = sb("gains", [P, LAYERS, 2, J])
        mods = sb("mods", [P, 6, J, 2])
        rope = sb("rope", [P, 2, 2, HEAD])
        rstd = sb("rstd", [P, NTOK])
        stats = sb("stats", [P, 128])
        arena = sb("arena", [P, 21200])
        bank = [ctx.enter_context(nc.psum_tensor(f"bank{i}", [P, 512], F32)) for i in range(8)]
        wt_dram = nc.dram_tensor("routing_rows", [LAYERS, EXPERTS, NTOK], F32).ap()

        C = {n: consts[:, i * P:(i + 1) * P] for i, n in enumerate(CONSTS)}
        c0 = len(CONSTS) * P
        halves = consts[:, c0:c0 + 2]
        token_col = consts[:, c0 + 5:c0 + 6]
        tile_cols = consts[:, c0 + 72:c0 + 72 + TILES]
        eps6, eps_ln, one_col = (consts[:, c0 + i:c0 + i + 1] for i in (2, 3, 4))
        lower_index = consts[:, c0 + 8:c0 + 72].rearrange("p (i j) -> p i j", i=GROUPS)
        masks = [consts[:, (2 + 2 * d) * P:(4 + 2 * d) * P] for d in range(2)]

        def region(*sizes, at=0):
            got = []
            for n in sizes:
                got.append((at, n))
                at += n
            assert at <= 21200, at
            return [arena[:, a:a + n] for a, n in got]

        def hregion(a, n):
            return hT[:, :, :].rearrange("p j n -> p (j n)")[:, a:a + n]

        def heads(ap, n):
            return ap.rearrange("p (h d) -> p h d", h=n)

        def along(ap, n):
            return ap.unsqueeze(len(ap.shape)).broadcast_to(list(ap.shape) + [n])

        pieces, group, loops = weight_pieces(w)

        def slot(n):
            return ring[:, n % RING, :]

        def piece_value(n):
            return 16 * (n // RING + 1)

        first = []
        for l in range(LAYERS):
            s = loops[l - 1] + 3 * EXPERTS if l else 0
            f = {"mod": s, "in": s + 24}
            f["shared"] = loops[l] - 3
            f["out"] = loops[l] - 7
            first.append(f)

        block = ctx.enter_context(nc.Block())

        MEMBERS = ("pe", "act", "dve")

        def phase_end(me, eng, n):
            eng.drain().then_inc(sem("phase_done", me), 1)
            for other in MEMBERS:
                if other != me:
                    eng.wait_ge(sem("phase_done", other), n)

        def proj_of(l):
            cols = EVEN_COLS if l % 2 == 0 else ODD_COLS
            return arena[:, 0:TILES * cols].rearrange("p (t n) -> p t n", t=TILES), TILES * cols

        def projected(l, t, a, b, src):
            dst, src = proj_of(l)[0][:, t, a:b], src[:, 0:b - a]
            if l % 2 == 0 and a == 0:
                return (dst.rearrange("p (j k d) -> p k j d", j=4, k=2), src.rearrange("p (k j d) -> p k j d", j=4, k=2))
            return dst, src

        squares = arena[:, 0:J * NTOK].rearrange("p (j n) -> p j n", j=J)

        def wait_slot_free(sp, n):
            m = n - RING
            for l in range(LAYERS):
                if loops[l] <= m < loops[l] + 3 * EXPERTS:
                    e, k = divmod(m - loops[l], 3)
                    sp.wait_ge(sem("down_used" if k == 2 else "gate_up_used"), EXPERTS * l + e + 1)
                    return
            if m >= 0:
                sp.wait_ge(sem("ring_released"), group[m] + 1)

        def load_experts(sp, l):
            n0 = loops[l]

            def load(k, e):
                src = w[("exp_w_gate", "exp_w_up", "exp_w_down")[k % 3]]
                c = 2 if k % 3 == 2 else J
                sp.dma_start(slot(n0 + k).rearrange("p (c k) -> p c k", c=c),
                             src[l, bass.ds(e, 1)].rearrange("e (p c) n -> (e p) c n", c=c))\
                    .then_inc(sem("ring_loaded", (n0 + k) % RING), 16)

            for k in range(6):
                wait_slot_free(sp, n0 + k)
                load(k, k // 3)
            with sp.Fori(1, EXPERTS // 2) as i:
                for k in range(6):
                    used = sem("down_used" if k % 3 == 2 else "gate_up_used")
                    sp.wait_ge(used, i * 2 + (EXPERTS * l + k // 3 - 1))
                    load(k, i * 2 + k // 3)

        @block.sync
        def _(sp):
            sp.dma_start(xT[:, :, :], w["xT"]).then_inc(sem("x_loaded"), 16)
            for n, src in enumerate(pieces):
                if src is None:
                    continue
                _, c, k = src.shape
                wait_slot_free(sp, n)
                sp.dma_start(slot(n)[:, 0:c * k].rearrange("p (c k) -> p c k", c=c), src)\
                    .then_inc(sem("ring_loaded", n % RING), 16)
                if n + 1 in loops:
                    l = loops.index(n + 1)
                    load_experts(sp, l)
            sp.wait_ge(sem("x_ready"), 2 * LAYERS)
            sp.dma_start(outs["yT"], xT[:, :, :]).then_inc(sem("stored"), 16)
            sp.wait_ge(sem("stored"), 16 * 7)

        RWKV_UNITS = [(0, 0), (0, 1), (1, 0), (2, 1), (2, 0), (1, 1)]
        DELTA_STEPS = [[(0, 0), (0, 1)], [(1, 0), (2, 1)], [(2, 0), (1, 1)]]
        RWKV_KEEPS = (0, 1, 2, 3)
        DELTA_KEEPS = (0, 1)

        class Attention:
            def __init__(self, l):
                self.l = l
                self.even = l % 2 == 0
                self.proj, po = proj_of(l)
                self.base = 0 if self.even else DQ
                self.nh = 10 if self.even else 16
                self.kc = 1 if self.even else 4
                self.vd = 64 if self.even else 128
                self.vbase = 640 if self.even else DV
                nkv = 2 if self.even else 4
                (self.qt, self.kctx, self.klat, self.vc, self.p, self.pt, self.t1, self.t2, self.ss, self.mx,
                 self.sums, self.rinv, self.neg) = region(1536, self.kc * 128, self.kc * 384, nkv * self.vd, 768, 768,
                                                          1024, 1024, 48, 24, 24, 24, 8, at=po)
                self.qt = self.qt.rearrange("p (t c n) -> p t c n", t=TILES, c=4)
                self.kctx = self.kctx.rearrange("p (c n) -> p c n", c=self.kc)
                self.klat = self.klat.rearrange("p (c t n) -> p c t n", c=self.kc, t=TILES)
                self.vc = self.vc.rearrange("p (h d) -> p h d", h=nkv)
                self.p = self.p.rearrange("p (b n) -> p b n", b=2)
                self.pt = self.pt.rearrange("p (b n) -> p b n", b=2)
                self.gain = params[:, 0:640] if self.even else params[:, 4608:5632]
                self.per_bank = 512 // self.vd

            def qk(self, t):
                return self.proj[:, t, self.base:self.base + 64 * self.nh]

            def unit(self, u):
                t, h = divmod(u, 8)
                kt = 1 if t == 0 else 3
                if self.even:
                    return t, kt, h % 4, 64 * (h // 4), 0, h // 4
                return t, kt, h // 2, 64 * (h % 2), h // 2, h // 2

            def values(self, t, kt, vh):
                if t > 0 and kt == 0:
                    return self.vc[:, vh, :]
                src = 0 if t == 0 else kt
                return self.proj[:, src, self.vbase + vh * self.vd:self.vbase + (vh + 1) * self.vd]

        attention = [Attention(l) for l in range(LAYERS)]

        class Inverse:
            def __init__(self, nt, off, t, tt, m1):
                four = lambda aps: [a.rearrange("p (h n) -> p h n", h=4) if len(a.shape) == 2 else a for a in aps]
                self.nt, self.off, self.t, self.tt, self.m1 = nt, four(off), four(t), four(tt), four(m1)

            def sem(self, name, g):
                return sem("inverse", name, g)

        proj0, po0 = proj_of(0)
        (r_ar, r_bt, r_kt, r_tokb, r_tokk, r_toka, r_tokr, r_nr0, r_nr1, r_ak0, r_ak1, *r_inv, r_rs, r_us) = region(
            1024, 512, 512, 512, 512, 512, 512, 1024, 1024, 1024, 1024, *([512] * 8), 512, 512, at=po0)
        r_ar = r_ar.rearrange("p (c k n) -> p c k n", c=4, k=2)
        r_bt, r_kt = (a.rearrange("p (c n) -> p c n", c=4) for a in (r_bt, r_kt))
        r_nr = [a.rearrange("p (c k n) -> p c k n", c=4, k=2) for a in (r_nr0, r_nr1)]
        r_ak = [a.rearrange("p (c k n) -> p c k n", c=4, k=2) for a in (r_ak0, r_ak1)]
        r_inverse = Inverse([a[:, :, 0, :] for a in r_nr], r_inv[0:2], r_inv[2:4], r_inv[4:6], r_inv[6:8])
        r_sig, r_gate, r_ei, r_ev, r_ee, r_x = r_inv[0:6]
        r_rs, r_us = (a.rearrange("p (h d) -> p h d", h=8) for a in (r_rs, r_us))
        r_lora, r_w0, r_a0 = hregion(0, 1024), hregion(1024, 1024), hregion(2048, 1024)
        r_mu = params[:, 640:2432]
        r_kk, r_ka, r_rk, r_lnw, r_lnb, r_g2 = (params[:, 2432 + 512 * i:2944 + 512 * i] for i in range(6))
        state4 = lambda ap: ap.rearrange("p (d j v) -> p d j v", d=2, j=4)
        r_sl = state4(params[:, 5504:6016])
        r_sc = state4(params[:, 640:1152])
        r_sw = params[:, 1152:1408].rearrange("p (j v) -> p j v", j=4)
        r_ec = params[:, 1408:1416].rearrange("p (j h) -> p j h", j=4)
        kk_of = lambda t: proj0[:, t, 0:512]
        lt_of = lambda t: proj0[:, t, 512:640]
        gt_of = lambda t: proj0[:, t, 640:768]
        yacc_of = lambda t: mixed[:, t, 512:1024]

        proj1, po1 = proj_of(1)
        d_buf = [region(*([512] * 10), at=po1 + g * 5120) for g in range(2)]
        d_di, d_at, d_n, d_off, d_t, d_tt, d_m1, d_rs, d_vn, d_kg = (
            [b[i].rearrange("p (h n) -> p h n", h=4) for b in d_buf] for i in range(10))
        d_inverse = Inverse(d_n, d_off, d_t, d_tt, d_m1)
        d_kt = hregion(0, 1536).rearrange("p (t h n) -> p t h n", t=TILES, h=4)
        d_qt = hregion(1536, 1536).rearrange("p (t h n) -> p t h n", t=TILES, h=4)
        d_sl = params[:, 0:1024].rearrange("p (d h v) -> p d h v", d=2, h=4)
        d_sc = params[:, 1024:2048].rearrange("p (d h v) -> p d h v", d=2, h=4)
        small = lambda i: params[:, 2048 + 24 * i:2072 + 24 * i].rearrange("p (t d h) -> p t d h", t=TILES, d=2)
        d_g, d_beta, d_tmp, d_gc, d_eg, d_es, d_et, d_neg = (small(i) for i in range(8))
        conv_w = params[:, 0:4608].rearrange("p (k n) -> p k n", k=3)
        conv_exp = lambda t: arena[:, po1 + 1536 * t:po1 + 1536 * (t + 1)]
        conv_tmp = arena[:, po1 + 4608:po1 + 5632]
        silu_z = arena[:, po1 + 1536:po1 + 3072].rearrange("p (t n) -> p t n", t=TILES)

        m_w, m_sc, m_bi, m_mk, m_eq, m_t0, m_cum = (
            a.rearrange("p (t e) -> p t e", t=TILES) for a in region(*([192] * 7), at=3072))
        m_small, = region(256, at=3072 + 7 * 192)
        m_rank = region(192, 192, at=3072 + 7 * 192 + 256)
        m_bias, m_router, m_wt = region(64, 512, 384, at=3072 + 9 * 192 + 256)
        m_bias_buf = m_bias
        m_bias = m_bias.unsqueeze(1).broadcast_to([P, TILES, EXPERTS])
        m_router = m_router.rearrange("p (c e) -> p c e", c=J)
        m_at = 3072 + 9 * 192 + 256 + 960
        x_bc0, x_bc1, x_e0, x_e1, x_h0, x_h1 = region(*([NTOK] * 6), at=m_at)
        x_bc, x_e, x_h = [x_bc0, x_bc1], [x_e0, x_e1], [x_h0, x_h1]
        y_at = m_at + 6 * NTOK
        x_y = arena[:, y_at:y_at + 3072].rearrange("p (t n) -> p t n", t=TILES)
        g_at = y_at + 3072
        (g_x0, g_x1, g_xt0, g_xt1, g_s0, g_s1, g_h0, g_h1, g_ht0, g_ht1, g_y0, g_y1, g_pos, g_tab, g_rows, g_w, g_idx,
         g_flag) = region(1024, 1024, 1024, 1024, 256, 256, 256, 256, 256, 256, 1024, 1024, 192, 576, 128, 64, 8, 8,
                          at=g_at)
        g_one0, g_one1 = g_xt0[:, 0:768], g_xt1[:, 0:768]
        g_x, g_y, g_s, g_h = [g_x0, g_x1], [g_y0, g_y1], [g_s0, g_s1], [g_h0, g_h1]
        g_xt = [a.rearrange("p (c n) -> p c n", c=J) for a in (g_xt0, g_xt1)]
        g_ht = [a.rearrange("p (c n) -> p c n", c=2) for a in (g_ht0, g_ht1)]
        g_pos = g_pos.rearrange("p (t e) -> p t e", t=TILES)
        g_tab = g_tab.bitcast(BF16).rearrange("p (t e k) -> p t e k", t=TILES, e=EXPERTS)
        g_rows = g_rows.bitcast(I32).rearrange("p (k e) -> p k e", k=2)
        g_one = [a.bitcast(BF16).rearrange("p (q t n) -> p q t n", q=4, t=TILES) for a in (g_one0, g_one1)]
        g_idx = g_idx.bitcast(I32)
        g_overflow = g_flag.bitcast(I32)[0:1, 0:1]
        y_load = [arena[:, a:a + 6144].rearrange("p (k n) -> p k n", k=TOP_K) for a in (0, g_at)]
        x_rows = [nc.dram_tensor(f"token_rows_{l}", [NTOK, D], F32).ap() for l in range(LAYERS)]
        y_rows = [nc.dram_tensor(f"choice_rows_{l}", [TOP_K * NTOK, D], F32).ap() for l in range(LAYERS)]

        class Turn:
            def __init__(self, l, e, i=None):
                self.l, self.e, self.i, self.b = l, e, i, e % 2
                n = loops[l] + 3 * e
                self.gate, self.up, self.down = n, n + 1, n + 2

            def count(self, back=0):
                n = EXPERTS * self.l + self.e + 1 - back
                return n if self.i is None else self.i * 2 + n

            def dmas(self, before=0):
                n = 16 * ((EXPERTS * self.l + self.e) // 2 + 1 - before)
                return n if self.i is None else self.i * 16 + n

            def scatters_before(self):
                n = 16 * (self.e // 2)
                return n if self.i is None else self.i * 16 + n

            def column(self):
                return slice(self.e, self.e + 1) if self.i is None else bass.ds(self.i * 2 + self.e, 1)

            def loaded(self, eng, n):
                v = piece_value(n)
                eng.wait_ge(sem("ring_loaded", n % RING), v if self.i is None else self.i * 16 + v)

        def each_expert(eng, l, step):
            for e in range(3):
                step(Turn(l, e))
            with eng.Fori(0, EXPERTS // 2 - 3) as i:
                for e in (3, 4):
                    step(Turn(l, e, i))
            for e in range(EXPERTS - 3, EXPERTS):
                step(Turn(l, e))

        def after(turn):
            return Turn(turn.l, turn.e + 1, turn.i)

        def before(turn):
            return Turn(turn.l, turn.e - 1, turn.i)

        def choices(t):
            return 8 * EXPERTS + 16 * (t // 2 + 1)

        row_banks = (4, 5, 6, 7, 0, 1)
        N = EXPERTS
        DENSE_PE = [(("gu_ready",), 2 * N), (("down_done",), 2 * N)]
        SPARSE_PE = [(("xt_ready",), N), (("ht_ready",), N)]
        DENSE_ACT = [(("gate_silu",), 2 * N)]
        SPARSE_ACT = [(("xt_saved_a",), N), (("ht_saved",), N), (("slots_saved_a",), N), (("slot_silu",), N)]
        DENSE_DVE = [(("gu_saved",), 2 * N), (("hid_ready",), 2 * N)]
        SPARSE_DVE = [(("xt_saved_b",), N), (("slot_hidden",), N), (("slots_saved_b",), N), (("choices_summed",), TILES * TOP_K)]

        def by_load(eng, l, dense, sparse, dense_counts, sparse_counts):
            overflow = eng.value_load(g_overflow, min_val=0, max_val=1)
            with eng.If(overflow > 0):
                dense(l)
                for name, n in sparse_counts:
                    eng.sem_inc(sem(*name), n)
            with eng.Else():
                sparse(l)
                for name, n in dense_counts:
                    eng.sem_inc(sem(*name), n)

        @block.tensor
        def _(pe):
            phase = [0]
            used = [0]

            def mm(out, lhsT, rhs, start=True, stop=True, **kw):
                return nc.tensor.matmul(out, lhsT, rhs, start=start, stop=stop, **kw)

            def end_phase():
                phase[0] += 1
                phase_end("pe", pe, phase[0])

            def loaded(n):
                pe.wait_ge(sem("ring_loaded", n % RING), piece_value(n))

            def rows(n, per, width):
                return slot(n)[:, 0:per * width].rearrange("p (c k) -> p c k", c=per)

            def modulation(l):
                pe.wait_ge(sem("cond_ready"), 1)
                n0 = first[l]["mod"]
                for s in range(6):
                    for q in range(4):
                        loaded(n0 + 4 * s + q)
                    for j in range(J):
                        o = (s * J + j) * 2
                        for c in range(J):
                            lhs = rows(n0 + 4 * s + c // 2, 2, D)[:, c % 2, j::J]
                            last = mm(bank[0][:, o:o + 2], lhs, cond[:, c, :], c == 0, c == J - 1)
                    last.then_inc(sem("ring_released"), 1)
                end_phase()

            def norm(n):
                pe.wait_ge(sem("squares_ready"), n)
                for c in range(J):
                    last = mm(bank[1][:, 0:NTOK], C["ones"], squares[:, c, :], c == 0, c == J - 1)
                last.then_inc(sem("sumsq_ready"), 1)

            def projection(l):
                pe.wait_ge(sem("h_ready"), 2 * l + 1)
                n = first[l]["in"]
                k = 0
                for a, b in (EVEN_BLOCKS if l % 2 == 0 else ODD_BLOCKS):
                    wide = b - a > 256
                    loaded(n)
                    if wide:
                        loaded(n + 1)
                    for t in range(TILES):
                        if k >= 6:
                            pe.wait_ge(sem("proj_saved", k % 2), 9 * l + (k - 6) // 2 + 1)
                        for c in range(J):
                            rhs = rows(n + c // 4, 4, b - a)[:, c % 4, :] if wide else rows(n, J, b - a)[:, c, :]
                            last = mm(bank[k % 6][:, 0:b - a], hT[:, c, t * P:(t + 1) * P], rhs, c == 0, c == J - 1)
                        last.then_inc(sem("proj_ready"), 1)
                        k += 1
                    n += 2 if wide else 1
                    pe.drain().then_inc(sem("ring_released"), 1)
                end_phase()

            def token_shift():
                for b in range(4):
                    cols = slice(XB + 448 * b, XB + 448 * (b + 1))
                    if b >= 2:
                        pe.wait_ge(sem("near_saved"), b - 1)
                    for t in range(TILES):
                        out = bank[3 * (b % 2) + t][:, 0:448]
                        last = mm(out, C["both"], proj0[:, t, cols], True, t == 0)
                        if t == 1:
                            last = mm(out, C["from_next"], proj0[:, 2, cols], False, True)
                        if t == 2:
                            last = mm(out, C["from_prev"], proj0[:, 1, cols], False, True)
                    last.then_inc(sem("near_ready"), 1)

            def convolution():
                for b in range(3):
                    cols = slice(512 * b, 512 * (b + 1))
                    if b >= 1:
                        pe.wait_ge(sem("near_saved"), 4 + b)
                    for t in range(TILES):
                        mm(bank[t][:, :], C["prev"], proj1[:, t, cols], True, t != 2)
                        if t == 2:
                            mm(bank[t][:, :], C["from_prev"], proj1[:, 1, cols], False, True)
                        last = mm(bank[3 + t][:, :], C["next"], proj1[:, t, cols], True, t != 1)
                        if t == 1:
                            last = mm(bank[3 + t][:, :], C["from_next"], proj1[:, 2, cols], False, True)
                    last.then_inc(sem("near_ready"), 1)

            def attend(l):
                A = attention[l]
                for t in range(TILES):
                    pe.wait_ge(sem("qk_ready"), TILES * l + t + 1)
                    for c in range(4):
                        src = A.qk(t)[:, 128 * c:128 * (c + 1)]
                        nc.tensor.transpose(bank[2 * t][:, 128 * c:128 * (c + 1)], src, C["ident"])
                    for c in range(A.kc):
                        k0 = 512 + 128 * c
                        last = nc.tensor.transpose(bank[2 * t + 1][:, 128 * c:128 * (c + 1)], A.qk(t)[:, k0:k0 + 128],
                                                   C["ident"])
                    last.then_inc(sem("qkT_ready"), 1)

                def scores(u):
                    t, kt, qc, p0, kc, _ = A.unit(u)
                    if u == 0:
                        pe.wait_ge(sem("parts_loaded"), 64 * l + 32)
                        pe.wait_ge(sem("qT_saved"), TILES * l + TILES)
                        pe.wait_ge(sem("kT_saved"), TILES * l + TILES)
                    if u >= 2:
                        pe.wait_ge(sem("p_ready"), 24 * l + u - 1)
                    rhs = (A.kctx[p0:p0 + 64, kc, :] if kt == 1 else A.klat[p0:p0 + 64, kc, :, :])
                    mm(bank[u % 2][:, 0:kt * P], A.qt[p0:p0 + 64, t, qc, :], rhs).then_inc(sem("s_ready"), 1)

                def turn(u):
                    _, kt, *_ = A.unit(u)
                    pe.wait_ge(sem("p_ready"), 24 * l + u + 1)
                    if u >= 2:
                        pe.wait_ge(sem("pT_saved"), 24 * l + u - 1)
                    for k in range(kt):
                        last = nc.tensor.transpose(bank[2 + u % 2][:, k * P:(k + 1) * P],
                                                   A.p[:, u % 2, k * P:(k + 1) * P], C["ident"])
                    last.then_inc(sem("pT_ready"), 1)

                def weigh(u):
                    t, kt, _, _, _, vh = A.unit(u)
                    g, r = divmod(u, A.per_bank)
                    pe.wait_ge(sem("pT_saved"), 24 * l + u + 1)
                    if r == 0 and g >= 2:
                        pe.wait_ge(sem("o_saved"), 3 * l + g - 1)
                    for k in range(kt):
                        last = mm(bank[4 + g % 2][:, r * A.vd:(r + 1) * A.vd], A.pt[:, u % 2, k * P:(k + 1) * P],
                                  A.values(t, k, vh), k == 0, k == kt - 1)
                    last.then_inc(sem("o_ready"), 1)

                for u in range(26):
                    if u < 24:
                        scores(u)
                    if 1 <= u <= 24:
                        turn(u - 1)
                    if u >= 2:
                        weigh(u - 2)
                end_phase()

            def invert(inv, n, groups=(0, 1)):
                for g in groups:
                    pe.wait_ge(inv.sem("off_ready", g), 7 * n + 1)
                    for h in range(4):
                        last = nc.tensor.transpose(bank[2 + g][:, h * P:(h + 1) * P], inv.off[g][:, h, :], C["ident"])
                    last.then_inc(inv.sem("turned", g), 1)
                for k in range(1, LEVELS):
                    for g in groups:
                        pe.wait_ge(inv.sem("off_ready", g), 7 * n + k + 1)
                        pe.wait_ge(inv.sem("t_ready", g), 7 * n + k)
                        for h in range(4):
                            last = mm(bank[g][:, h * P:(h + 1) * P], inv.off[g][:, h, :], inv.t[g][:, h, :])
                        last.then_inc(inv.sem("m_ready", g), 1)
                    for g in groups:
                        pe.wait_ge(inv.sem("m_saved", g), 6 * n + k)
                        for h in range(4):
                            if k < LEVELS - 1:
                                mm(bank[2 + g][:, h * P:(h + 1) * P], inv.tt[g][:, h, :], inv.m1[g][:, h, :])
                            last = mm(bank[4 + g][:, h * P:(h + 1) * P], inv.m1[g][:, h, :], inv.tt[g][:, h, :])
                        last.then_inc(inv.sem("join_ready", g), 1)

            def rwkv():
                for t in range(TILES):
                    pe.wait_ge(sem("lora_ready"), 1)
                    if t >= 1:
                        pe.wait_ge(sem("lora_saved"), t)
                    nc.tensor.transpose(bank[0][:, 0:P], proj0[:, t, XW:XW + P], C["ident"])
                    nc.tensor.transpose(bank[0][:, P:2 * P], proj0[:, t, XG:XG + P], C["ident"])\
                        .then_inc(sem("lora_turned"), 1)
                pe.wait_ge(sem("state_loaded"), 16 * 6)
                for u, (t, d) in enumerate(RWKV_UNITS):
                    pe.wait_ge(sem("lora_saved"), TILES)
                    if u:
                        pe.wait_ge(sem("unit_saved"), u)
                    mm(bank[0][:, :], lt_of(t)[0:64, :], r_lora[0:64, 512 * d:512 * (d + 1)])
                    mm(bank[1][:, :], lt_of(t)[64:128, :], r_lora[64:128, 512 * d:512 * (d + 1)])\
                        .then_inc(sem("za_ready"), 1)
                    pe.wait_ge(sem("sig_ready"), u + 1)
                    mm(bank[2][:, :], C[f"cum_incl{d}"], r_sig)
                    mm(bank[3][:, :], C[f"cum_excl{d}"], r_sig)
                    for j in range(4):
                        last = mm(bank[4][:, 2 * j:2 * j + 2], r_sig[:, 128 * j:128 * (j + 1)], halves)
                    last.then_inc(sem("cum_ready"), 1)
                    pe.wait_ge(sem("tok_ready"), u + 1)
                    for b, src in enumerate((r_toka, r_tokr, r_tokb, r_tokk)):
                        for j in range(4):
                            last = nc.tensor.transpose(bank[b][:, j * P:(j + 1) * P], src[:, j * P:(j + 1) * P], C["ident"])
                    last.then_inc(sem("tokT_ready"), 1)
                    pe.wait_ge(sem("arT_saved"), u + 1)
                    pe.wait_ge(sem("bkT_saved"), u + 1)
                    for g in range(2):
                        p = slice(64 * g, 64 * g + 64)
                        if g:
                            pe.wait_ge(sem("gram_saved"), 2 * u + g)
                        for j in range(4):
                            mm(bank[4 + j // 2][:, 256 * (j % 2):256 * (j % 2) + 256], r_bt[p, j, :], r_ar[p, j, :, :])
                            last = mm(bank[6 + j // 2][:, 256 * (j % 2):256 * (j % 2) + 256], r_kt[p, j, :],
                                      r_ar[p, j, :, :])
                        last.then_inc(sem("gram_ready"), 1)
                    pe.wait_ge(sem("gram_saved"), 2 * u + 2)
                    for g in range(2):
                        p = slice(64 * g, 64 * g + 64)
                        for j in range(4):
                            h = 2 * j + g
                            v = proj0[:, t, XV + 64 * h:XV + 64 * h + 64]
                            out = bank[6 + g][:, 64 * j:64 * j + 64]
                            if t:
                                mm(out, r_ar[p, j, 0, :], r_sw[p, j, :], True, False)
                            last = mm(out, r_ak[g][:, j, 0, :], v, t == 0, True)
                    last.then_inc(sem("read_ready"), 1)
                    invert(r_inverse, u)
                    pe.wait_ge(sem("read_saved"), u + 1)
                    for g in range(2):
                        pe.wait_ge(r_inverse.sem("t_ready", g), 7 * (u + 1))
                        for j in range(4):
                            last = mm(bank[g][:, 64 * j:64 * j + 64], r_inverse.tt[g][:, j, :], r_rs[:, 2 * j + g, :])
                    last.then_inc(sem("u_ready"), 1)
                    pe.wait_ge(sem("u_saved"), u + 1)
                    for g in range(2):
                        p = slice(64 * g, 64 * g + 64)
                        for j in range(4):
                            h = 2 * j + g
                            v = proj0[:, t, XV + 64 * h:XV + 64 * h + 64]
                            out = bank[2 + g][:, 64 * j:64 * j + 64]
                            if t:
                                mm(out, r_ar[p, j, 1, :], r_sw[p, j, :], True, False)
                            mm(out, r_nr[g][:, j, 1, :], r_us[:, h, :], t == 0, False)
                            last = mm(out, r_ak[g][:, j, 1, :], v, False, True)
                            if u in RWKV_KEEPS:
                                out = bank[4 + g][p, 64 * j:64 * j + 64]
                                mm(out, r_tokb[:, 64 * h:64 * h + 64], r_us[:, h, :], True, False)
                                last = mm(out, r_tokk[:, 64 * h:64 * h + 64], v, False, True)
                    last.then_inc(sem("y_unit_ready"), 1)
                pe.wait_ge(sem("unit_saved"), 6)
                for t in range(TILES):
                    last = mm(bank[t][:, :], gt_of(t), r_g2)
                last.then_inc(sem("gate_ready"), 1)
                end_phase()

            def delta():
                for t in range(TILES):
                    pe.wait_ge(sem("ck_ready"), 1)
                    for h in range(4):
                        nc.tensor.transpose(bank[2 * t][:, h * P:(h + 1) * P], proj1[:, t, CK + h * P:CK + (h + 1) * P],
                                            C["ident"])
                        last = nc.tensor.transpose(bank[2 * t + 1][:, h * P:(h + 1) * P],
                                                   proj1[:, t, CQ + h * P:CQ + (h + 1) * P], C["ident"])
                    last.then_inc(sem("ckT_ready"), 1)
                pe.wait_ge(sem("g_ready"), 1)
                for t in range(TILES):
                    for d in range(2):
                        for i, m in enumerate((f"incl{d}", f"strict{1 - d}", "ones")):
                            o = ((i * TILES + t) * 2 + d) * 4
                            last = mm(bank[6][:, o:o + 4], C[m], d_g[:, t, d, :])
                last.then_inc(sem("gsum_ready"), 1)
                for n, step in enumerate(DELTA_STEPS):
                    if n:
                        pe.wait_ge(sem("step_saved"), 2 * n)
                    else:
                        pe.wait_ge(sem("ckT_saved"), TILES)
                        pe.wait_ge(sem("cqT_saved"), TILES)
                        pe.wait_ge(sem("decay_cols_ready"), 1)
                    for g, (t, d) in enumerate(step):
                        pe.wait_ge(sem("gi_ready"), 2 * n + g + 1)
                        mm(bank[g][:, :], C["ones"], d_t[g].rearrange("p h n -> p (h n)"))
                        for h in range(4):
                            mm(bank[2 + g][:, h * P:(h + 1) * P], d_kt[:, t, h, :], d_kt[:, t, h, :])
                            last = mm(bank[4 + g][:, h * P:(h + 1) * P], d_qt[:, t, h, :], d_kt[:, t, h, :])
                        last.then_inc(sem("dgram_ready"), 1)
                    for g, (t, d) in enumerate(step):
                        pe.wait_ge(sem("na_ready"), 2 * n + g + 1)
                        for h in range(4):
                            nc.tensor.transpose(bank[g][:, h * P:(h + 1) * P], d_m1[g][:, h, :], C["ident"])
                            last = nc.tensor.transpose(bank[2 + g][:, h * P:(h + 1) * P], d_tt[g][:, h, :], C["ident"])
                        last.then_inc(sem("naT_ready"), 1)
                    if n:
                        pe.wait_ge(sem("state_loaded"), 16 * 7)
                        for g, (t, d) in enumerate(step):
                            for h in range(4):
                                last = mm(bank[6 + g][:, h * P:(h + 1) * P], d_kt[:, t, h, :], d_sl[:, d, h, :])
                        last.then_inc(sem("ks_ready"), 1)
                    for g in range(2):
                        pe.wait_ge(sem("naT_saved"), 2 * n + g + 1)
                    invert(d_inverse, len(RWKV_UNITS) + n)
                    for g in range(2):
                        pe.wait_ge(sem("rs_ready"), 2 * n + g + 1)
                        pe.wait_ge(d_inverse.sem("t_ready", g), LEVELS * (len(RWKV_UNITS) + n + 1))
                        for h in range(4):
                            last = mm(bank[g][:, h * P:(h + 1) * P], d_tt[g][:, h, :], d_rs[g][:, h, :])
                        last.then_inc(sem("vn_ready"), 1)
                    for g, (t, d) in enumerate(step):
                        pe.wait_ge(sem("vn_saved"), 2 * n + g + 1)
                        for h in range(4):
                            last = mm(bank[2 + g][:, h * P:(h + 1) * P], d_at[g][:, h, :], d_vn[g][:, h, :])
                            if n:
                                last = mm(bank[6 + g][:, h * P:(h + 1) * P], d_qt[:, t, h, :], d_sl[:, d, h, :])
                            if n in DELTA_KEEPS:
                                last = mm(bank[4 + g][:, h * P:(h + 1) * P], d_kg[g][:, h, :], d_vn[g][:, h, :])
                        last.then_inc(sem("od_ready"), 1)
                end_phase()

            def output_projection(l):
                pe.wait_ge(sem("mixed_ready"), l + 1)
                for k in range(6):
                    t, half = divmod(k, 2)
                    for i in range(4):
                        last = nc.tensor.transpose(bank[k][:, i * P:(i + 1) * P], mixed[:, t, 4 * half + i::J], C["ident"])
                    last.then_inc(sem("mixedT_ready"), 1)
                pe.wait_ge(sem("mixedT_saved", 0), 3 * (l + 1))
                pe.wait_ge(sem("mixedT_saved", 1), 3 * (l + 1))
                n = first[l]["out"]
                for q in range(4):
                    loaded(n + q)
                for j in range(J):
                    for c in range(J):
                        last = mm(bank[j][:, 0:NTOK], rows(n + c // 2, 2, D)[:, c % 2, j::J], hT[:, c, :], c == 0,
                                  c == J - 1)
                    last.then_inc(sem("out_ready"), 1)
                pe.drain().then_inc(sem("ring_released"), 1)
                end_phase()

            def router(l):
                pe.wait_ge(sem("h_ready"), 2 * l + 2)
                pe.wait_ge(sem("parts_loaded"), 64 * l + 64)
                for k in range(6):
                    t, half = divmod(k, 2)
                    for i in range(4):
                        last = nc.tensor.transpose(bank[row_banks[k]][:, i * P:(i + 1) * P],
                                                   hT[:, 4 * half + i, t * P:(t + 1) * P], C["ident"])
                    last.then_inc(sem("rows_ready"), 1)
                for t in range(TILES):
                    for c in range(J):
                        last = mm(bank[2][:, 64 * t:64 * t + 64], hT[:, c, t * P:(t + 1) * P], m_router[:, c, :], c == 0,
                                  c == J - 1)
                last.then_inc(sem("logits_ready"), 1)
                pe.wait_ge(sem("routing_ready"), l + 1)
                for t in range(TILES):
                    last = nc.tensor.transpose(bank[3][0:EXPERTS, t * P:(t + 1) * P], m_w[:, t, :], C["ident"])
                last.then_inc(sem("routingT_ready"), 1)
                for t in range(TILES):
                    for s in range(t):
                        mm(bank[2][:, 64 * t:64 * t + 64], C["ones"], m_t0[:, s, :], s == 0, False)
                    mm(bank[2][:, 64 * t:64 * t + 64], C["strict0"], m_t0[:, t, :], t == 0, True)
                for t in range(TILES):
                    last = mm(bank[2][:, 192:256], C["ones"], m_t0[:, t, :], t == 0, t == 2)
                last.then_inc(sem("places_ready"), 1)
                pe.wait_ge(sem("table_ready"), l + 1)
                pe.wait_ge(sem("routingT_saved"), l + 1)
                groups = EXPERTS // 4
                with pe.Fori(0, groups // 2) as i:
                    for b in range(2):
                        pe.wait_ge(sem("one_hot_ready"), i * 2 + (groups * l + b + 1))
                        for q in range(4):
                            for t in range(TILES):
                                last = mm(bank[3][:, bass.ds(i * 48 + (4 * b + q) * 6, 6)], g_one[b][:, q, t, :],
                                          g_tab[:, t, bass.ds(i * 8 + (4 * b + q), 1), :].rearrange("p a k -> p (a k)"),
                                          t == 0, t == TILES - 1)
                        last.then_inc(sem("one_hot_used"), 1)
                pe.drain().then_inc(sem("picks_ready"), 1)
                end_phase()

            def gate_up(gate, up, half):
                for w_, b in ((gate, 6), (up, 7)):
                    for c in range(J):
                        last = mm(bank[b][:, 0:NTOK], w_[:, c, half::2], hT[:, c, :], c == 0, c == J - 1)
                return last

            def down(wd, half, hid, opens):
                for t in range(TILES):
                    for b in range(2):
                        last = mm(bank[2 * t + b][:, :], hid[:, t * P:(t + 1) * P], wd[:, half, b * 512:(b + 1) * 512],
                                  opens, True, skip_group_check=True)
                return last

            def dense(l):
                q0 = 2 * (EXPERTS + 1) * l + 2
                n0 = loops[l]
                with pe.Fori(0, EXPERTS // 2) as i:
                    for e in range(2):
                        m = n0 + 3 * e
                        q = q0 + 2 * e
                        gate, up, dn = (rows(m, J, FF), rows(m + 1, J, FF), rows(m + 2, 2, D))
                        for k in range(2):
                            pe.wait_ge(sem("ring_loaded", (m + k) % RING), i * 16 + piece_value(m + k))
                        pe.wait_ge(sem("gu_saved"), i * 4 + q)
                        gate_up(gate, up, 0).then_inc(sem("gu_ready"), 1)
                        pe.wait_ge(sem("gu_saved"), i * 4 + (q + 1))
                        gate_up(gate, up, 1).then_inc(sem("gu_ready"), 1)
                        pe.drain().then_inc(sem("gate_up_used"), 1)
                        pe.wait_ge(sem("ring_loaded", (m + 2) % RING), i * 16 + piece_value(m + 2))
                        pe.wait_ge(sem("hid_ready"), i * 4 + (q + 1))
                        down(dn, 0, x_h[0], False).then_inc(sem("down_done"), 1)
                        pe.wait_ge(sem("hid_ready"), i * 4 + (q + 2))
                        down(dn, 1, x_h[1], False).then_inc(sem("down_done"), 1)
                        pe.drain().then_inc(sem("down_used"), 1)
                pe.drain().then_inc(sem("y_sums_ready"), 1)

            def sparse(l):
                pe.drain().then_inc(sem("y_sums_ready"), 1)
                pe.wait_ge(sem("y_sums_saved"), 6 * (l + 1))

                def turn_tokens(x):
                    pe.wait_ge(sem("expert_loaded", x.b), x.dmas())
                    if x.l or x.e:
                        pe.wait_ge(sem("xt_saved_a"), x.count(1))
                        pe.wait_ge(sem("xt_saved_b"), x.count(1))
                    for c in range(J):
                        last = nc.tensor.transpose(bank[c // 4][:, (c % 4) * P:(c % 4 + 1) * P],
                                                   g_x[x.b][:, c * P:(c + 1) * P], C["ident"])
                    last.then_inc(sem("xt_ready"), 1)

                def hidden(x):
                    pe.wait_ge(sem("xt_saved_a"), x.count())
                    pe.wait_ge(sem("xt_saved_b"), x.count())
                    x.loaded(pe, x.gate)
                    x.loaded(pe, x.up)
                    if x.count(2) is not None and (x.l or x.e >= 2):
                        pe.wait_ge(sem("slot_hidden"), x.count(2))
                    for o, n in ((0, x.gate), (FF, x.up)):
                        for c in range(J):
                            last = mm(bank[2 + x.b][:, o:o + FF], g_xt[x.b][:, c, :], rows(n, J, FF)[:, c, :], c == 0,
                                      c == J - 1)
                    last.then_inc(sem("gate_up_used"), 1)

                def turn_hidden(x):
                    pe.wait_ge(sem("slot_hidden"), x.count())
                    if x.l or x.e:
                        pe.wait_ge(sem("ht_saved"), x.count(1))
                    for c in range(2):
                        last = nc.tensor.transpose(bank[4][:, c * P:(c + 1) * P], g_h[x.b][:, c::2], C["ident"])
                    last.then_inc(sem("ht_ready"), 1)

                def output(x):
                    pe.wait_ge(sem("ht_saved"), x.count())
                    x.loaded(pe, x.down)
                    if x.l or x.e:
                        pe.wait_ge(sem("slots_saved_a"), x.count(1))
                        pe.wait_ge(sem("slots_saved_b"), x.count(1))
                    for half in range(2):
                        for c in range(2):
                            last = mm(bank[5 + half][:, :], g_ht[x.b][:, c, :],
                                      rows(x.down, 2, D)[:, c, 512 * half:512 * (half + 1)], c == 0, c == 1)
                    last.then_inc(sem("down_used"), 1)

                def step(x):
                    hidden(x)
                    if x.e + 1 < EXPERTS:
                        turn_tokens(after(x))
                    turn_hidden(x)
                    if x.e:
                        output(before(x))

                turn_tokens(Turn(l, 0))
                each_expert(pe, l, step)
                output(Turn(l, EXPERTS - 1))

            def experts(l):
                q0 = 2 * (EXPERTS + 1) * l
                n = first[l]["shared"]
                gate, up, dn = (rows(n, J, FF), rows(n + 1, J, FF), rows(n + 2, 2, D))
                loaded(n)
                loaded(n + 1)
                gate_up(gate, up, 0).then_inc(sem("gu_ready"), 1)
                pe.wait_ge(sem("gu_saved"), q0 + 1)
                gate_up(gate, up, 1).then_inc(sem("gu_ready"), 1)
                pe.drain().then_inc(sem("ring_released"), 1)
                loaded(n + 2)
                pe.wait_ge(sem("hid_ready"), q0 + 1)
                down(dn, 0, x_h[0], True).then_inc(sem("down_done"), 1)
                pe.wait_ge(sem("hid_ready"), q0 + 2)
                down(dn, 1, x_h[1], False).then_inc(sem("down_done"), 1)
                pe.drain().then_inc(sem("ring_released"), 1)
                by_load(pe, l, dense, sparse, DENSE_PE, SPARSE_PE)
                pe.wait_ge(sem("y_sums_saved"), 6 * (l + 1))
                pe.wait_ge(sem("y_total_ready"), l + 1)
                for k in range(6):
                    t, half = divmod(k, 2)
                    for i in range(4):
                        last = nc.tensor.transpose(bank[k][:, i * P:(i + 1) * P], x_y[:, t, 4 * half + i::J], C["ident"])
                    last.then_inc(sem("yT_ready"), 1)
                end_phase()

            for l in range(LAYERS):
                modulation(l)
                norm(2 * l + 1)
                projection(l)
                (token_shift if l % 2 == 0 else convolution)()
                end_phase()
                attend(l)
                (rwkv if l % 2 == 0 else delta)()
                output_projection(l)
                norm(2 * l + 2)
                router(l)
                experts(l)

        @block.scalar
        def _(act):
            phase = [0]
            chain = [0]

            def link(ins):
                chain[0] += 1
                ins.then_inc(sem("act_chain"), 1)
                act.wait_ge(sem("act_chain"), chain[0])

            def f(out, in_, func, **kw):
                return nc.scalar.activation(out, in_, func, **kw)

            def rsqrt(ap, scale, eps):
                link(f(ap, ap, ACT.Ln, scale=scale, bias=eps))
                return f(ap, ap, ACT.Exp, scale=-0.5)

            def end_phase():
                phase[0] += 1
                phase_end("act", act, phase[0])

            def load(out, in_, s):
                act.dma_start(out, in_).then_inc(s, 16)

            def rows_of(ap, n=P):
                return ap.unsqueeze(0).broadcast_to([n] + list(ap.shape))

            def load_params(l):
                s = sem("params_loaded")
                if l % 2 == 0:
                    load(heads(params[:, 0:512], 8), w["a_qn"][0].unsqueeze(0).unsqueeze(0).broadcast_to([P, 8, 64]), s)
                    load(heads(params[:, 512:640], 2), w["a_kn"][0].unsqueeze(0).unsqueeze(0).broadcast_to([P, 2, 64]), s)
                    load(r_mu, rows_of(w["b_mu"][0]), s)
                    for dst, name in ((r_kk, "b_kk"), (r_ka, "b_ka"), (r_lnw, "b_lnx_w"), (r_lnb, "b_lnx_b")):
                        load(dst, rows_of(w[name][0]), s)
                    load(r_rk, rows_of(w["b_rk"][0].rearrange("h d -> (h d)")), s)
                else:
                    load(conv_w, rows_of(w["c_conv"][0]), s)
                    load(heads(params[:, 4608:5120], 8), w["d_qn"][0].unsqueeze(0).unsqueeze(0).broadcast_to([P, 8, 64]), s)
                    load(heads(params[:, 5120:5632], 8), w["d_kn"][0].unsqueeze(0).unsqueeze(0).broadcast_to([P, 8, 64]), s)
                    load(params[:, 5632:5760], rows_of(w["c_onorm"][0]), s)
                    load(params[:, 5760:5888], rows_of(w["d_subln"][0]), s)
                    load(params[:, 5888:6144], rows_of(w["d_lambda"][0].rearrange("k d -> (k d)")), s)
                    load(params[:, 6144:6152], rows_of(w["c_A_log"][0].rearrange("d h -> (d h)")), s)
                    load(params[:, 6152:6160], rows_of(w["c_dt_bias"][0].rearrange("d h -> (d h)")), s)

            def norm(n):
                if n == 1:
                    act.wait_ge(sem("x_loaded"), 16)
                else:
                    act.wait_ge(sem("x_ready"), n - 1)
                f(squares, xT[:, :, :], ACT.Square).then_inc(sem("squares_ready"), 1)
                act.wait_ge(sem("sumsq_ready"), n)
                link(f(rstd[:, :], bank[1][:, 0:NTOK], ACT.Ln, scale=1.0 / D, bias=eps6))
                f(rstd[:, :], rstd[:, :], ACT.Exp, scale=-0.5).then_inc(sem("rstd_ready"), 1)

            def projection(l):
                proj, _ = proj_of(l)
                k = 0
                for a, b in (EVEN_BLOCKS if l % 2 == 0 else ODD_BLOCKS):
                    for t in range(TILES):
                        if k % 2 == 1:
                            act.wait_ge(sem("proj_ready"), 18 * l + k + 1)
                            nc.scalar.copy(*projected(l, t, a, b, bank[k % 6])).then_inc(sem("proj_saved", 1), 1)
                        k += 1
                end_phase()

            def load_cached(l):
                A = attention[l]
                s = sem("parts_loaded")
                load(A.klat[:, :, 0, :], w["keys_a"].unsqueeze(1) if A.even else w["keys_d"], s)
                load(A.vc, w["values_a"] if A.even else w["values_d"], s)
                if not A.even:
                    load(d_sl, w["state_d"], sem("state_loaded"))
                else:
                    s = sem("state_loaded")
                    load(r_lora[0:64, :].rearrange("p (d n) -> p d n", d=2), w["b_w2"][0].rearrange("d k n -> k d n"), s)
                    load(r_lora[64:128, :].rearrange("p (d n) -> p d n", d=2), w["b_a2"][0].rearrange("d k n -> k d n"), s)
                    load(r_w0.rearrange("p (d n) -> p d n", d=2), rows_of(w["b_w0"][0]), s)
                    load(r_a0.rearrange("p (d n) -> p d n", d=2), rows_of(w["b_a0"][0]), s)
                    load(r_sl, w["state_r"], s)
                    load(r_g2, w["b_g2"][0], s)

            def conv_silu():
                for t in range(TILES):
                    act.wait_ge(sem("conv_done"), t + 1)
                    f(conv_exp(t), proj1[:, t, 0:1536], ACT.Exp, scale=-1.0).then_inc(sem("conv_exp_ready"), 1)

            def attend(l):
                A = attention[l]
                for t in range(TILES):
                    act.wait_ge(sem("qk_sumsq"), TILES * l + t + 1)
                    rsqrt(A.ss[:, 16 * t:16 * t + A.nh], 1.0 / HEAD, eps6).then_inc(sem("qk_rstd"), 1)
                if not A.even:
                    act.wait_ge(sem("exp_inputs"), 1)
                    f(A.neg[:, 0:2], A.neg[:, 0:2], ACT.Exp).then_inc(sem("exp_outputs"), 1)
                act.wait_ge(sem("qk_ready"), TILES * l + 1)
                k0 = A.base + 512
                nk = 64 * (A.nh - 8)
                load(outs["k_a"] if A.even else outs["k_d"], A.proj[:, 0, k0:k0 + nk], sem("stored"))
                load(outs["v_a"] if A.even else outs["v_d"],
                     A.proj[:, 0, A.vbase:A.vbase + (128 if A.even else 512)], sem("stored"))
                for t in range(TILES):
                    act.wait_ge(sem("qkT_ready"), TILES * l + t + 1)
                    nc.scalar.copy(A.qt[:, t, :, :], bank[2 * t][:, :].rearrange("p (c n) -> p c n", c=4))\
                        .then_inc(sem("qT_saved"), 1)
                for u in range(25):
                    if u < 24:
                        kt = A.unit(u)[1]
                        act.wait_ge(sem("max_ready"), 24 * l + u + 1)
                        if u >= 2:
                            act.wait_ge(sem("pT_ready"), 24 * l + u - 1)
                        f(A.p[:, u % 2, 0:kt * P], bank[u % 2][:, 0:kt * P], ACT.Exp, bias=A.mx[:, u:u + 1],
                          accum_out=A.sums[:, u:u + 1]).then_inc(sem("p_ready"), 1)
                    if u >= 1:
                        v = u - 1
                        kt = A.unit(v)[1]
                        act.wait_ge(sem("pT_ready"), 24 * l + v + 1)
                        if v >= 2:
                            act.wait_ge(sem("o_ready"), 24 * l + v - 1)
                        nc.scalar.copy(A.pt[:, v % 2, 0:kt * P], bank[2 + v % 2][:, 0:kt * P])\
                            .then_inc(sem("pT_saved"), 1)
                if not A.even:
                    act.wait_ge(sem("head_sumsq"), 3)
                    rsqrt(stats[:, 0:12], 1.0 / P, eps6).then_inc(sem("head_rstd"), 1)
                end_phase()

            def invert(inv, n, groups=(0, 1)):
                for k in range(1, LEVELS):
                    for g in groups:
                        act.wait_ge(inv.sem("m_ready", g), 6 * n + k)
                        nc.scalar.copy(inv.m1[g], bank[g][:, :].rearrange("p (h n) -> p h n", h=4))\
                            .then_inc(inv.sem("m_saved", g), 1)

            def rwkv():
                act.wait_ge(sem("stored"), 32)
                f(proj0[:, :, XW:XW + 64], proj0[:, :, XW:XW + 64], ACT.Exp, scale=2.0)
                f(proj0[:, :, XG:XG + P], proj0[:, :, XG:XG + P], ACT.Exp, scale=-1.0).then_inc(sem("lora_exp"), 1)
                for t in range(TILES):
                    act.wait_ge(sem("lora_turned"), t + 1)
                    nc.scalar.copy(proj0[:, t, 512:768], bank[0][:, 0:2 * P]).then_inc(sem("lora_saved"), 1)
                act.wait_ge(sem("head_sumsq"), 1)
                rsqrt(stats[:, 0:24], 1.0, eps6).then_inc(sem("head_rstd"), 1)
                for u, (t, d) in enumerate(RWKV_UNITS):
                    act.wait_ge(sem("zw_sum"), u + 1)
                    f(r_sig, r_sig, ACT.Exp, scale=-1.0)
                    f(r_gate, r_gate, ACT.Exp, scale=-1.0).then_inc(sem("z_exp"), 1)
                    act.wait_ge(sem("cum_ready"), u + 1)
                    f(r_ei, bank[2][:, :], ACT.Exp, scale=-DECAY)
                    f(r_ev, bank[2][:, :], ACT.Exp, scale=DECAY)
                    f(r_ee, bank[3][:, :], ACT.Exp, scale=-DECAY)
                    f(r_ec, bank[4][:, 0:8].rearrange("p (j h) -> p j h", j=4), ACT.Exp, scale=-DECAY)\
                        .then_inc(sem("exps_ready"), 1)
                    act.wait_ge(sem("tokT_ready"), u + 1)
                    nc.scalar.copy(r_ar[:, :, 0, :], bank[0][:, :].rearrange("p (c n) -> p c n", c=4))
                    nc.scalar.copy(r_ar[:, :, 1, :], bank[1][:, :].rearrange("p (c n) -> p c n", c=4))\
                        .then_inc(sem("arT_saved"), 1)
                    act.wait_ge(sem("read_ready"), u + 1)
                    for g in range(2):
                        last = nc.scalar.copy(r_rs[:, g::2, :], heads(bank[6 + g][:, 0:256], 4))
                    last.then_inc(sem("read_saved"), 1)
                    invert(r_inverse, u)
                    act.wait_ge(sem("u_ready"), u + 1)
                    for g in range(2):
                        last = nc.scalar.copy(r_us[:, g::2, :], heads(bank[g][:, 0:256], 4))
                    last.then_inc(sem("u_saved"), 1)
                    if u == 2:
                        load(outs["state_r"], r_sc, sem("stored"))
                act.wait_ge(sem("head_sumsq"), 2)
                rsqrt(stats[:, 24:48], 1.0 / HEAD, eps_ln).then_inc(sem("head_rstd"), 1)
                act.wait_ge(sem("stored"), 48)
                end_phase()

            def delta():
                act.wait_ge(sem("head_sumsq"), 4)
                rsqrt(stats[:, 0:24], 1.0, eps6).then_inc(sem("head_rstd"), 1)
                act.wait_ge(sem("exp_inputs"), 2)
                link(f(d_tmp, d_tmp, ACT.Exp))
                f(d_tmp, d_tmp, ACT.Ln, bias=one_col)
                f(params[:, 6144:6152], params[:, 6144:6152], ACT.Exp)
                f(d_beta, proj1[:, :, CAB + 8:CAB + 16].rearrange("p t (d h) -> p t d h", d=2), ACT.Exp, scale=-1.0)\
                    .then_inc(sem("exp_outputs"), 1)
                for t in range(TILES):
                    act.wait_ge(sem("ckT_ready"), t + 1)
                    nc.scalar.copy(d_kt[:, t, :, :], heads(bank[2 * t][:, :], 4)).then_inc(sem("ckT_saved"), 1)
                act.wait_ge(sem("gsum_ready"), 1)
                for i, dst in enumerate((d_eg, d_es, d_et)):
                    last = f(dst, bank[6][:, 24 * i:24 * i + 24].rearrange("p (t d h) -> p t d h", t=TILES, d=2), ACT.Exp)
                last.then_inc(sem("decay_exps"), 1)
                for n, step in enumerate(DELTA_STEPS):
                    for g in range(2):
                        act.wait_ge(sem("dneg_ready"), 2 * n + g + 1)
                        f(d_off[g], d_off[g], ACT.Exp, scale=-1.0).then_inc(sem("dexp_ready"), 1)
                    invert(d_inverse, len(RWKV_UNITS) + n)
                    for g in range(2):
                        act.wait_ge(sem("vn_ready"), 2 * n + g + 1)
                        nc.scalar.copy(d_vn[g], heads(bank[g][:, :], 4)).then_inc(sem("vn_saved"), 1)
                    if n == 1:
                        load(outs["state_d"], d_sc, sem("stored"))
                act.wait_ge(sem("head_sumsq"), 5)
                rsqrt(stats[:, 12:24], 1.0 / P, eps6)
                f(silu_z, proj1[:, :, CZ:CZ + 512], ACT.Exp, scale=-1.0).then_inc(sem("head_rstd"), 1)
                act.wait_ge(sem("stored"), 96)
                end_phase()

            def output_projection(l):
                act.wait_ge(sem("mixed_ready"), l + 1)
                for k in (0, 2, 4):
                    t, half = divmod(k, 2)
                    act.wait_ge(sem("mixedT_ready"), 6 * l + k + 1)
                    nc.scalar.copy(hT[:, 4 * half:4 * half + 4, t * P:(t + 1) * P], heads(bank[k][:, :], 4))\
                        .then_inc(sem("mixedT_saved", 0), 1)
                end_phase()

            def router(l):
                for k in (0, 2, 4):
                    act.wait_ge(sem("rows_ready"), 6 * l + k + 1)
                    nc.scalar.copy(x_y[:, k // 2, 0:512], bank[row_banks[k]][:, :]).then_inc(sem("rows_saved_a"), 1)
                act.wait_ge(sem("rows_saved_a"), 3 * (l + 1))
                act.wait_ge(sem("rows_saved_b"), 3 * (l + 1))
                load(x_rows[l].rearrange("(t p) d -> p t d", t=TILES), x_y, sem("rows_stored"))
                act.wait_ge(sem("logits_ready"), l + 1)
                f(m_sc, heads(bank[2][:, 0:192], 3), ACT.Exp, scale=-1.0).then_inc(sem("logit_exps"), 1)
                act.wait_ge(sem("routingT_saved"), l + 1)
                load(wt_dram[l], m_wt[0:EXPERTS, :], sem("routing_stored"))
                end_phase()

            def silu(half, q, l, i=None):
                v = lambda n: n if i is None else i * 4 + n
                act.wait_ge(sem("gu_ready"), v(q + 1))
                if i is not None or l:
                    act.wait_ge(sem("gu_saved"), v(q - 1))
                f(x_e[half], bank[6][:, 0:NTOK], ACT.Silu).then_inc(sem("gate_silu"), 1)

            def save_sums(l):
                act.wait_ge(sem("y_sums_ready"), l + 1)
                for k in (0, 2, 4):
                    nc.scalar.copy(x_y[:, k // 2, 0:512], bank[k][:, :]).then_inc(sem("y_sums_saved"), 1)

            def dense(l):
                q0 = 2 * (EXPERTS + 1) * l + 2
                with act.Fori(0, EXPERTS // 2) as i:
                    for e in range(2):
                        for half in range(2):
                            silu(half, q0 + 2 * e + half, l, i)
                save_sums(l)

            def sparse(l):
                save_sums(l)

                def tokens(x):
                    act.wait_ge(sem("xt_ready"), x.count())
                    if x.l or x.e >= 2:
                        act.wait_ge(sem("gate_up_used"), x.count(2))
                    nc.scalar.copy(g_xt[x.b][:, 0:4, :], heads(bank[0][:, :], 4)).then_inc(sem("xt_saved_a"), 1)

                def step(x):
                    act.wait_ge(sem("gate_up_used"), x.count())
                    if x.l or x.e >= 2:
                        act.wait_ge(sem("slot_hidden"), x.count(2))
                    f(g_s[x.b], bank[2 + x.b][:, 0:FF], ACT.Silu).then_inc(sem("slot_silu"), 1)
                    if x.e + 1 < EXPERTS:
                        tokens(after(x))
                    act.wait_ge(sem("ht_ready"), x.count())
                    if x.l or x.e >= 2:
                        act.wait_ge(sem("down_used"), x.count(2))
                    nc.scalar.copy(g_ht[x.b], heads(bank[4][:, 0:2 * P], 2)).then_inc(sem("ht_saved"), 1)
                    if x.e:
                        save(before(x))

                def save(x):
                    act.wait_ge(sem("down_used"), x.count())
                    if x.e >= 2:
                        act.wait_ge(sem("scattered", l, x.b), x.scatters_before())
                    nc.scalar.copy(g_y[x.b][:, 0:512], bank[5][:, :]).then_inc(sem("slots_saved_a"), 1)

                tokens(Turn(l, 0))
                each_expert(act, l, step)
                save(Turn(l, EXPERTS - 1))

            def experts(l):
                nc.scalar.preload_act_table(ACT.Silu)
                act.wait_ge(sem("rows_stored"), 16 * (l + 1))
                q0 = 2 * (EXPERTS + 1) * l
                silu(0, q0, l)
                silu(1, q0 + 1, l)
                by_load(act, l, dense, sparse, DENSE_ACT, SPARSE_ACT)
                nc.scalar.preload_act_table_set("natural_log_exp_and_others")
                end_phase()

            nc.scalar.preload_act_table_set("natural_log_exp_and_others")
            for dst, name in ((consts[:, :], "consts"), (cond[:, :, :], "cond"), (mod_b[:, :, :, :], "mod_b"),
                              (gains[:, :, :, :], "gains"), (rope[:, :, :, :], "rope")):
                load(dst, w[name], sem("start_loaded"))
            load_params(0)
            act.wait_ge(sem("start_loaded"), 80)
            f(cond_exp[:, :, :], cond[:, :, :], ACT.Exp, scale=-1.0).then_inc(sem("cond_exps"), 1)
            for l in range(LAYERS):
                end_phase()
                norm(2 * l + 1)
                projection(l)
                if l % 2:
                    conv_silu()
                end_phase()
                load_cached(l)
                attend(l)
                (rwkv if l % 2 == 0 else delta)()
                if l + 1 < LAYERS:
                    load_params(l + 1)
                load(m_router, w["router_w"][l].rearrange("(p c) e -> p c e", c=J), sem("parts_loaded"))
                load(m_bias_buf, rows_of(w["router_bias"][l]), sem("parts_loaded"))
                output_projection(l)
                norm(2 * l + 2)
                router(l)
                experts(l)

        @block.vector
        def _(dve):
            phase = [0]
            chain = [0]

            def link(ins):
                chain[0] += 1
                ins.then_inc(sem("dve_chain"), 1)
                dve.wait_ge(sem("dve_chain"), chain[0])

            def tt(out, a, b, op):
                return nc.vector.tensor_tensor(out, a, b, op)

            def ts(out, a, s1, op0, s2=None, op1=None):
                if op1 is None:
                    return nc.vector.tensor_scalar(out, a, s1, None, op0)
                return nc.vector.tensor_scalar(out, a, s1, s2, op0, op1)

            def stt(out, a, s, b, op0, op1):
                return nc.vector.scalar_tensor_tensor(out=out, in0=a, scalar=s, in1=b, op0=op0, op1=op1)

            def total(out, a, op=ALU.add, **kw):
                return nc.vector.tensor_reduce(out, a, AX.X, op, **kw)

            def copy(out, a):
                return nc.vector.tensor_copy(out, a)

            def recip(ap):
                return nc.vector.reciprocal(ap, ap)

            def sigmoid_of(ap):
                link(ts(ap, ap, 1.0, ALU.add))
                return recip(ap)

            def end_phase():
                phase[0] += 1
                phase_end("dve", dve, phase[0])

            def modulation(l):
                if l == 0:
                    dve.wait_ge(sem("cond_exps"), 1)
                    link(sigmoid_of(cond_exp[:, :, :]))
                    tt(cond[:, :, :], cond[:, :, :], cond_exp[:, :, :], ALU.mult).then_inc(sem("cond_ready"), 1)
                end_phase()
                link(tt(mods[:, :, :, :].rearrange("p s j c -> p (s j) c"),
                        bank[0][:, 0:96].rearrange("p (k c) -> p k c", c=2),
                        along(mod_b[:, l, :, :].rearrange("p s j -> p (s j)"), 2), ALU.add))
                for which, s in ((0, 1), (1, 4)):
                    link(stt(mods[:, s, :, :], mods[:, s, :, :], 1.0, along(gains[:, l, which, :], 2), ALU.add, ALU.mult))

            def norm(n):
                l, which = divmod(n - 1, 2)
                if n == 1:
                    dve.wait_ge(sem("x_loaded"), 16)
                dve.wait_ge(sem("rstd_ready"), n)
                link(tt(squares, xT[:, :, :], rstd[:, :].unsqueeze(1).broadcast_to([P, J, NTOK]), ALU.mult))
                for j in range(J):
                    for c, a, b in ((0, 0, P), (1, P, NTOK)):
                        last = ts(hT[:, j, a:b], squares[:, j, a:b], mods[:, 3 * which + 1, j, c:c + 1], ALU.mult,
                                  mods[:, 3 * which, j, c:c + 1], ALU.add)
                last.then_inc(sem("h_ready"), 1)

            def projection(l):
                proj, _ = proj_of(l)
                k = 0
                for a, b in (EVEN_BLOCKS if l % 2 == 0 else ODD_BLOCKS):
                    for t in range(TILES):
                        if k % 2 == 0:
                            dve.wait_ge(sem("proj_ready"), 18 * l + k + 1)
                            copy(*projected(l, t, a, b, bank[k % 6])).then_inc(sem("proj_saved", 0), 1)
                        k += 1
                end_phase()
                dve.wait_ge(sem("params_loaded"), 128 * l + 16 * 8)

            def token_shift():
                tmp = attention[0].t1[:, 0:448]
                for b in range(4):
                    dve.wait_ge(sem("near_ready"), b + 1)
                    for t in range(TILES):
                        x = proj0[:, t, XB + 448 * b:XB + 448 * (b + 1)]
                        link(stt(tmp, bank[3 * (b % 2) + t][:, 0:448], 0.5, x, ALU.mult, ALU.subtract))
                        link(tt(tmp, tmp, r_mu[:, 448 * b:448 * (b + 1)], ALU.mult))
                        link(tt(x, x, tmp, ALU.add))
                    dve.drain().then_inc(sem("near_saved"), 1)

            def convolution():
                tmp, tmp2 = conv_tmp[:, 0:512], conv_tmp[:, 512:1024]
                for b in range(3):
                    cols = slice(512 * b, 512 * (b + 1))
                    dve.wait_ge(sem("near_ready"), 4 + b + 1)
                    for t in range(TILES):
                        x = proj1[:, t, cols]
                        tt(tmp, bank[t][:, :], conv_w[:, 0, cols], ALU.mult)
                        tt(tmp2, bank[3 + t][:, :], conv_w[:, 2, cols], ALU.mult)
                        link(tt(x, x, conv_w[:, 1, cols], ALU.mult))
                        link(tt(x, x, tmp, ALU.add))
                        link(tt(x, x, tmp2, ALU.add))
                    dve.drain().then_inc(sem("near_saved"), 1)
                for t in range(TILES):
                    dve.drain().then_inc(sem("conv_done"), 1)
                for t in range(TILES):
                    x = proj1[:, t, 0:1536]
                    dve.wait_ge(sem("conv_exp_ready"), t + 1)
                    link(sigmoid_of(conv_exp(t)))
                    link(tt(x, x, conv_exp(t), ALU.mult))

            def attend(l):
                A = attention[l]
                n = 64 * A.nh
                link(ts(A.gain[:, 0:512], A.gain[:, 0:512], HEAD ** -0.5, ALU.mult))
                for t in range(TILES):
                    link(tt(A.t1[:, 0:n], A.qk(t), A.qk(t), ALU.mult))
                    total(A.ss[:, 16 * t:16 * t + A.nh], heads(A.t1[:, 0:n], A.nh)).then_inc(sem("qk_sumsq"), 1)
                    dve.wait_ge(sem("qk_sumsq"), TILES * l + t + 1)
                if not A.even:
                    lam = params[:, 5888:6144].rearrange("p (k d) -> p k d", k=4)
                    link(tt(heads(A.t1[:, 0:128], 2), lam[:, 0::2, :], lam[:, 1::2, :], ALU.mult))
                    total(A.neg[:, 0:2], heads(A.t1[:, 0:128], 2)).then_inc(sem("exp_inputs"), 1)
                    dve.wait_ge(sem("exp_outputs"), 1)
                    link(stt(A.neg[:, 2:3], A.neg[:, 1:2], LAM_INIT, A.neg[:, 0:1], ALU.subtract, ALU.subtract))
                for t in range(TILES):
                    qk = heads(A.qk(t), A.nh)
                    dve.wait_ge(sem("qk_rstd"), TILES * l + t + 1)
                    link(tt(qk, qk, along(A.ss[:, 16 * t:16 * t + A.nh], 64), ALU.mult))
                    scaled = tt(A.qk(t), A.qk(t), A.gain, ALU.mult)
                    if t == 0:
                        scaled.then_inc(sem("qk_ready"), 1)
                        continue
                    link(scaled)
                    cos, sin = (rope[:, t - 1, i, :] for i in range(2))
                    wide = lambda ap: ap.unsqueeze(1).broadcast_to([P, A.nh, ap.shape[-1]])
                    t1, t2 = heads(A.t1[:, 0:n], A.nh), heads(A.t2[:, 0:n], A.nh)
                    tt(t2[:, :, 0::2], qk[:, :, 1::2], wide(sin[:, 0::2]), ALU.mult)
                    tt(t2[:, :, 1::2], qk[:, :, 0::2], wide(sin[:, 1::2]), ALU.mult)
                    link(tt(t1, qk, wide(cos), ALU.mult))
                    tt(qk, t1, t2, ALU.add).then_inc(sem("qk_ready"), 1)
                    dve.wait_ge(sem("qk_ready"), TILES * l + t + 1)
                for t in range(TILES):
                    dve.wait_ge(sem("qkT_ready"), TILES * l + t + 1)
                    dst = A.kctx if t == 0 else A.klat[:, :, t, :]
                    copy(dst, heads(bank[2 * t + 1][:, 0:A.kc * P], A.kc)).then_inc(sem("kT_saved"), 1)

                def normalise(g):
                    n = A.per_bank
                    units = slice(n * g, n * (g + 1))
                    dve.wait_ge(sem("o_ready"), 24 * l + n * (g + 1))
                    link(nc.vector.reciprocal(A.rinv[:, units], A.sums[:, units]))
                    src = heads(bank[4 + g % 2][:, :], n)
                    if A.even:
                        tt(heads(mixed[:, g, 0:512], 8), src, along(A.rinv[:, units], 64), ALU.mult)\
                            .then_inc(sem("o_saved"), 1)
                        return
                    t, half = divmod(g, 2)
                    r2 = A.rinv[:, n * g + 1:n * (g + 1):2]
                    link(ts(r2, r2, A.neg[:, 2:3], ALU.mult))
                    t1, t2 = heads(A.t1[:, 0:256], 2), heads(A.t2[:, 0:256], 2)
                    tt(t1, src[:, 0::2, :], along(A.rinv[:, n * g:n * (g + 1):2], P), ALU.mult)
                    link(tt(t2, src[:, 1::2, :], along(r2, P), ALU.mult))
                    out = heads(mixed[:, t, 512 + 256 * half:768 + 256 * half], 2)
                    tt(out, t1, t2, ALU.add).then_inc(sem("o_saved"), 1)
                    dve.wait_ge(sem("o_saved"), 3 * l + g + 1)

                n_groups = 24 // A.per_bank
                done = 0
                for u in range(24):
                    kt = A.unit(u)[1]
                    dve.wait_ge(sem("s_ready"), 24 * l + u + 1)
                    total(A.mx[:, u:u + 1], bank[u % 2][:, 0:kt * P], ALU.max, negate=True)\
                        .then_inc(sem("max_ready"), 1)
                    if done < n_groups and u >= A.per_bank * (done + 1) + 2:
                        normalise(done)
                        done += 1
                while done < n_groups:
                    normalise(done)
                    done += 1
                if not A.even:
                    od = mixed[:, :, 512:1024].rearrange("p t (h d) -> p t h d", h=4)
                    tmp = arena[:, po1:po1 + 1536].rearrange("p (t h d) -> p t h d", t=TILES, h=4)
                    st = stats[:, 0:12].rearrange("p (t h) -> p t h", t=TILES)
                    link(tt(tmp, od, od, ALU.mult))
                    total(st, tmp).then_inc(sem("head_sumsq"), 1)
                    dve.wait_ge(sem("head_rstd"), 3)
                    link(ts(st, st, 1.0 - LAM_INIT, ALU.mult))
                    link(tt(od, od, along(st, P), ALU.mult))
                    sub = params[:, 5760:5888].unsqueeze(1).unsqueeze(1).broadcast_to([P, TILES, 4, P])
                    link(tt(od, od, sub, ALU.mult))
                end_phase()

            def join(inv, n, groups=(0, 1)):
                ident = C["ident"].unsqueeze(1).broadcast_to([P, 4, P])
                for g in groups:
                    dve.wait_ge(inv.sem("off_ready", g), 7 * n + 1)
                    tt(inv.tt[g], inv.off[g], ident, ALU.add)
                for g in groups:
                    dve.wait_ge(inv.sem("turned", g), n + 1)
                    tt(inv.t[g], heads(bank[2 + g][:, :], 4), ident, ALU.add).then_inc(inv.sem("t_ready", g), 1)
                for k in range(1, LEVELS):
                    for g in groups:
                        dve.wait_ge(inv.sem("join_ready", g), 6 * n + k)
                        dve.wait_ge(inv.sem("t_ready", g), 7 * n + k)
                        if k < LEVELS - 1:
                            tt(inv.t[g], inv.t[g], heads(bank[2 + g][:, :], 4), ALU.add)
                        tt(inv.tt[g], inv.tt[g], heads(bank[4 + g][:, :], 4), ALU.add)\
                            .then_inc(inv.sem("t_ready", g), 1)

            def rwkv():
                dve.wait_ge(sem("lora_exp"), 1)
                th, sg = proj0[:, :, XW:XW + 64], proj0[:, :, XG:XG + P]
                ts(sg, sg, 1.0, ALU.add)
                link(ts(th, th, 1.0, ALU.add))
                recip(sg)
                link(recip(th))
                ts(th, th, -2.0, ALU.mult, 1.0, ALU.add).then_inc(sem("lora_ready"), 1)
                wide = lambda ap: ap.unsqueeze(1).broadcast_to([P, TILES, 512])
                kk = proj0[:, :, 0:512]
                tmp = arena[:, po0:po0 + 1536].rearrange("p (t n) -> p t n", t=TILES)
                h4 = lambda ap: ap.rearrange("p t (h d) -> p t h d", h=8)
                st = stats[:, 0:24].rearrange("p (t h) -> p t h", t=TILES)
                link(tt(kk, proj0[:, :, XK:XK + 512], wide(r_kk), ALU.mult))
                link(tt(tmp, kk, kk, ALU.mult))
                total(st, h4(tmp)).then_inc(sem("head_sumsq"), 1)
                dve.wait_ge(sem("head_rstd"), 1)
                link(tt(h4(kk), h4(kk), along(st, 64), ALU.mult))
                dve.wait_ge(sem("state_loaded"), 16 * 6)
                for u, (t, d) in enumerate(RWKV_UNITS):
                    dve.wait_ge(sem("za_ready"), u + 1)
                    tt(r_sig, bank[0][:, :], r_w0[:, 512 * d:512 * (d + 1)], ALU.add)
                    tt(r_gate, bank[1][:, :], r_a0[:, 512 * d:512 * (d + 1)], ALU.add).then_inc(sem("zw_sum"), 1)
                    dve.wait_ge(sem("z_exp"), u + 1)
                    ts(r_gate, r_gate, 1.0, ALU.add)
                    link(ts(r_sig, r_sig, 1.0, ALU.add))
                    recip(r_sig).then_inc(sem("sig_ready"), 1)
                    link(recip(r_gate))
                    tt_k = proj0[:, t, XK:XK + 512]
                    stt(r_tokb, kk_of(t), -1.0, r_gate, ALU.mult, ALU.mult)
                    link(stt(r_tokk, r_gate, 1.0, r_ka, ALU.subtract, ALU.mult))
                    link(stt(r_tokk, r_tokk, 1.0, tt_k, ALU.add, ALU.mult))
                    dve.wait_ge(sem("exps_ready"), u + 1)
                    if t:
                        tt(r_sw, r_sl[:, d, :, :], along(r_ec[:, :, d], 64), ALU.mult)
                    tt(r_toka, kk_of(t), r_ee, ALU.mult)
                    tt(r_tokr, proj0[:, t, XR:XR + 512], r_ei, ALU.mult)
                    tt(r_tokb, r_tokb, r_ev, ALU.mult)
                    tt(r_tokk, r_tokk, r_ev, ALU.mult).then_inc(sem("tok_ready"), 1)
                    dve.wait_ge(sem("tokT_ready"), u + 1)
                    copy(r_bt, heads(bank[2][:, :], 4))
                    copy(r_kt, heads(bank[3][:, :], 4)).then_inc(sem("bkT_saved"), 1)
                    mask = masks[d].unsqueeze(1).broadcast_to([P, 2, 256])
                    for g in range(2):
                        dve.wait_ge(sem("gram_ready"), 2 * u + g + 1)
                        two = lambda ap, i: ap[:, 2 * i:2 * i + 2, :, :].rearrange("p c k n -> p c (k n)")
                        for i in range(2):
                            last = tt(two(r_nr[g], i), heads(bank[4 + i][:, :], 2), mask, ALU.mult)
                        last.then_inc(r_inverse.sem("nt_ready", g), 1)
                        for i in range(2):
                            last = tt(two(r_ak[g], i), heads(bank[6 + i][:, :], 2), mask, ALU.mult)
                        last.then_inc(sem("gram_saved"), 1)
                    join(r_inverse, u)
                    dve.wait_ge(sem("y_unit_ready"), u + 1)
                    first_visit = u in (0, 2, 3)
                    for g in range(2):
                        y = heads(yacc_of(t), 8)[:, g::2, :]
                        src = heads(bank[2 + g][:, 0:256], 4)
                        last = copy(y, src) if first_visit else tt(y, y, src, ALU.add)
                        if u in RWKV_KEEPS:
                            p = slice(64 * g, 64 * g + 64)
                            src = heads(bank[4 + g][p, 0:256], 4)
                            end = along(r_ec[p, :, 1 - d], 64)
                            if t:
                                link(tt(r_sw[p, :, :], r_sw[p, :, :], src, ALU.add))
                                last = tt(r_sl[p, d, :, :], r_sw[p, :, :], end, ALU.mult)
                            else:
                                last = tt(r_sc[p, d, :, :], src, end, ALU.mult)
                    last.then_inc(sem("unit_saved"), 1)
                    dve.wait_ge(sem("unit_saved"), u + 1)
                y = mixed[:, :, 512:1024]
                mean = stats[:, 0:24].rearrange("p (t h) -> p t h", t=TILES)
                var = stats[:, 24:48].rearrange("p (t h) -> p t h", t=TILES)
                link(total(mean, h4(y)))
                link(ts(mean, mean, 1.0 / HEAD, ALU.mult))
                link(tt(h4(y), h4(y), along(mean, 64), ALU.subtract))
                link(tt(tmp, y, y, ALU.mult))
                total(var, h4(tmp)).then_inc(sem("head_sumsq"), 1)
                dve.wait_ge(sem("head_sumsq"), 2)
                link(tt(tmp, proj0[:, :, XR:XR + 512], proj0[:, :, XK:XK + 512], ALU.mult))
                link(tt(tmp, tmp, wide(r_rk), ALU.mult))
                link(total(mean, h4(tmp)))
                link(tt(h4(tmp), h4(proj0[:, :, XV:XV + 512]), along(mean, 64), ALU.mult))
                dve.wait_ge(sem("head_rstd"), 2)
                link(tt(h4(y), h4(y), along(var, 64), ALU.mult))
                link(tt(y, y, wide(r_lnw), ALU.mult))
                link(tt(y, y, wide(r_lnb), ALU.add))
                link(tt(y, y, tmp, ALU.add))
                dve.wait_ge(sem("gate_ready"), 1)
                for t in range(TILES):
                    last = tt(mixed[:, t, 512:1024], mixed[:, t, 512:1024], bank[t][:, :], ALU.mult)
                last.then_inc(sem("mixed_ready"), 1)
                end_phase()

            def delta():
                h8 = lambda ap: ap.rearrange("p t (h d) -> p t h d", h=8)
                qk = proj1[:, :, 0:1024]
                tmp = arena[:, po1:po1 + 3072].rearrange("p (t n) -> p t n", t=TILES)
                st = stats[:, 0:24].rearrange("p (t h) -> p t h", t=TILES)
                link(tt(tmp, qk, qk, ALU.mult))
                total(st, h8(tmp)).then_inc(sem("head_sumsq"), 1)
                td = lambda ap: ap.rearrange("p (d h) -> p d h", d=2).unsqueeze(1).broadcast_to([P, TILES, 2, 4])
                flat = lambda ap: ap.rearrange("p t d h -> p (t d h)")
                a_in = proj1[:, :, CAB:CAB + 8].rearrange("p t (d h) -> p t d h", d=2)
                link(tt(d_g, a_in, td(params[:, 6152:6160]), ALU.add))
                stt(flat(d_tmp), flat(d_g), -1.0, flat(d_g), ALU.mult, ALU.min).then_inc(sem("exp_inputs"), 1)
                dve.wait_ge(sem("exp_inputs"), 2)
                link(ts(d_g, d_g, 0.0, ALU.max))
                dve.wait_ge(sem("head_rstd"), 4)
                link(ts(st[:, :, 0:4], st[:, :, 0:4], P ** -0.5, ALU.mult))
                tt(h8(qk), h8(qk), along(st, P), ALU.mult).then_inc(sem("ck_ready"), 1)
                dve.wait_ge(sem("exp_outputs"), 2)
                link(tt(d_g, d_g, d_tmp, ALU.add))
                link(tt(d_g, d_g, td(params[:, 6144:6152]), ALU.mult))
                ts(d_g, d_g, -1.0, ALU.mult).then_inc(sem("g_ready"), 1)
                link(sigmoid_of(d_beta))
                link(ts(d_neg, d_beta, -1.0, ALU.mult))
                for t in range(TILES):
                    dve.wait_ge(sem("ckT_ready"), t + 1)
                    copy(d_qt[:, t, :, :], heads(bank[2 * t + 1][:, :], 4)).then_inc(sem("cqT_saved"), 1)
                dve.wait_ge(sem("gsum_ready"), 1)
                dve.wait_ge(sem("decay_exps"), 1)
                copy(d_gc, bank[6][:, 0:24].rearrange("p (t d h) -> p t d h", t=TILES, d=2))
                dve.drain().then_inc(sem("decay_cols_ready"), 1)
                dve.wait_ge(sem("decay_cols_ready"), 1)
                dve.wait_ge(sem("g_ready"), 1)
                dve.wait_ge(sem("ck_ready"), 1)
                dve.wait_ge(sem("state_loaded"), 16 * 7)
                for n, step in enumerate(DELTA_STEPS):
                    for g, (t, d) in enumerate(step):
                        for h in range(4):
                            last = ts(d_t[g][:, h, :], C[f"incl{d}"], d_g[:, t, d, h:h + 1], ALU.mult)
                        last.then_inc(sem("gi_ready"), 1)
                    for g, (t, d) in enumerate(step):
                        dve.wait_ge(sem("dgram_ready"), 2 * n + g + 1)
                        for h in range(4):
                            last = ts(d_off[g][:, h, :], bank[g][:, h * P:(h + 1) * P], d_gc[:, t, d, h:h + 1],
                                      ALU.subtract, 0.0, ALU.max)
                        last.then_inc(sem("dneg_ready"), 1)
                    for g, (t, d) in enumerate(step):
                        strict, incl = (masks[1 - d][:, 128 * i:128 * (i + 1)].unsqueeze(1).broadcast_to([P, 4, P])
                                        for i in range(2))
                        dve.wait_ge(sem("dexp_ready"), 2 * n + g + 1)
                        tt(d_m1[g], d_off[g], strict, ALU.mult)
                        link(tt(d_tt[g], d_off[g], incl, ALU.mult))
                        tt(d_tt[g], d_tt[g], heads(bank[4 + g][:, :], 4), ALU.mult)
                        link(tt(d_m1[g], d_m1[g], heads(bank[2 + g][:, :], 4), ALU.mult))
                        tt(d_m1[g], d_m1[g], along(d_neg[:, t, d, :], P), ALU.mult).then_inc(sem("na_ready"), 1)
                    for g, (t, d) in enumerate(step):
                        dve.wait_ge(sem("naT_ready"), 2 * n + g + 1)
                        copy(d_n[g], heads(bank[g][:, :], 4)).then_inc(d_inverse.sem("nt_ready", g), 1)
                        copy(d_at[g], heads(bank[2 + g][:, :], 4)).then_inc(sem("naT_saved"), 1)
                    for g, (t, d) in enumerate(step):
                        v = heads(proj1[:, t, CV:CV + 512], 4)
                        k = heads(proj1[:, t, CK:CK + 512], 4)
                        beta = along(d_beta[:, t, d, :], P)
                        tt(d_kg[g], k, along(d_es[:, t, d, :], P), ALU.mult)
                        if n:
                            dve.wait_ge(sem("ks_ready"), n)
                            link(tt(d_rs[g], heads(bank[6 + g][:, :], 4), along(d_eg[:, t, d, :], P), ALU.mult))
                            link(tt(d_rs[g], v, d_rs[g], ALU.subtract))
                            tt(d_rs[g], d_rs[g], beta, ALU.mult).then_inc(sem("rs_ready"), 1)
                        else:
                            tt(d_rs[g], v, beta, ALU.mult).then_inc(sem("rs_ready"), 1)
                    join(d_inverse, len(RWKV_UNITS) + n)
                    for g, (t, d) in enumerate(step):
                        dve.wait_ge(sem("od_ready"), 2 * n + g + 1)
                        o = heads(mixed[:, t, 0:512], 4)
                        src = heads(bank[2 + g][:, :], 4)
                        first_visit = (n, g) in ((0, 0), (1, 0), (1, 1))
                        if n:
                            link(tt(d_rs[g], heads(bank[6 + g][:, :], 4), along(d_eg[:, t, d, :], P), ALU.mult))
                            link(tt(d_rs[g], d_rs[g], src, ALU.add))
                            src = d_rs[g]
                        link(copy(o, src) if first_visit else tt(o, o, src, ALU.add))
                        if n == 0:
                            link(copy(d_sc[:, d, :, :], heads(bank[4 + g][:, :], 4)))
                        if n == 1:
                            s = d_sl[:, d, :, :]
                            link(tt(s, s, along(d_et[:, t, d, :], P), ALU.mult))
                            link(tt(s, s, heads(bank[4 + g][:, :], 4), ALU.add))
                        dve.drain().then_inc(sem("step_saved"), 1)
                oc = mixed[:, :, 0:512].rearrange("p t (h d) -> p t h d", h=4)
                tmp = arena[:, po1:po1 + 1536].rearrange("p (t h d) -> p t h d", t=TILES, h=4)
                st = stats[:, 12:24].rearrange("p (t h) -> p t h", t=TILES)
                link(tt(tmp, oc, oc, ALU.mult))
                total(st, tmp).then_inc(sem("head_sumsq"), 1)
                dve.wait_ge(sem("head_rstd"), 5)
                link(tt(oc, oc, along(st, P), ALU.mult))
                link(tt(oc, oc, params[:, 5632:5760].unsqueeze(1).unsqueeze(1).broadcast_to([P, TILES, 4, P]), ALU.mult))
                link(sigmoid_of(silu_z))
                link(tt(silu_z, silu_z, proj1[:, :, CZ:CZ + 512], ALU.mult))
                tt(mixed[:, :, 0:512], mixed[:, :, 0:512], silu_z, ALU.mult).then_inc(sem("mixed_ready"), 1)
                end_phase()

            def output_projection(l):
                for k in (1, 3, 5):
                    t, half = divmod(k, 2)
                    dve.wait_ge(sem("mixedT_ready"), 6 * l + k + 1)
                    copy(hT[:, 4 * half:4 * half + 4, t * P:(t + 1) * P], heads(bank[k][:, :], 4))\
                        .then_inc(sem("mixedT_saved", 1), 1)
                for j in range(J):
                    dve.wait_ge(sem("out_ready"), J * l + j + 1)
                    for c, a, b in ((0, 0, P), (1, P, NTOK)):
                        last = stt(xT[:, j, a:b], bank[j][:, a:b], mods[:, 2, j, c:c + 1], xT[:, j, a:b], ALU.mult,
                                   ALU.add)
                last.then_inc(sem("x_ready"), 1)
                dve.wait_ge(sem("x_ready"), 2 * l + 1)
                end_phase()

            def router(l):
                for k in (1, 3, 5):
                    dve.wait_ge(sem("rows_ready"), 6 * l + k + 1)
                    copy(x_y[:, k // 2, 512:1024], bank[row_banks[k]][:, :]).then_inc(sem("rows_saved_b"), 1)
                dve.wait_ge(sem("logit_exps"), l + 1)
                dve.wait_ge(sem("parts_loaded"), 64 * l + 64)
                link(sigmoid_of(m_sc))
                link(tt(m_bi, m_sc, m_bias, ALU.add))
                top = m_t0.rearrange("p t e -> p (t e)").rearrange("p (k e) -> p k e", e=8)
                bi = m_bi.rearrange("p t e -> p (t e)").rearrange("p (k e) -> p k e", e=8)
                for k in range(TILES * GROUPS):
                    last = nc.vector.max(top[:, k, :], bi[:, k, :])
                link(last)
                gs, sel, pen = (m_small[:, 24 * i:24 * i + 24] for i in range(3))
                link(tt(gs, top[:, :, 0], top[:, :, 1], ALU.add))
                g3 = heads(gs, TILES)
                gj = g3.unsqueeze(2).broadcast_to([P, TILES, GROUPS, GROUPS])
                gi = along(g3, GROUPS)
                above, equal = (a.rearrange("p (t i j) -> p t i j", t=TILES, i=GROUPS) for a in m_rank)
                tt(above, gj, gi, ALU.is_gt)
                link(tt(equal, gj, gi, ALU.is_equal))
                link(tt(equal, equal, lower_index.unsqueeze(1).broadcast_to([P, TILES, GROUPS, GROUPS]), ALU.mult))
                link(tt(above, above, equal, ALU.add))
                link(total(heads(sel, TILES), above))
                link(ts(sel, sel, float(TOP_GROUPS), ALU.is_lt))
                link(ts(pen, sel, 1.0, ALU.subtract, 1e30, ALU.mult))
                mk = m_mk.rearrange("p t e -> p (t e)").rearrange("p (k e) -> p k e", e=8)
                link(tt(mk, bi, along(sel, 8), ALU.mult))
                link(tt(mk, mk, along(pen, 8), ALU.add))
                best = m_small[:, 72:96].rearrange("p (t k) -> p t k", t=TILES)
                for t in range(TILES):
                    last = nc.vector.max(best[:, t, :], m_mk[:, t, :])
                link(last)
                def scan(t):
                    return nc.vector.tensor_tensor_scan(m_cum[:, t, :], C["ones"][:, 0:EXPERTS], m_eq[:, t, :], 0.0,
                                                        ALU.mult, ALU.add)

                for t in range(TILES):
                    ts(m_t0[:, t, :], m_mk[:, t, :], best[:, t, TOP_K - 1:TOP_K], ALU.is_gt)
                    last = ts(m_eq[:, t, :], m_mk[:, t, :], best[:, t, TOP_K - 1:TOP_K], ALU.is_equal)
                link(last)
                for t in range(TILES):
                    scan(t)
                room = m_small[:, 96:99]
                link(total(room, m_t0))
                link(ts(room, room, -1.0, ALU.mult, float(TOP_K), ALU.add))
                for t in range(TILES):
                    last = ts(m_cum[:, t, :], m_cum[:, t, :], room[:, t:t + 1], ALU.is_le)
                link(last)
                link(tt(m_eq, m_eq, m_cum, ALU.mult))
                link(tt(m_t0, m_t0, m_eq, ALU.add))
                link(tt(m_w, m_t0, m_sc, ALU.mult))
                norm_ = m_small[:, 99:102]
                link(total(norm_, m_w))
                link(ts(norm_, norm_, 1e-20, ALU.add))
                link(recip(norm_))
                tt(m_w, m_w, along(norm_, EXPERTS), ALU.mult).then_inc(sem("routing_ready"), 1)
                dve.wait_ge(sem("routingT_ready"), l + 1)
                copy(m_wt[0:EXPERTS, :], bank[3][0:EXPERTS, 0:NTOK]).then_inc(sem("routingT_saved"), 1)
                link(copy(m_eq, m_t0))
                for t in range(TILES):
                    last = scan(t)
                link(last)
                chosen_from = m_sc
                link(ts(chosen_from, m_cum, 1.0, ALU.subtract, float(NTOK), ALU.mult))
                copy(g_tab[:, :, :, 0], token_col.unsqueeze(1).broadcast_to([P, TILES, EXPERTS]))
                copy(g_tab[:, :, :, 1], along(tile_cols, EXPERTS))
                copy(g_tab[:, :, :, 2], chosen_from)
                link(copy(g_tab[:, :, :, 3], m_w))
                link(tt(m_w, m_w, g_tab[:, :, :, 3], ALU.subtract))
                link(copy(g_tab[:, :, :, 4], m_w))
                link(tt(m_w, m_w, g_tab[:, :, :, 4], ALU.subtract))
                link(copy(g_tab[:, :, :, 5], m_w))
                dve.wait_ge(sem("places_ready"), l + 1)
                link(stt(g_pos, heads(bank[2][:, 0:192], TILES), 1.0, m_t0, ALU.add, ALU.mult))
                link(ts(g_pos, g_pos, 1.0, ALU.subtract))
                most = m_small[:, 102:103]
                link(total(most, bank[2][:, 192:256], ALU.max))
                link(ts(g_overflow, most[0:1, :], float(SLOTS), ALU.is_gt))
                dve.drain().then_inc(sem("table_ready"), 1)
                groups = EXPERTS // 4
                dve.wait_ge(sem("table_ready"), l + 1)
                dve.sem_inc(sem("one_hot_used"), 2)
                with dve.Fori(0, groups // 2) as i:
                    for b in range(2):
                        dve.wait_ge(sem("one_hot_used"), i * 2 + ((groups + 2) * l + b + 1))
                        for q in range(4):
                            for t in range(TILES):
                                last = ts(g_one[b][:, q, t, :], C["slot_index"],
                                          g_pos[:, t, bass.ds(i * 8 + (4 * b + q), 1)], ALU.is_equal)
                        last.then_inc(sem("one_hot_ready"), 1)
                dve.wait_ge(sem("picks_ready"), l + 1)
                picks = bank[3][:, 0:6 * EXPERTS].rearrange("p (e k) -> p k e", k=6)
                src, dst, wgt = (m_t0[:, k, :] for k in range(3))
                link(copy(src, picks[:, 0, :]))
                link(tt(src, src, picks[:, 1, :], ALU.add))
                link(ts(src, src, float(NOWHERE), ALU.add))
                copy(g_rows[:, 0, :], src)
                link(tt(dst, src, picks[:, 2, :], ALU.add))
                copy(g_rows[:, 1, :], dst)
                link(copy(wgt, picks[:, 5, :]))
                link(tt(wgt, wgt, picks[:, 4, :], ALU.add))
                link(tt(g_w, wgt, picks[:, 3, :], ALU.add))
                for b in range(2):
                    last = nc.vector.memset(g_x[b], 0.0)
                link(last)
                end_phase()

            def hidden_half(half, q, l, i=None, e=0):
                v = lambda n: n if i is None else i * 4 + n
                dve.wait_ge(sem("gate_silu"), v(q + 1))
                if i is not None or l:
                    dve.wait_ge(sem("down_done"), v(q - 1))
                tt(x_h[half], bank[7][:, 0:NTOK], x_e[half], ALU.mult).then_inc(sem("gu_saved"), 1)
                dve.wait_ge(sem("gu_saved"), v(q + 1))
                if i is None:
                    dve.drain().then_inc(sem("hid_ready"), 1)
                    return
                if half == 0:
                    dve.wait_ge(sem("expert_loaded", e), i * 16 + 16 * (l * EXPERTS // 2 + 1))
                tt(x_h[half], x_h[half], x_bc[e], ALU.mult).then_inc(sem("hid_ready"), 1)

            def save_sums(l):
                dve.wait_ge(sem("y_sums_ready"), l + 1)
                for k in (1, 3, 5):
                    copy(x_y[:, k // 2, 512:1024], bank[k][:, :]).then_inc(sem("y_sums_saved"), 1)

            def dense(l):
                q0 = 2 * (EXPERTS + 1) * l + 2
                with dve.Fori(0, EXPERTS // 2) as i:
                    for e in range(2):
                        for half in range(2):
                            hidden_half(half, q0 + 2 * e + half, l, i, e)
                save_sums(l)
                dve.wait_ge(sem("y_sums_saved"), 6 * (l + 1))

            def sparse(l):
                save_sums(l)

                def tokens(x):
                    dve.wait_ge(sem("xt_ready"), x.count())
                    if x.l or x.e >= 2:
                        dve.wait_ge(sem("gate_up_used"), x.count(2))
                    copy(g_xt[x.b][:, 4:8, :], heads(bank[1][:, :], 4)).then_inc(sem("xt_saved_b"), 1)

                def save(x):
                    dve.wait_ge(sem("down_used"), x.count())
                    if x.e >= 2:
                        dve.wait_ge(sem("scattered", l, x.b), x.scatters_before())
                    copy(g_y[x.b][:, 512:1024], bank[6][:, :]).then_inc(sem("slots_saved_b"), 1)

                def step(x):
                    dve.wait_ge(sem("slot_silu"), x.count())
                    if x.l or x.e >= 2:
                        dve.wait_ge(sem("ht_ready"), x.count(2))
                    stt(g_h[x.b], bank[2 + x.b][:, FF:2 * FF], g_w[:, x.column()], g_s[x.b], ALU.mult, ALU.mult)\
                        .then_inc(sem("slot_hidden"), 1)
                    if x.e + 1 < EXPERTS:
                        tokens(after(x))
                    if x.e:
                        save(before(x))

                tokens(Turn(l, 0))
                each_expert(dve, l, step)
                save(Turn(l, EXPERTS - 1))
                dve.wait_ge(sem("y_sums_saved"), 6 * (l + 1))
                for t in range(TILES):
                    dve.wait_ge(sem("scattered", l, t % 2), choices(t))
                    for k in range(TOP_K):
                        tt(x_y[:, t, :], x_y[:, t, :], y_load[t % 2][:, k, :], ALU.add)\
                            .then_inc(sem("choices_summed"), 1)
                        dve.wait_ge(sem("choices_summed"), TOP_K * (TILES * l + t) + k + 1)

            def experts(l):
                q0 = 2 * (EXPERTS + 1) * l
                hidden_half(0, q0, l)
                hidden_half(1, q0 + 1, l)
                by_load(dve, l, dense, sparse, DENSE_DVE, SPARSE_DVE)
                dve.drain().then_inc(sem("y_total_ready"), 1)
                for k in range(6):
                    t, half = divmod(k, 2)
                    c = min(t, 1)
                    dve.wait_ge(sem("yT_ready"), 6 * l + k + 1)
                    for i in range(4):
                        j = 4 * half + i
                        x = xT[:, j, t * P:(t + 1) * P]
                        last = stt(x, bank[k][:, i * P:(i + 1) * P], mods[:, 5, j, c:c + 1], x, ALU.mult, ALU.add)
                last.then_inc(sem("x_ready"), 1)
                dve.wait_ge(sem("x_ready"), 2 * l + 2)
                end_phase()

            for l in range(LAYERS):
                modulation(l)
                norm(2 * l + 1)
                projection(l)
                (token_shift if l % 2 == 0 else convolution)()
                end_phase()
                attend(l)
                (rwkv if l % 2 == 0 else delta)()
                output_projection(l)
                norm(2 * l + 2)
                router(l)
                experts(l)

        @block.gpsimd
        def _(pool):
            def masked_parts(inv, n, groups=(0, 1)):
                for k in range(LEVELS):
                    mask = C[f"join{k}"].unsqueeze(1).broadcast_to([P, 4, P])
                    for g in groups:
                        if k == 0:
                            pool.wait_ge(inv.sem("nt_ready", g), n + 1)
                            if n:
                                pool.wait_ge(inv.sem("m_ready", g), 6 * n)
                        elif k == 1:
                            pool.wait_ge(inv.sem("t_ready", g), 7 * n + 1)
                        else:
                            pool.wait_ge(inv.sem("m_ready", g), 6 * n + k - 1)
                        nc.gpsimd.tensor_tensor(inv.off[g], inv.nt[g], mask, ALU.mult)\
                            .then_inc(inv.sem("off_ready", g), 1)

            def dense(l):
                q0 = 2 * (EXPERTS + 1) * l
                with pool.Fori(0, EXPERTS // 2) as i:
                    for e in range(2):
                        pool.wait_ge(sem("hid_ready"), i * 4 + max(q0 + 2 * e, 1))
                        pool.dma_start(x_bc[e], wt_dram[l, bass.ds(i * 2 + e, 1), :].broadcast_to([P, NTOK]))\
                            .then_inc(sem("expert_loaded", e), 16)

            def sparse(l):
                def rows_of_slots(x, k):
                    nc.gpsimd.tensor_copy(g_idx[:, 2 * k + x.b:2 * k + x.b + 1], g_rows[:, k, x.column()])\
                        .then_inc(sem("index_ready"), 1)

                def copied(x, n):
                    v = 2 * EXPERTS * l + n
                    pool.wait_ge(sem("index_ready"), v if x.i is None else x.i * 4 + v)

                def at(x, k):
                    c = g_idx[:, 2 * k + x.b:2 * k + x.b + 1]
                    return bass.IndirectOffsetOnAxis(ap=c, axis=0)

                def gather(x):
                    nc.gpsimd.indirect_dma_start(g_x[x.b], None, x_rows[l], at(x, 0), bounds_check=NTOK - 1,
                                                 oob_is_err=False).then_inc(sem("expert_loaded", x.b), 16)

                def scatter(x):
                    nc.gpsimd.indirect_dma_start(y_rows[l], at(x, 1), g_y[x.b], None, bounds_check=TOP_K * NTOK - 1,
                                                 oob_is_err=False).then_inc(sem("scattered", l, x.b), 16)

                def step(x):
                    e, last, past = Turn(l, x.e + 2, x.i), before(x), before(before(x))
                    if x.e >= 2:
                        copied(x, min(2 * x.e + 1, EXPERTS + x.e - 1) if x.e < EXPERTS - 1 else 2 * EXPERTS - 2)
                        pool.wait_ge(sem("slots_saved_a"), past.count())
                        pool.wait_ge(sem("slots_saved_b"), past.count())
                    if e.e < EXPERTS:
                        pool.wait_ge(sem("expert_loaded", x.b), x.dmas())
                        pool.wait_ge(sem("xt_ready"), x.count())
                        rows_of_slots(e, 0)
                    if x.e >= 2:
                        scatter(past)
                    if e.e < EXPERTS:
                        copied(x, 2 * x.e + 2 if x.e else 3)
                    if x.e >= 3:
                        pool.wait_ge(sem("scattered", l, last.b), last.scatters_before())
                    if x.e:
                        rows_of_slots(last, 1)
                    if e.e < EXPERTS:
                        gather(e)

                for e in range(2):
                    x = Turn(l, e)
                    if l:
                        pool.wait_ge(sem("xt_ready"), x.count(2))
                    rows_of_slots(x, 0)
                    copied(x, e + 1)
                    gather(x)
                each_expert(pool, l, step)
                last = Turn(l, EXPERTS - 1)
                copied(last, 2 * EXPERTS - 1)
                pool.wait_ge(sem("slots_saved_a"), last.count(1))
                pool.wait_ge(sem("slots_saved_b"), last.count(1))
                scatter(before(last))
                pool.wait_ge(sem("scattered", l, last.b), last.scatters_before())
                rows_of_slots(last, 1)
                copied(last, 2 * EXPERTS)
                pool.wait_ge(sem("slots_saved_a"), last.count())
                pool.wait_ge(sem("slots_saved_b"), last.count())
                scatter(last)
                for b in range(2):
                    pool.wait_ge(sem("scattered", l, b), 8 * EXPERTS)
                for t in range(TILES):
                    if t >= 2:
                        pool.wait_ge(sem("choices_summed"), TOP_K * (TILES * l + t - 1))
                    pool.dma_start(y_load[t % 2], y_rows[l].rearrange("(k t p) d -> t p k d", k=TOP_K, t=TILES)[t])\
                        .then_inc(sem("scattered", l, t % 2), 16)

            def experts(l):
                pool.wait_ge(sem("routing_stored"), 16 * (l + 1))
                pool.wait_ge(sem("rows_stored"), 16 * (l + 1))
                pool.wait_ge(sem("phase_done", "dve"), 8 * l + 7)
                by_load(pool, l, dense, sparse, [], [])

            for u in range(len(RWKV_UNITS)):
                masked_parts(r_inverse, u)
            experts(0)
            for n in range(len(DELTA_STEPS)):
                masked_parts(d_inverse, len(RWKV_UNITS) + n)
            experts(1)


_PLAIN = ["mod_w", "ev_w_in", "ev_w_out", "a_qn", "a_kn", "b_mu", "b_w0", "b_w2", "b_a0", "b_a2", "b_g2", "b_kk", "b_ka",
          "b_rk", "b_lnx_w", "b_lnx_b", "od_w_in", "od_w_out", "c_conv", "c_A_log", "c_dt_bias", "c_onorm", "d_qn",
          "d_kn", "d_lambda", "d_subln", "router_w", "router_bias", "exp_w_gate", "exp_w_up", "exp_w_down",
          "sh_w_gate", "sh_w_up", "sh_w_down"]
_OUTS = {"yT": (P, J, NTOK), "k_a": (P, 128), "v_a": (P, 128), "state_r": (P, 2, 4, 64), "state_d": (P, 2, 4, 128),
         "k_d": (P, 512), "v_d": (P, 512)}


def kernel(**inputs):
    import numpy as _np
    import concourse.bacc as _bacc
    from concourse import mybir as _mybir
    from concourse.bass_utils import run_bass_kernel_spmd as _run

    x = {k: _np.asarray(v) for k, v in inputs.items()}
    lay = {n: x[n] for n in _PLAIN}
    lay["xT"] = _np.concatenate([x["x_prompt"][0], x["x_sample"][0]], 0).T.reshape(P, J, NTOK)
    lay["cond"] = _np.stack([x["c_ctx"], x["c"][0]], 1).reshape(P, J, 2)
    lay["mod_b"] = x["mod_b"].reshape(LAYERS, 6, P, J).transpose(2, 0, 1, 3)
    lay["gains"] = _np.stack([x["norm1_g"], x["norm2_g"]], 1).reshape(LAYERS, 2, P, J).transpose(2, 0, 1, 3)
    lay["keys_a"] = x["cache_attn_k"][0, 0].transpose(0, 2, 1).reshape(P, P)
    lay["values_a"] = x["cache_attn_v"][0, 0].transpose(1, 0, 2)
    lay["keys_d"] = x["cache_diff_k"][0, 0].transpose(1, 3, 0, 2).reshape(P, 4, P)
    lay["values_d"] = x["cache_diff_v"][0, 0].transpose(1, 0, 2)
    lay["state_r"] = x["state_rwkv"][0, 0].reshape(2, 4, 2, 64, 64).transpose(2, 4, 0, 1, 3).reshape(P, 2, 4, 64)
    lay["state_d"] = x["state_delta"][0, 0].transpose(2, 0, 1, 3)
    lay["consts"] = constants()
    lay["rope"] = rope_rows().reshape(2, P, 2, HEAD).transpose(1, 0, 2, 3)

    nc = _bacc.Bacc("TRN2", target_bir_lowering=False, num_devices=1)
    arrays, aps = {}, {}
    for n, a in lay.items():
        a = _np.ascontiguousarray(a)
        arrays[f"in_{n}"] = a
        aps[n] = nc.dram_tensor(f"in_{n}", a.shape, _mybir.dt.from_np(a.dtype), kind="ExternalInput").ap()
    outs = {n: nc.dram_tensor(f"out_{n}", s, _mybir.dt.float32, kind="ExternalOutput").ap() for n, s in _OUTS.items()}
    build(nc, aps, outs)
    r = _run(nc, [arrays], core_ids=[0]).results[0]
    got = {n: r[f"out_{n}"] for n in _OUTS}
    y = got["yT"].reshape(D, NTOK).T
    return (y[None, :P], y[None, P:],
            got["k_a"].reshape(P, 2, 64).transpose(1, 0, 2)[None, None],
            got["v_a"].reshape(P, 2, 64).transpose(1, 0, 2)[None, None],
            got["state_r"].reshape(2, 64, 2, 4, 64).transpose(2, 3, 0, 4, 1).reshape(1, 1, 2, 8, 64, 64),
            got["state_d"].transpose(1, 2, 0, 3)[None, None],
            got["k_d"].reshape(P, 4, 2, 64).transpose(1, 2, 0, 3)[None, None],
            got["v_d"].reshape(P, 4, P).transpose(1, 0, 2)[None, None])
```
